# Optimizing a Trainium2 kernel written in Bass

```python
import math
import numpy as np
import jax
import jax.numpy as jnp
from jax import lax

D_MODEL = 1024
BATCH = 1
SEQ = 256
DEPTH = 2

S5_GROUP = 16
S5_CHANNELS = D_MODEL // 4
S5_GROUPS = S5_CHANNELS // S5_GROUP
S5_STATE = 64
SB_HEAD_DIM = 64
SB_HEADS = (D_MODEL - S5_CHANNELS) // SB_HEAD_DIM
SB_WIDTH = SB_HEADS * SB_HEAD_DIM
EVEN_IN = S5_CHANNELS + 3 * SB_WIDTH
EVEN_MIX = S5_CHANNELS + SB_WIDTH
Q_BLOCK = 128
NSA_HEADS = 16
NSA_KV_HEADS = 4
NSA_GROUP = NSA_HEADS // NSA_KV_HEADS
NSA_HEAD_DIM = 64
NSA_Q_WIDTH = NSA_HEADS * NSA_HEAD_DIM
NSA_KV_WIDTH = NSA_KV_HEADS * NSA_HEAD_DIM
NSA_BRANCHES = 3
ODD_IN = NSA_Q_WIDTH + 2 * NSA_BRANCHES * NSA_KV_WIDTH + NSA_BRANCHES * NSA_HEADS
CMP_BLOCK = 32
CMP_STRIDE = 16
CMP_HIDDEN = 128
SEL_BLOCK = 64
SEL_TOPK = 16
SEL_Q_CHUNK = 16
WINDOW = 512
FORCE_BONUS = 1000.0
PEER_HEADS = 8
PEER_KEYS = 128
PEER_EXPERTS = PEER_KEYS * PEER_KEYS
PEER_KEY_DIM = 256
PEER_HALF = PEER_KEY_DIM // 2
PEER_TOPK = 16
PEER_CHUNK = 128
DN_ALPHA = (2 * DEPTH) ** 0.25
DN_BETA = (8 * DEPTH) ** -0.25
LN_EPS = 1e-5
N_EVEN = (DEPTH + 1) // 2
N_ODD = DEPTH // 2

kernel_name = 'hybrid_s5_stickbreak_nsa_peer_deepnorm'

def layer_norm(x, g, b):
    xf = x.astype(jnp.float32)
    mu = jnp.mean(xf, axis=-1, keepdims=True)
    var = jnp.mean(jnp.square(xf - mu), axis=-1, keepdims=True)
    return ((xf - mu) * lax.rsqrt(var + LN_EPS) * g + b).astype(x.dtype)

def masked_softmax(s, mask):
    s = jnp.where(mask, s, -jnp.inf)
    m = jnp.max(s, axis=-1, keepdims=True)
    m = jnp.where(jnp.isfinite(m), m, 0.0)
    e = jnp.where(mask, jnp.exp(s - m), 0.0)
    return e / jnp.maximum(jnp.sum(e, axis=-1, keepdims=True), 1e-30)

def alibi_slopes(n):
    return jnp.asarray(2.0 ** (-8.0 * np.arange(1, n + 1) / n), jnp.float32)

def cmp_to_sel_matrix(n_cmp, n_sel):
    cs = np.arange(n_cmp)[:, None] * CMP_STRIDE
    ss = np.arange(n_sel)[None, :] * SEL_BLOCK
    ov = np.clip(np.minimum(cs + CMP_BLOCK, ss + SEL_BLOCK) - np.maximum(cs, ss), 0, None) / CMP_BLOCK
    return jnp.asarray(ov, jnp.float32)

def s5_mixer(u, lam_re, lam_im, log_dt, b_re, b_im, c_re, c_im, d_skip, w_glu, b_glu):
    f32 = jnp.float32
    bsz, L, _ = u.shape
    uf = u.astype(f32)
    ug = uf.reshape(bsz, L, S5_GROUPS, S5_GROUP)
    lr = lam_re.astype(f32)
    li = lam_im.astype(f32)
    dt = jnp.exp(log_dt.astype(f32))[:, None]
    mag = jnp.exp(lr * dt)
    ab_re = mag * jnp.cos(li * dt)
    ab_im = mag * jnp.sin(li * dt)
    nr = ab_re - 1.0
    den = lr * lr + li * li
    f_re = (nr * lr + ab_im * li) / den
    f_im = (ab_im * lr - nr * li) / den
    bb_re = f_re[..., None] * b_re.astype(f32) - f_im[..., None] * b_im.astype(f32)
    bb_im = f_re[..., None] * b_im.astype(f32) + f_im[..., None] * b_re.astype(f32)
    bu_re = jnp.einsum('blgi,gpi->blgp', ug, bb_re)
    bu_im = jnp.einsum('blgi,gpi->blgp', ug, bb_im)
    a_re = jnp.broadcast_to(ab_re, bu_re.shape)
    a_im = jnp.broadcast_to(ab_im, bu_im.shape)

    def combine(e1, e2):
        a1r, a1i, b1r, b1i = e1
        a2r, a2i, b2r, b2i = e2
        return (a2r * a1r - a2i * a1i,
                a2r * a1i + a2i * a1r,
                a2r * b1r - a2i * b1i + b2r,
                a2r * b1i + a2i * b1r + b2i)

    _, _, x_re, x_im = lax.associative_scan(combine, (a_re, a_im, bu_re, bu_im), axis=1)
    y = (jnp.einsum('blgp,gip->blgi', x_re, c_re.astype(f32))
         - jnp.einsum('blgp,gip->blgi', x_im, c_im.astype(f32)))
    y = y.reshape(bsz, L, S5_CHANNELS) + d_skip.astype(f32) * uf
    y = jax.nn.gelu(y)
    y = y * jax.nn.sigmoid(y @ w_glu.astype(f32) + b_glu.astype(f32))
    return y.astype(u.dtype)

def stick_breaking_attention(q, k, v):
    L = q.shape[1]
    scale = SB_HEAD_DIM ** -0.5
    outs = []
    for blk in range(L // Q_BLOCK):
        t0 = blk * Q_BLOCK
        t1 = t0 + Q_BLOCK
        z = jnp.einsum('bqhd,bkhd->bhqk', q[:, t0:t1], k[:, :t1]).astype(jnp.float32) * scale
        tq = t0 + jnp.arange(Q_BLOCK)[:, None]
        sk = jnp.arange(t1)[None, :]
        mask = sk < tq
        log1m = jnp.where(mask, jax.nn.log_sigmoid(-z), 0.0)
        tail = lax.cumsum(log1m, axis=3, reverse=True) - log1m
        w = jnp.where(mask, jnp.exp(jax.nn.log_sigmoid(z) + tail), 0.0)
        outs.append(jnp.einsum('bhqk,bkhd->bqhd', w.astype(v.dtype), v[:, :t1]))
    return jnp.concatenate(outs, axis=1)

def even_mixer(x, w_in, lam_re, lam_im, log_dt, b_re, b_im, c_re, c_im, d_skip, w_glu, b_glu, w_out):
    bsz, L, _ = x.shape
    proj = x @ w_in
    u = proj[..., :S5_CHANNELS]
    o = S5_CHANNELS
    q = proj[..., o:o + SB_WIDTH].reshape(bsz, L, SB_HEADS, SB_HEAD_DIM)
    k = proj[..., o + SB_WIDTH:o + 2 * SB_WIDTH].reshape(bsz, L, SB_HEADS, SB_HEAD_DIM)
    v = proj[..., o + 2 * SB_WIDTH:].reshape(bsz, L, SB_HEADS, SB_HEAD_DIM)
    y_a = s5_mixer(u, lam_re, lam_im, log_dt, b_re, b_im, c_re, c_im, d_skip, w_glu, b_glu)
    y_b = stick_breaking_attention(q, k, v).reshape(bsz, L, SB_WIDTH).astype(x.dtype)
    return jnp.concatenate([y_a, y_b], axis=-1) @ w_out

def nsa_mixer(x, w_in, pe_k, w1_k, w2_k, pe_v, w1_v, w2_v, w_out):
    f32 = jnp.float32
    bsz, L, _ = x.shape
    G, R, hd = NSA_KV_HEADS, NSA_GROUP, NSA_HEAD_DIM
    scale = hd ** -0.5
    proj = x @ w_in
    q = proj[..., :NSA_Q_WIDTH].reshape(bsz, L, G, R, hd)
    kv = proj[..., NSA_Q_WIDTH:NSA_Q_WIDTH + 2 * NSA_BRANCHES * NSA_KV_WIDTH].reshape(bsz, L, 2 * NSA_BRANCHES, G, hd)
    kc, vc, ks, vs, kw, vw = [kv[:, :, j] for j in range(2 * NSA_BRANCHES)]
    gates = jax.nn.sigmoid(proj[..., NSA_Q_WIDTH + 2 * NSA_BRANCHES * NSA_KV_WIDTH:].astype(f32))
    gates = gates.reshape(bsz, L, NSA_BRANCHES, G, R)
    slopes = alibi_slopes(NSA_HEADS).reshape(G, R)
    pos = jnp.arange(L)

    n_cmp = (L - CMP_BLOCK) // CMP_STRIDE + 1
    starts = jnp.arange(n_cmp) * CMP_STRIDE
    idx = starts[:, None] + jnp.arange(CMP_BLOCK)[None, :]

    def compress(t, pe, w1, w2):
        blocks = t[:, idx] + pe[None, None, :, None, :]
        blocks = jnp.moveaxis(blocks, 3, 2).reshape(bsz, n_cmp, G, CMP_BLOCK * hd)
        return jax.nn.gelu(blocks @ w1) @ w2

    k_cmp = compress(kc, pe_k, w1_k, w2_k)
    v_cmp = compress(vc, pe_v, w1_v, w2_v)
    ends = starts + CMP_BLOCK - 1
    dist_c = (pos[:, None] - ends[None, :]).astype(f32)
    s_c = jnp.einsum('btgrd,bngd->bgrtn', q, k_cmp).astype(f32) * scale
    s_c = s_c - slopes[:, :, None, None] * dist_c
    p_c = masked_softmax(s_c, dist_c >= 0)
    o_cmp = jnp.einsum('bgrtn,bngd->btgrd', p_c.astype(v_cmp.dtype), v_cmp)

    n_sel = L // SEL_BLOCK
    k_sel = min(SEL_TOPK, n_sel)
    imp = jnp.einsum('bgrtn,nj->bgtj', p_c, cmp_to_sel_matrix(n_cmp, n_sel))
    jb = jnp.arange(n_sel)[None, :]
    cur = (pos // SEL_BLOCK)[:, None]
    causal = jb * SEL_BLOCK <= pos[:, None]
    forced = (jb == 0) | (jb == cur) | (jb == cur - 1)
    imp = jnp.where(causal, imp + jnp.where(forced, FORCE_BONUS, 0.0), -jnp.inf)
    _, sel_idx = lax.top_k(imp, k_sel)

    ks_blk = jnp.moveaxis(ks.reshape(bsz, n_sel, SEL_BLOCK, G, hd), 3, 1)
    vs_blk = jnp.moveaxis(vs.reshape(bsz, n_sel, SEL_BLOCK, G, hd), 3, 1)
    gather_bg = jax.vmap(jax.vmap(lambda tbl, ix: tbl[ix]))
    n_chunk = L // SEL_Q_CHUNK
    q_ch = jnp.moveaxis(q.reshape(bsz, n_chunk, SEL_Q_CHUNK, G, R, hd), 1, 0)
    idx_ch = jnp.moveaxis(sel_idx.reshape(bsz, G, n_chunk, SEL_Q_CHUNK, k_sel), 2, 0)
    pos_ch = pos.reshape(n_chunk, SEL_Q_CHUNK)
    m_keys = k_sel * SEL_BLOCK

    def sel_chunk(args):
        qc, ic, tc = args
        kg = gather_bg(ks_blk, ic).reshape(bsz, G, SEL_Q_CHUNK, m_keys, hd)
        vg = gather_bg(vs_blk, ic).reshape(bsz, G, SEL_Q_CHUNK, m_keys, hd)
        kpos = (ic[..., None] * SEL_BLOCK + jnp.arange(SEL_BLOCK)).reshape(bsz, G, SEL_Q_CHUNK, m_keys)
        dist = (tc[None, None, :, None] - kpos).astype(f32)
        s = jnp.einsum('bcgrd,bgcmd->bgrcm', qc, kg).astype(f32) * scale
        s = s - slopes[None, :, :, None, None] * dist[:, :, None]
        p = masked_softmax(s, dist[:, :, None] >= 0)
        return jnp.einsum('bgrcm,bgcmd->bcgrd', p.astype(vg.dtype), vg)

    o_slc = lax.map(sel_chunk, (q_ch, idx_ch, pos_ch))
    o_slc = jnp.moveaxis(o_slc, 0, 1).reshape(bsz, L, G, R, hd)

    kw_pad = jnp.pad(kw, ((0, 0), (WINDOW, 0), (0, 0), (0, 0)))
    vw_pad = jnp.pad(vw, ((0, 0), (WINDOW, 0), (0, 0), (0, 0)))
    n_qb = L // Q_BLOCK
    span = WINDOW + Q_BLOCK
    q_b = jnp.moveaxis(q.reshape(bsz, n_qb, Q_BLOCK, G, R, hd), 1, 0)

    def win_block(args):
        qb, i = args
        t0 = i * Q_BLOCK
        kb = lax.dynamic_slice_in_dim(kw_pad, t0, span, axis=1)
        vb = lax.dynamic_slice_in_dim(vw_pad, t0, span, axis=1)
        tq = t0 + jnp.arange(Q_BLOCK)
        sk = t0 - WINDOW + jnp.arange(span)
        dist = tq[:, None] - sk[None, :]
        mask = (dist >= 0) & (dist < WINDOW) & (sk[None, :] >= 0)
        s = jnp.einsum('bqgrd,bkgd->bgrqk', qb, kb).astype(f32) * scale
        s = s - slopes[:, :, None, None] * dist.astype(f32)
        p = masked_softmax(s, mask)
        return jnp.einsum('bgrqk,bkgd->bqgrd', p.astype(vb.dtype), vb)

    o_win = lax.map(win_block, (q_b, jnp.arange(n_qb)))
    o_win = jnp.moveaxis(o_win, 0, 1).reshape(bsz, L, G, R, hd)

    o = (gates[:, :, 0, :, :, None] * o_cmp + gates[:, :, 1, :, :, None] * o_slc
         + gates[:, :, 2, :, :, None] * o_win)
    return o.reshape(bsz, L, NSA_Q_WIDTH).astype(x.dtype) @ w_out

def peer_ffn(x, w_q, sub_keys, u_tab, v_tab):
    f32 = jnp.float32
    bsz, L, D = x.shape
    tok = x.reshape(-1, PEER_CHUNK, D)

    def chunk(xc):
        q = (xc @ w_q).reshape(PEER_CHUNK, PEER_HEADS, 2, PEER_HALF)
        s1 = jnp.einsum('chd,hkd->chk', q[:, :, 0], sub_keys[:, 0]).astype(f32)
        s2 = jnp.einsum('chd,hkd->chk', q[:, :, 1], sub_keys[:, 1]).astype(f32)
        v1, i1 = lax.top_k(s1, PEER_TOPK)
        v2, i2 = lax.top_k(s2, PEER_TOPK)
        cand = (v1[..., :, None] + v2[..., None, :]).reshape(PEER_CHUNK, PEER_HEADS, PEER_TOPK * PEER_TOPK)
        top, flat = lax.top_k(cand, PEER_TOPK)
        e1 = jnp.take_along_axis(i1, flat // PEER_TOPK, axis=-1)
        e2 = jnp.take_along_axis(i2, flat % PEER_TOPK, axis=-1)
        expert = e1 * PEER_KEYS + e2
        g = jax.nn.softmax(top, axis=-1)
        h = jax.nn.gelu(jnp.einsum('cd,chkd->chk', xc, u_tab[expert]).astype(f32))
        return jnp.einsum('chk,chkd->cd', (g * h).astype(v_tab.dtype), v_tab[expert])

    return lax.map(chunk, tok).reshape(bsz, L, D)

def setup_inputs(seed: int = 0) -> dict:
    key = jax.random.key(seed)
    ks = iter(jax.random.split(key, 48))
    f32 = jnp.float32

    def nrm(shape, std):
        return jax.random.normal(next(ks), shape, f32) * std

    D = D_MODEL
    x = nrm((BATCH, SEQ, D), 1.0)
    even_w_in = nrm((N_EVEN, D, EVEN_IN), D ** -0.5)
    even_lam_re = -0.5 + nrm((N_EVEN, S5_GROUPS, S5_STATE), 0.01)
    even_lam_im = math.pi * jnp.arange(S5_STATE, dtype=f32) + nrm((N_EVEN, S5_GROUPS, S5_STATE), 0.01)
    even_log_dt = jax.random.uniform(next(ks), (N_EVEN, S5_GROUPS), f32, math.log(1e-3), math.log(1e-1))
    b_std = (2.0 * S5_GROUP) ** -0.5
    even_b_re = nrm((N_EVEN, S5_GROUPS, S5_STATE, S5_GROUP), b_std)
    even_b_im = nrm((N_EVEN, S5_GROUPS, S5_STATE, S5_GROUP), b_std)
    c_std = (0.5 * S5_STATE) ** -0.5
    even_c_re = nrm((N_EVEN, S5_GROUPS, S5_GROUP, S5_STATE), c_std)
    even_c_im = nrm((N_EVEN, S5_GROUPS, S5_GROUP, S5_STATE), c_std)
    even_d = nrm((N_EVEN, S5_CHANNELS), 1.0)
    even_w_glu = nrm((N_EVEN, S5_CHANNELS, S5_CHANNELS), S5_CHANNELS ** -0.5)
    even_b_glu = nrm((N_EVEN, S5_CHANNELS), 0.02)
    even_w_out = nrm((N_EVEN, EVEN_MIX, D), EVEN_MIX ** -0.5 * DN_BETA)
    odd_w_in = nrm((N_ODD, D, ODD_IN), D ** -0.5)
    odd_pe_k = nrm((N_ODD, CMP_BLOCK, NSA_HEAD_DIM), 0.1)
    odd_w1_k = nrm((N_ODD, CMP_BLOCK * NSA_HEAD_DIM, CMP_HIDDEN), (CMP_BLOCK * NSA_HEAD_DIM) ** -0.5)
    odd_w2_k = nrm((N_ODD, CMP_HIDDEN, NSA_HEAD_DIM), CMP_HIDDEN ** -0.5)
    odd_pe_v = nrm((N_ODD, CMP_BLOCK, NSA_HEAD_DIM), 0.1)
    odd_w1_v = nrm((N_ODD, CMP_BLOCK * NSA_HEAD_DIM, CMP_HIDDEN), (CMP_BLOCK * NSA_HEAD_DIM) ** -0.5)
    odd_w2_v = nrm((N_ODD, CMP_HIDDEN, NSA_HEAD_DIM), CMP_HIDDEN ** -0.5)
    odd_w_out = nrm((N_ODD, NSA_Q_WIDTH, D), NSA_Q_WIDTH ** -0.5 * DN_BETA)
    peer_w_q = nrm((DEPTH, D, PEER_HEADS * PEER_KEY_DIM), D ** -0.5)
    peer_sub_keys = nrm((DEPTH, PEER_HEADS, 2, PEER_KEYS, PEER_HALF), PEER_HALF ** -0.5)
    peer_u = nrm((DEPTH, PEER_EXPERTS, D), D ** -0.5)
    peer_v = nrm((DEPTH, PEER_EXPERTS, D), DN_BETA)
    ln1_g = 1.0 + nrm((DEPTH, D), 0.02)
    ln1_b = nrm((DEPTH, D), 0.02)
    ln2_g = 1.0 + nrm((DEPTH, D), 0.02)
    ln2_b = nrm((DEPTH, D), 0.02)
    return {'x': x, 'even_w_in': even_w_in, 'even_lam_re': even_lam_re, 'even_lam_im': even_lam_im,
            'even_log_dt': even_log_dt, 'even_b_re': even_b_re, 'even_b_im': even_b_im,
            'even_c_re': even_c_re, 'even_c_im': even_c_im, 'even_d': even_d,
            'even_w_glu': even_w_glu, 'even_b_glu': even_b_glu, 'even_w_out': even_w_out,
            'odd_w_in': odd_w_in, 'odd_pe_k': odd_pe_k, 'odd_w1_k': odd_w1_k, 'odd_w2_k': odd_w2_k,
            'odd_pe_v': odd_pe_v, 'odd_w1_v': odd_w1_v, 'odd_w2_v': odd_w2_v, 'odd_w_out': odd_w_out,
            'peer_w_q': peer_w_q, 'peer_sub_keys': peer_sub_keys, 'peer_u': peer_u, 'peer_v': peer_v,
            'ln1_g': ln1_g, 'ln1_b': ln1_b, 'ln2_g': ln2_g, 'ln2_b': ln2_b}

def reference(x, even_w_in, even_lam_re, even_lam_im, even_log_dt, even_b_re, even_b_im,
              even_c_re, even_c_im, even_d, even_w_glu, even_b_glu, even_w_out,
              odd_w_in, odd_pe_k, odd_w1_k, odd_w2_k, odd_pe_v, odd_w1_v, odd_w2_v, odd_w_out,
              peer_w_q, peer_sub_keys, peer_u, peer_v, ln1_g, ln1_b, ln2_g, ln2_b):
    h = x
    for i in range(DEPTH):
        j = i // 2
        if i % 2 == 0:
            mix = even_mixer(h, even_w_in[j], even_lam_re[j], even_lam_im[j], even_log_dt[j],
                             even_b_re[j], even_b_im[j], even_c_re[j], even_c_im[j], even_d[j],
                             even_w_glu[j], even_b_glu[j], even_w_out[j])
        else:
            mix = nsa_mixer(h, odd_w_in[j], odd_pe_k[j], odd_w1_k[j], odd_w2_k[j],
                            odd_pe_v[j], odd_w1_v[j], odd_w2_v[j], odd_w_out[j])
        h = layer_norm(DN_ALPHA * h + mix, ln1_g[i], ln1_b[i])
        ffn = peer_ffn(h, peer_w_q[i], peer_sub_keys[i], peer_u[i], peer_v[i])
        h = layer_norm(DN_ALPHA * h + ffn, ln2_g[i], ln2_b[i])
    return h


_drawn_inputs = setup_inputs


def setup_inputs(seed=0):
    import zlib

    import numpy as np

    out = dict(_drawn_inputs(seed))
    spreads = {}
    factors = {'even_lam_re': 200.0,
     'even_b_glu': 16.14,
     'odd_pe_k': 25.945,
     'even_lam_im': 16.99,
     'even_log_dt': 15.506,
     'even_b_re': 19.854,
     'even_b_im': 21.26,
     'even_c_re': 20.413,
     'even_c_im': 21.568,
     'odd_pe_v': 2.775}
    for name, (base, spread) in spreads.items():
        noise = np.random.default_rng([zlib.crc32(name.encode()), seed]).standard_normal(out[name].shape)
        drawn = base * np.exp(spread * noise) if base else spread * noise
        out[name] = jnp.asarray(drawn.astype(out[name].dtype))
    for name, factor in factors.items():
        out[name] = (out[name] * factor).astype(out[name].dtype)
    return out
```

```python
from contextlib import ExitStack

import numpy as np

import concourse.bass as bass
from concourse import mybir

ALU = mybir.AluOpType
ACT = mybir.ActivationFunctionType
AX = mybir.AxisListType
F32 = mybir.dt.float32
F32R = mybir.dt.float32r
U32 = mybir.dt.uint32

P = 128
SEQ = 256
D = 1024
T = SEQ // P
KC = D // P
LAYERS = 2
RING = 4

GROUPS, STATE, CH = 16, 64, 16
UT = GROUPS * CH // P
ST = GROUPS * STATE // P
SB_PAIRS = 6
HEAD = 64
SCALE = HEAD ** -0.5
CMP_BLOCK, CMP_STRIDE = 32, 16
NCMP = (SEQ - CMP_BLOCK) // CMP_STRIDE + 1
NSA_HEADS = 16
NBR = 3
EPS = 1e-5
ALPHA = (2 * LAYERS) ** 0.25
PEER_HEADS, KEYS, TOPK = 8, 128, 16
SUBS = 2 * PEER_HEADS
NEG = -1e30

PROJ, OUTW, WQ, EXP = 20, 8, 16, 2 * KEYS
PER_LAYER = PROJ + OUTW + WQ + EXP
SLABS = LAYERS * PER_LAYER
PROJ_PER_LAYER = PROJ + WQ

TWO_PI = 2 * np.pi
PI_A = 6.28125
PI_B = float(np.float32(TWO_PI - PI_A))
PI_C = float(np.float32(TWO_PI - PI_A - PI_B))
ROUND = 1.5 * 2.0 ** 23
PI_IN = float(np.nextafter(np.float32(np.pi), np.float32(0)))

C_IDENT, C_TRI, C_ONES, C_BELOW, C_NEGDIAG = 0, 128, 256, 384, 512
C_IOTA, C_IOTA16, C_DIST, C_SLOPE = 640, 768, 784, 784 + 384
C_CMPBIAS = C_SLOPE + NSA_HEADS
C_CMPMASK = C_CMPBIAS + T * NSA_HEADS * NCMP
C_ALL = C_CMPMASK + T * NCMP


def constants():
    c = np.zeros((P, C_ALL), np.float32)
    i = np.arange(P)
    c[:, C_IDENT:C_IDENT + P] = np.eye(P)
    c[:, C_TRI:C_TRI + P] = -1.0 * (i[:, None] >= i[None, :])
    c[:, C_ONES:C_ONES + P] = -1
    c[:, C_BELOW:C_BELOW + P] = i[:, None] < i[None, :]
    c[:, C_NEGDIAG:C_NEGDIAG + P] = np.where(i[:, None] < i[None, :], 0, NEG)
    c[:, C_IOTA:C_IOTA + P] = i[None, :]
    c[:, C_IOTA16:C_IOTA16 + TOPK] = np.arange(TOPK)[None, :]
    col = C_DIST
    for t in range(T):
        n = P * (t + 1)
        dist = (t * P + i[:, None]) - np.arange(n)[None, :]
        c[:, col:col + n] = np.where(dist >= 0, -dist, NEG)
        col += n
    head = np.arange(NSA_HEADS)
    order = np.array([(2 * p + half) * 4 + r for p in range(2) for r in range(4) for half in range(2)])
    slope = (2.0 ** (-8.0 * (head + 1) / NSA_HEADS)).astype(np.float32)[order]
    c[:, C_SLOPE:C_SLOPE + NSA_HEADS] = slope
    ends = np.arange(NCMP) * CMP_STRIDE + CMP_BLOCK - 1
    for t in range(T):
        dist = ((t * P + i[:, None]) - ends[None, :]).astype(np.float32)
        bias = np.where(dist[:, None, :] >= 0, -slope[None, :, None] * dist[:, None, :], np.float32(NEG))
        a = C_CMPBIAS + t * NSA_HEADS * NCMP
        c[:, a:a + NSA_HEADS * NCMP] = bias.reshape(P, -1)
        a = C_CMPMASK + t * NCMP
        c[:, a:a + NCMP] = dist >= 0
    return c


def wide(ap, axis, n):
    shape = list(ap.shape)
    shape[axis] = n
    return ap.broadcast_to(tuple(shape))


class Steps:

    def __init__(self, eng, sem):
        self.eng, self.sem, self.n, self.turn = eng, sem, 0, 0

    def __call__(self, ins):
        self.n += 1
        ins.then_inc(self.sem, 1)

    def wait(self):
        self.eng.wait_ge(self.sem, self.turn + self.n)

    def enter(self, i, per):
        self.turn = 0 if isinstance(i, int) else (i - 1) * per
        self.start, self.per = self.n, per

    def leave(self, turns):
        assert self.n - self.start == self.per, (self.n - self.start, self.per)
        self.n, self.turn = self.n + (turns - 1) * self.per, 0


def build(nc, a):
    with ExitStack() as ctx:
        def sb(name, shape, dt=F32):
            return ctx.enter_context(nc.sbuf_tensor(name, shape, dt))

        def sem(name):
            return ctx.enter_context(nc.semaphore(name))

        psum = ctx.enter_context(nc.psum_tensor("psum", [P, 8, 512], F32))
        ring = sb("ring", [P, RING, D])
        h_nat = sb("h_nat", [P, T, D])
        hT_hi = sb("hT_hi", [P, KC, SEQ], F32R)
        hT_lo = sb("hT_lo", [P, KC, SEQ], F32R)
        slab_hi = sb("slab_hi", [P, 2, D], F32R)
        slab_lo = sb("slab_lo", [P, 2, D], F32R)
        weighted_hi = sb("weighted_hi", [P, 2, SEQ], F32R)
        weighted_lo = sb("weighted_lo", [P, 2, SEQ], F32R)
        big = sb("big", [P, SEQ * KEYS])
        const = sb("const", [P, C_ALL])
        hidden = sb("hidden", [P, 2, SEQ])
        pairsT = sb("pairsT", [P, 3, SEQ])
        hot2 = sb("hot2", [P, 8, KEYS])
        hot1 = sb("hot1", [P, 8, KEYS])
        small = sb("small", [P, 32])

        used = [0]

        def view(n):
            used[0] += n
            assert used[0] <= SEQ * KEYS
            return big[:, used[0] - n:used[0]]

        G = big[:, :].rearrange("p (e t) -> p e t", t=SEQ)
        mixT = view(KC * SEQ).rearrange("p (c t) -> p c t", c=KC)
        hT = view(KC * SEQ).rearrange("p (c t) -> p c t", c=KC)
        shared = used[0]
        uT = view(UT * SEQ).rearrange("p (c t) -> p c t", c=UT)
        v_nat = view(T * SB_PAIRS * P).rearrange("p (t n) -> p t n", t=T)
        b_lay = view(ST * 2 * P).rearrange("p (j r n) -> p j r n", j=ST, r=2)
        c_lay = view(ST * 2 * P).rearrange("p (j r n) -> p j r n", j=ST, r=2)
        glu_w = view(UT * UT * P).rearrange("p (c n) -> p c n", c=UT)
        s5_par = view(3 * ST + 2 * UT)
        phase = view(2 * ST * SEQ).rearrange("p (r j t) -> p r j t", r=2, j=ST)
        drive = view(2 * ST * SEQ).rearrange("p (r j t) -> p r j t", r=2, j=ST)
        turned = view(2 * ST * SEQ).rearrange("p (r j t) -> p r j t", r=2, j=ST)
        temp = view(2 * ST * SEQ).rearrange("p (r j t) -> p r j t", r=2, j=ST)
        s5_small = view(24 * ST).rearrange("p (n j) -> p n j", j=ST)
        qk = view(4 * SEQ).rearrange("p (n t) -> p n t", n=4)
        v_pair = view(2 * T * P).rearrange("p (n t d) -> p n t d", n=2, t=T)
        stick_flat = view(4 * 2 * 384)
        stick = stick_flat.rearrange("p (h n c) -> p h n c", h=4, n=2)
        yT = stick_flat[:, 0:3 * UT * SEQ].rearrange("p (n c t) -> p n c t", n=3, c=UT)
        used[0] = shared
        kvc = view(4 * SEQ).rearrange("p (n t) -> p n t", n=4)
        w1 = view(2 * CMP_BLOCK * P).rearrange("p (n o m) -> p n o m", n=2, o=CMP_BLOCK)
        w2 = view(2 * P).rearrange("p (n m) -> p n m", n=2)
        peT = view(2 * CMP_BLOCK).rearrange("p (n o) -> p n o", n=2)
        gate_w = view(KC * 48).rearrange("p (c n) -> p c n", c=KC)
        gates = view(T * 48).rearrange("p (t g n) -> p t g n", t=T, g=2)
        cmp_hid = view(2 * 2 * 2 * NCMP).rearrange("p (n f g m) -> p n f g m", n=2, f=2, g=2)
        cmp_bias = view(4).rearrange("p (n f) -> p n f", n=2)
        kcT = view(2 * NCMP).rearrange("p (g m) -> p g m", g=2)
        vc = view(2 * P).rearrange("p (g m) -> p g m", g=2)
        kc_now = view(NCMP)
        vc_now = view(P)
        kT = view(2 * SEQ).rearrange("p (n t) -> p n t", n=2)
        vN = view(2 * T * P).rearrange("p (n t d) -> p n t d", n=2, t=T)
        qT = view(4 * SEQ).rearrange("p (r t) -> p r t", r=4)
        pc = view(T * 8 * NCMP).rearrange("p (t h m) -> p t h m", t=T, h=8)
        pc_red = view(T * 8 * 2).rearrange("p (n t h) -> p n t h", n=2, t=T)
        prob = view(2 * 512).rearrange("p (s c) -> p s c", s=2)
        probT = view(2 * 512).rearrange("p (s c) -> p s c", s=2)
        pcT = view(2 * P).rearrange("p (s c) -> p s c", s=2)
        red = view(2 * 8).rearrange("p (s c) -> p s c", s=2)
        used[0] = shared
        scores = view(T * SUBS * KEYS).rearrange("p (t j k) -> p t j k", t=T, j=SUBS)
        sub_q = view(2 * SEQ).rearrange("p (s t) -> p s t", s=2)
        sub_top = view(T * SUBS * TOPK).rearrange("p (t j k) -> p t j k", t=T, j=SUBS)
        sub_idx = view(T * SUBS * TOPK).rearrange("p (t j k) -> p t j k", t=T, j=SUBS)
        sub_idf = view(T * SUBS * TOPK).rearrange("p (t j k) -> p t j k", t=T, j=SUBS)
        cand = view(T * TOPK * TOPK).rearrange("p (t c) -> p t c", t=T)
        best = view(T * PEER_HEADS * TOPK).rearrange("p (t h k) -> p t h k", t=T, h=PEER_HEADS)
        flat = view(T * PEER_HEADS * TOPK).rearrange("p (t h k) -> p t h k", t=T, h=PEER_HEADS)
        part = view(2 * PEER_HEADS * TOPK).rearrange("p (s c) -> p s c", s=2)
        partf = view(2 * PEER_HEADS * TOPK).rearrange("p (s c) -> p s c", s=2)
        match = view(PEER_HEADS * TOPK * TOPK).rearrange("p (h k c) -> p h k c", h=PEER_HEADS, k=TOPK)
        pairs = view(3 * PEER_HEADS * TOPK).rearrange("p (n c) -> p n c", n=3)
        soft_red = view(2 * PEER_HEADS).rearrange("p (n h) -> p n h", n=2)
        keysT = view(SUBS * KEYS).rearrange("p (j k) -> p j k", j=SUBS)
        used[0] = shared
        squares = view(T * D).rearrange("p (t d) -> p t d", t=T)
        ln_rows = (used[0] // SEQ, used[0] // SEQ + 2 * D // SEQ)
        ln_par = view(2 * D).rearrange("p (k d) -> p k d", k=2)

        ident = const[:, C_IDENT:C_IDENT + P]
        neg_tri = const[:, C_TRI:C_TRI + P]
        neg_ones = const[:, C_ONES:C_ONES + P]
        below = const[:, C_BELOW:C_BELOW + P]
        neg_diag = const[:, C_NEGDIAG:C_NEGDIAG + P]
        iota = const[:, C_IOTA:C_IOTA + P]
        iota16 = const[:, C_IOTA16:C_IOTA16 + TOPK]

        names = """const_loaded x_loaded xT_loaded s5_loaded ln_loaded keys_loaded nsa_loaded out_stored dumped
            slab_done proj_copied hi_done split_done hidden_hi hidden_lo raw_weighted
            act_steps dve_steps pool_steps
            ln_sum ln_mean ln_square ln_var ln_rstd ln_done ln_turned ln_copied
            s5_dt s5_rates s5_mag s5_angle s5_sine s5_tables s5_pq s5_pq_used s5_states s5_y s5_y_in s5_gelu s5_z s5_gate s5_out
            v_staged z_ready z_log stick_ready tails_ready masked stick_w pv_ready o_copied
            cmp_ready cmp_hidden cmp_kv cmp_kv_copied gate_ready gate_done cmp_staged cmp_scores cmp_shifted cmp_exp cmp_aux cmp_probs
            sel_scores sel_biased sel_exp sel_prob sel_turned sel_copied sel_out sel_stored
            score_ready score_copied route_exp_in route_exp route_out route_turned route_copied
            hot_ready g_ready g_copied hidden_ready weighted_ready""".split()
        S = {n: sem(n) for n in names}
        slab_loaded = [sem(f"slab_loaded{s}") for s in range(RING)]
        slab_done, proj_copied, split_done = S["slab_done"], S["proj_copied"], S["split_done"]
        block = ctx.enter_context(nc.Block())

        def base(layer):
            return layer * PER_LAYER

        @block.sync
        def _(sp):
            sp.dma_start(hT[:, :, :], a["xT"]).then_inc(S["xT_loaded"], 16)
            for s in range(RING):
                sp.dma_start(ring[:, s, :], a["slabs"][s]).then_inc(slab_loaded[s], 16)
            for layer in range(LAYERS):
                first, experts = layer * PER_LAYER // RING, (PER_LAYER - EXP) // RING
                if layer:
                    for s in range(RING):
                        sp.wait_ge(split_done, 2 * (layer * EXP + s + 1 - RING))
                        sp.dma_start(ring[:, s, :], a["slabs"][first * RING + s]).then_inc(slab_loaded[s], 16)
                with sp.Fori(first + 1, first + experts + 1) as r:
                    for s in range(RING):
                        sp.wait_ge(slab_done, r * RING + (s + 1 - RING))
                        sp.dma_start(ring[:, s, :], a["slabs"][r * RING + s]).then_inc(slab_loaded[s], 16)
                with sp.Fori(1, EXP // RING) as r:
                    for s in range(RING):
                        sp.wait_ge(split_done, r * (2 * RING) + 2 * (layer * EXP + s + 1 - RING))
                        sp.dma_start(ring[:, s, :], a["slabs"][r * RING + ((first + experts) * RING + s)]).then_inc(
                            slab_loaded[s], 16)
            for t in range(T):
                sp.wait_ge(S["ln_done"], 2 * LAYERS * T - T + t + 1)
                sp.dma_start(a["out"][t * P:(t + 1) * P, :], h_nat[:, t, :]).then_inc(S["out_stored"], 16)
            sp.wait_ge(S["out_stored"], 16 * T)

        @block.tensor
        def _(pe):
            def landed(n):
                return (n // RING + 1) * 16

            def slab(slot, count):
                pe.wait_ge(slab_loaded[slot], count)
                return ring[:, slot, :]

            def project(n, slot, turn, pi, natural=False):
                w = slab(slot, turn * 16 + landed(n))
                w = w.rearrange("p (c n) -> p c n", c=KC)
                if not isinstance(pi, int) or pi >= 2:
                    pe.wait_ge(proj_copied, pi - 1)
                out = psum[:, 4 + slot % 2, 0:SEQ]
                if natural:
                    for t in range(T):
                        for c in range(KC):
                            last = pe.matmul(out[:, t * P:(t + 1) * P], hT[:, c, t * P:(t + 1) * P], w[:, c, :],
                                             start=(c == 0), stop=(c == KC - 1))
                else:
                    for c in range(KC):
                        last = pe.matmul(out, w[:, c, :], hT[:, c, :], start=(c == 0), stop=(c == KC - 1))
                last.then_inc(slab_done, 1)

            def accumulate(w, rows, first, last):
                for t in range(T):
                    for n in range(2):
                        mm = pe.matmul(psum[:, 2 * t + n, :], rows[:, t * P:(t + 1) * P], w[:, n * 512:(n + 1) * 512],
                                       start=first, stop=last)
                mm.then_inc(slab_done, 1)

            def turn_hidden(ln):
                pe.wait_ge(S["ln_done"], T * (ln + 1))
                for b in range(4):
                    for k in range(2):
                        for t in range(T):
                            mm = pe.transpose(psum[:, b, k * SEQ + t * P:k * SEQ + (t + 1) * P],
                                              h_nat[:, t, (2 * b + k) * P:(2 * b + k + 1) * P], ident)
                    mm.then_inc(S["ln_turned"], 1)

            def s5_inputs():
                pe.wait_ge(S["s5_loaded"], 5 * 16)
                pe.wait_ge(proj_copied, UT)
                for j in range(ST):
                    if j >= 2:
                        pe.wait_ge(S["s5_pq_used"], j - 1)
                    for r in range(2):
                        mm = pe.matmul(psum[:, 6 + j % 2, r * SEQ:(r + 1) * SEQ], b_lay[:, j, r, :], uT[:, j // 4, :],
                                       start=(r == 0), stop=True, skip_group_check=True)
                    mm.then_inc(S["s5_pq"], 1)
                pe.wait_ge(S["s5_pq_used"], ST)

            def s5_outputs():
                pe.wait_ge(S["s5_states"], 1)
                first = True
                for c in range(UT):
                    for j in range(4 * c, 4 * c + 4):
                        for r in range(2):
                            mm = pe.matmul(psum[:, 3, c * SEQ:(c + 1) * SEQ], c_lay[:, j, r, :], turned[:, r, j, :],
                                           start=first, stop=(j == 4 * c + 3 and r == 1), skip_group_check=True)
                            first = False
                mm.then_inc(S["s5_y"], 1)
                pe.wait_ge(S["s5_gelu"], 1)
                first = True
                for c in range(UT):
                    for k in range(UT):
                        mm = pe.matmul(psum[:, 2, c * SEQ:(c + 1) * SEQ], glu_w[:, k, c * P:(c + 1) * P],
                                       yT[:, 1, k, :], start=first, stop=(k == UT - 1), skip_group_check=True)
                        first = False
                mm.then_inc(S["s5_z"], 1)

            def stick_logits(i, pr):
                pe.wait_ge(proj_copied, i * 4 + (8 + 2 * pr + 2))
                for h in range(2):
                    z = psum[:, (6 if pr == 0 else 0) + h, :]
                    lo, hi = 64 * h, 64 * h + 64
                    q, k = qk[lo:hi, 2 * pr, :], qk[lo:hi, 2 * pr + 1, :]
                    pe.matmul(z[:, 0:P], k[:, 0:P], q[:, 0:P], start=True, stop=False, skip_group_check=True)
                    pe.matmul(z[:, P:2 * P], k[:, P:SEQ], q[:, P:SEQ], start=False, stop=False, skip_group_check=True)
                    pe.matmul(z[:, 2 * P:3 * P], k[:, 0:P], q[:, P:SEQ], start=False, stop=False,
                              skip_group_check=True).then_inc(S["z_ready"], 1)

            def stick_tails(i, pr):
                for h in range(2):
                    pe.wait_ge(S["stick_ready"], i * 4 + (2 * pr + h + 1))
                    z = psum[:, (6 if pr == 0 else 0) + h, :]
                    s = stick[:, 2 * pr + h, 0, :]
                    pe.matmul(z[:, 0:2 * P], neg_tri, s[:, 0:2 * P], start=False, stop=False, skip_group_check=True)
                    pe.matmul(z[:, 2 * P:3 * P], neg_tri, s[:, 2 * P:3 * P], start=False, stop=False,
                              skip_group_check=True)
                    pe.matmul(z[:, 2 * P:3 * P], neg_ones, s[:, P:2 * P], start=False, stop=True,
                              skip_group_check=True).then_inc(S["tails_ready"], 1)

            def stick_values(i, pr):
                pe.wait_ge(S["v_staged"], i * 2 + (pr + 1))
                pe.wait_ge(S["o_copied"], i * 4 + 2 * pr)
                for h in range(2):
                    pe.wait_ge(S["stick_w"], i * 4 + (2 * pr + h + 1))
                    w = stick[:, 2 * pr + h, 1, :]
                    o = psum[:, 2, h * SEQ:(h + 1) * SEQ]
                    pe.matmul(o[:, 0:P], v_pair[:, pr, 0, :], w[:, 0:P], start=(h == 0), stop=True,
                              skip_group_check=True)
                    pe.matmul(o[:, P:SEQ], v_pair[:, pr, 1, :], w[:, P:2 * P], start=False, stop=False,
                              skip_group_check=True)
                    mm = pe.matmul(o[:, P:SEQ], v_pair[:, pr, 0, :], w[:, 2 * P:3 * P], start=False, stop=True,
                                   skip_group_check=True)
                mm.then_inc(S["pv_ready"], 1)

            def even_mixer():
                pe.wait_ge(S["xT_loaded"], 16)
                for n in range(UT):
                    project(n, n % RING, 0, n)
                for n in range(UT, 8):
                    project(n, n % RING, 0, n, natural=True)
                s5_inputs()
                def turn(i):
                    for pr in range(2):
                        for m in range(2):
                            n = 8 + 2 * pr + m
                            project(n, n % RING, i, i * 4 + n)
                        if pr == 0:
                            stick_logits(i, 0)
                    stick_tails(i, 0)
                    stick_logits(i, 1)
                    stick_values(i, 0)
                    stick_tails(i, 1)
                    stick_values(i, 1)

                turn(0)
                with pe.Fori(1, SB_PAIRS // 2) as i:
                    turn(i)
                s5_outputs()
                pe.wait_ge(S["o_copied"], 2 * SB_PAIRS)
                pe.wait_ge(S["s5_out"], UT)

            def compress():
                pe.wait_ge(S["nsa_loaded"], 7 * 16)
                pe.wait_ge(proj_copied, PROJ_PER_LAYER + 4)
                pe.wait_ge(S["const_loaded"], 16)
                for n in range(2):
                    src = kvc[:, 2 * n:2 * n + 2, :].rearrange("p g (b o) -> p g b o", o=CMP_STRIDE)
                    for f in range(2):
                        rows, bank = slice(64 * f, 64 * f + 64), 3 * f
                        for o in range(CMP_BLOCK):
                            b = o // CMP_STRIDE
                            pe.matmul(psum[:, bank, n * 2 * NCMP:(n + 1) * 2 * NCMP], w1[rows, n, o, :],
                                      src[rows, :, b:b + NCMP, o % CMP_STRIDE], start=(n == 0 and o == 0),
                                      stop=(o == CMP_BLOCK - 1), skip_group_check=True)
                        for o in range(CMP_BLOCK):
                            mm = pe.matmul(psum[:, bank, 480 + n:481 + n], w1[rows, n, o, :],
                                           peT[rows, n, o:o + 1], start=False, stop=(o == CMP_BLOCK - 1),
                                           skip_group_check=True)
                        mm.then_inc(S["cmp_ready"], 1)
                pe.wait_ge(S["cmp_hidden"], 4)
                pe.matmul(psum[:, 1, 0:4 * NCMP], w2[:, 0, :],
                          cmp_hid[:, 0, :, :, :].rearrange("p f g m -> p (f g m)"), start=True, stop=True,
                          skip_group_check=True)
                for f in range(2):
                    for g in range(2):
                        mm = pe.matmul(psum[0:NCMP, 1, 128 + g * P + 64 * f:128 + g * P + 64 * f + 64],
                                       cmp_hid[:, 1, f, g, :], w2[:, 1, 0:64], start=False, stop=True,
                                       skip_group_check=True)
                mm.then_inc(S["cmp_kv"], 1)
                for t in range(T):
                    for c in range(KC):
                        mm = pe.matmul(psum[:, 2, 48 * t:48 * t + 48], hT[:, c, t * P:(t + 1) * P], gate_w[:, c, :],
                                       start=(c == 0 and t == 0), stop=(c == KC - 1), skip_group_check=True)
                mm.then_inc(S["gate_ready"], 1)

            def nsa_scores(i, s):
                r, half, t = s // 4, s // 2 % 2, s % 2
                if s >= 2:
                    pe.wait_ge(S["sel_biased"], i * 16 + (s - 1))
                rows, n = slice(64 * half, 64 * half + 64), P * (t + 1)
                for br in range(2):
                    mm = pe.matmul(psum[:, 6 + s % 2, br * n:(br + 1) * n], qT[rows, r, t * P:(t + 1) * P],
                                   kT[rows, br, 0:n], start=(br == 0), stop=True, skip_group_check=True)
                mm.then_inc(S["sel_scores"], 1)

            def nsa_turn(i, s):
                r, half, t = s // 4, s // 2 % 2, s % 2
                pe.wait_ge(S["sel_prob"], i * 16 + (s + 1))
                if s >= 2:
                    pe.wait_ge(S["sel_copied"], i * 16 + (s - 1))
                if s == 0:
                    pe.wait_ge(S["cmp_probs"], i + 1)
                    pe.wait_ge(S["sel_copied"], i * 16)
                pe.transpose(psum[0:NCMP, 3, 256 + P * (s % 2):256 + P * (s % 2) + P], pc[:, t, 2 * r + half, :], ident)
                for m in range(2 * (t + 1)):
                    mm = pe.transpose(psum[:, s % 2, m * P:(m + 1) * P], prob[:, s % 2, m * P:(m + 1) * P], ident)
                mm.then_inc(S["sel_turned"], 1)

            def nsa_values(i, s):
                r, half, t = s // 4, s // 2 % 2, s % 2
                pe.wait_ge(S["sel_copied"], i * 16 + (s + 1))
                if s % 4 == 0:
                    pe.wait_ge(S["sel_stored"], i * 8 + 2 * (s // 4))
                out = psum[:, 2, half * SEQ + t * P:half * SEQ + (t + 1) * P]
                first = s % 4 == 0
                for br in range(2):
                    for k in range(t + 1):
                        m = br * (t + 1) + k
                        pe.matmul(out, vN[:, br, k, :], probT[:, s % 2, m * P:(m + 1) * P], start=first, stop=False,
                                  skip_group_check=True)
                        first = False
                pe.matmul(out, vc_now[0:NCMP, :], pcT[0:NCMP, s % 2, :], start=False, stop=True,
                          skip_group_check=True).then_inc(S["sel_out"], 1)

            def odd_mixer(layer):
                b, p = base(layer), layer * PROJ_PER_LAYER
                for n in range(4):
                    project(b + n, n % RING, 0, p + n)
                compress()
                pe.wait_ge(S["gate_done"], 1)
                pe.wait_ge(S["cmp_kv_copied"], 4)
                def turn(i):
                    for m in range(8):
                        n = 4 + m
                        project(b + n, n % RING, i * 2, i * 8 + (p + n), natural=m in (2, 3))
                    pe.wait_ge(proj_copied, i * 8 + (p + 12))
                    pe.wait_ge(S["cmp_staged"], i * 2 + 2)
                    pe.wait_ge(S["sel_copied"], i * 16)
                    for t in range(T):
                        for r in range(4):
                            for half in range(2):
                                rows = slice(64 * half, 64 * half + 64)
                                c = (t * 4 + r) * NCMP
                                mm = pe.matmul(psum[:, 3 * half, c:c + NCMP], qT[rows, r, t * P:(t + 1) * P],
                                               kc_now[rows, :], start=(c == 0), stop=True, skip_group_check=True)
                    mm.then_inc(S["cmp_scores"], 1)
                    nsa_scores(i, 0)
                    for s in range(16):
                        if s + 1 < 16:
                            nsa_scores(i, s + 1)
                        nsa_turn(i, s)
                        nsa_values(i, s)

                turn(0)
                with pe.Fori(1, 2) as i:
                    turn(i)
                pe.wait_ge(S["sel_stored"], 16)

            def out_projection(layer):
                b = base(layer) + PROJ
                for c in range(OUTW):
                    accumulate(slab((b + c) % RING, landed(b + c)), mixT[:, c, :], c == 0, c == OUTW - 1)

            def route_scores(layer):
                b, p = base(layer) + PROJ + OUTW, layer * PROJ_PER_LAYER + PROJ
                pe.wait_ge(S["ln_copied"], (2 * layer + 1) * 4)
                pe.wait_ge(S["keys_loaded"], 16 * (layer + 1))
                def turn(i):
                    for pr in range(2):
                        for m in range(2):
                            s = 2 * pr + m
                            project(b + s, s, i, i * 4 + (p + s))
                        for m in range(2):
                            s = 2 * pr + m
                            pe.wait_ge(proj_copied, i * 4 + (p + s + 1))
                            if layer == 0:
                                pe.wait_ge(S["score_copied"], i * 4 + max(s - 1, 0))
                            else:
                                pe.wait_ge(S["score_copied"], i * 4 + (SUBS * layer + s - 1))
                            for t in range(T):
                                mm = pe.matmul(psum[:, 6 + m, t * P:(t + 1) * P], sub_q[:, m, t * P:(t + 1) * P],
                                               keysT[:, i * 4 + s, :], start=(t == 0), stop=True,
                                               skip_group_check=True)
                            mm.then_inc(S["score_ready"], 1)

                turn(0)
                with pe.Fori(1, WQ // RING) as i:
                    turn(i)

            def spread(layer):
                for t in range(T):
                    pe.wait_ge(S["route_out"], layer * T + t + 1)
                    for n in range(3):
                        mm = pe.transpose(psum[:, 6 + t, n * P:(n + 1) * P], pairs[:, n, :], ident)
                    mm.then_inc(S["route_turned"], 1)
                def turn(i):
                    for q in range(2):
                        k = layer * (SEQ // 4) + q
                        pe.wait_ge(S["hot_ready"], i * 2 + (k + 1))
                        if layer or q:
                            pe.wait_ge(S["g_copied"], i * 2 + (k - 1))
                        else:
                            pe.wait_ge(S["g_copied"], i * 2)
                        for m in range(4):
                            mm = pe.matmul(psum[:, 6 + q, m * KEYS:(m + 1) * KEYS], hot2[:, 4 * q + m, :],
                                           hot1[:, 4 * q + m, :], start=(m == 0), stop=True, skip_group_check=True)
                        mm.then_inc(S["g_ready"], 1)

                turn(0)
                with pe.Fori(1, SEQ // 8) as i:
                    turn(i)

            def experts(layer):
                b, w = base(layer) + PROJ + OUTW + WQ, layer * KEYS

                def up(slot, split, e):
                    out = psum[:, 4 + e[0], 0:SEQ]
                    if e[1] is not None:
                        pe.wait_ge(S["hidden_ready"], e[1])
                    hi = slab_hi[:, slot % 2, :].rearrange("p (c n) -> p c n", c=KC)
                    lo = slab_lo[:, slot % 2, :].rearrange("p (c n) -> p c n", c=KC)
                    for c in range(KC):
                        if c % (KC // 2) == 0:
                            pe.wait_ge(split_done, split + 1 + 2 * c // KC)
                        pe.matmul(out, hi[:, c, :], hT_hi[:, c, :], start=(c == 0), stop=False)
                        pe.matmul(out, hi[:, c, :], hT_lo[:, c, :], start=False, stop=False)
                        mm = pe.matmul(out, lo[:, c, :], hT_hi[:, c, :], start=False, stop=(c == KC - 1))
                    mm.then_inc(slab_done, 1)

                def down(slot, split, parity, e, first=False, last=False):
                    pe.wait_ge(S["weighted_ready"], e)
                    for n in range(2):
                        pe.wait_ge(split_done, split + 1 + n)
                        hi = slab_hi[:, slot % 2, n * 512:(n + 1) * 512]
                        lo = slab_lo[:, slot % 2, n * 512:(n + 1) * 512]
                        for t in range(T):
                            out, tok = psum[:, 2 * t + n, :], slice(t * P, (t + 1) * P)
                            pe.matmul(out, weighted_hi[:, parity, tok], hi, start=first, stop=False)
                            pe.matmul(out, weighted_hi[:, parity, tok], lo, start=False, stop=False)
                            mm = pe.matmul(out, weighted_lo[:, parity, tok], hi, start=False, stop=last)
                    mm.then_inc(slab_done, 1)

                z = 2 * layer * EXP
                pe.wait_ge(S["hidden_lo"], 4 * (layer + 1))
                up(0, z, (0, None))
                up(1, z + 2, (1, None))
                down(2, z + 4, 0, w + 1, first=True)
                up(3, z + 6, (0, w + 1))
                with pe.Fori(1, EXP // RING - 1) as k:
                    down(0, k * 8 + z, 1, k * 2 + w)
                    up(1, k * 8 + (z + 2), (1, k * 2 + w))
                    down(2, k * 8 + (z + 4), 0, k * 2 + (w + 1))
                    up(3, k * 8 + (z + 6), (0, k * 2 + (w + 1)))
                down(0, z + 504, 1, w + 126)
                up(1, z + 506, (1, w + 126))
                down(2, z + 508, 0, w + 127)
                down(3, z + 510, 1, w + 128, last=True)

            pe.wait_ge(S["const_loaded"], 16)
            for layer in range(LAYERS):
                even_mixer() if layer == 0 else odd_mixer(layer)
                out_projection(layer)
                turn_hidden(2 * layer)
                route_scores(layer)
                spread(layer)
                experts(layer)
                if layer + 1 < LAYERS:
                    turn_hidden(2 * layer + 1)
                    pe.wait_ge(S["ln_copied"], (2 * layer + 2) * 4)

        @block.scalar
        def _(act):
            step = Steps(act, S["act_steps"])

            def copy_proj(n, dst, scale=1.0, natural=None):
                act.wait_ge(slab_done, n[0])
                src = psum[:, 4 + n[1], 0:SEQ]
                if natural is not None:
                    src = src.rearrange("p (t d) -> p t d", t=T)
                act.activation(dst, src, ACT.Copy, scale=scale).then_inc(proj_copied, 1)

            def layer_norm(layer, which):
                ln = 2 * layer + which
                for t in range(T):
                    act.wait_ge(S["ln_mean"], T * ln + t + 1)
                    act.activation(squares[:, t, :], h_nat[:, t, :], ACT.Square, bias=small[:, 8 + t:9 + t],
                                   accum_out=small[:, 12 + t:13 + t]).then_inc(S["ln_square"], 1)
                for t in range(T):
                    act.wait_ge(S["ln_var"], T * ln + t + 1)
                    act.activation(small[:, 20 + t:21 + t], small[:, 16 + t:17 + t],
                                   ACT.Sqrt).then_inc(S["ln_rstd"], 1)

            def copy_hidden(ln, split):
                for b in range(4):
                    act.wait_ge(S["ln_turned"], 4 * ln + b + 1)
                    act.activation(hT[:, 2 * b:2 * b + 2, :], psum[:, b, :].rearrange("p (k t) -> p k t", k=2),
                                   ACT.Copy).then_inc(S["ln_copied"], 1)
                if split:
                    act.wait_ge(S["ln_copied"], 4 * (ln + 1))
                    for b in range(4):
                        act.activation(hT_hi[:, 2 * b:2 * b + 2, :], hT[:, 2 * b:2 * b + 2, :],
                                       ACT.Copy).then_inc(S["hidden_hi"], 1)

            def even_mixer():
                act.dma_start(s5_par[:, :], a["s5_par"]).then_inc(S["s5_loaded"], 16)
                act.dma_start(b_lay[:, :, :, :], a["s5_b"]).then_inc(S["s5_loaded"], 16)
                act.dma_start(c_lay[:, :, :, :], a["s5_c"]).then_inc(S["s5_loaded"], 16)
                act.dma_start(glu_w[:, :, :], a["glu_w"]).then_inc(S["s5_loaded"], 16)
                act.dma_start(h_nat[:, :, :], a["x"]).then_inc(S["s5_loaded"], 16)
                act.wait_ge(S["s5_loaded"], 5 * 16)
                act.activation(s5_small[:, 0, :], s5_par[:, 2 * ST:3 * ST], ACT.Exp).then_inc(S["s5_dt"], 1)
                act.wait_ge(S["s5_rates"], 1)
                act.activation(s5_small[:, 3, :], s5_small[:, 1, :], ACT.Exp).then_inc(S["s5_mag"], 1)
                act.wait_ge(S["s5_angle"], 1)
                act.activation(s5_small[:, 8, :], s5_small[:, 6, :], ACT.Sin).then_inc(S["s5_sine"], 1)
                act.activation(s5_small[:, 9, :], s5_small[:, 7, :], ACT.Sin).then_inc(S["s5_sine"], 1)
                for n in range(UT):
                    copy_proj((n + 1, n % 2), uT[:, n, :])
                for n in range(UT, 8):
                    copy_proj((n + 1, n % 2), v_nat[:, :, (n - UT) * P:(n - UT + 1) * P], natural=1)
                def turn(i):
                    def take(pr):
                        act.wait_ge(S["z_ready"], i * 4)
                        copy_proj((i * 4 + (9 + 2 * pr), 0), qk[:, 2 * pr, :], SCALE)
                        copy_proj((i * 4 + (10 + 2 * pr), 1), qk[:, 2 * pr + 1, :])

                    def logs(pr):
                        for h in range(2):
                            k = 2 * pr + h
                            z = psum[:, (6 if pr == 0 else 0) + h, 0:384]
                            s0, s1 = stick[:, k, 0, :], stick[:, k, 1, :]
                            act.wait_ge(S["z_ready"], i * 4 + (k + 1))
                            act.wait_ge(S["pv_ready"], i * 2)
                            step(act.activation(s1, z, ACT.Abs))
                            step.wait()
                            step(act.activation(s1, s1, ACT.Exp, scale=-1.0))
                            step.wait()
                            act.activation(s1, s1, ACT.Ln, bias=1.0).then_inc(S["z_log"], 1)

                    def weights(pr):
                        for h in range(2):
                            k = 2 * pr + h
                            z = psum[:, (6 if pr == 0 else 0) + h, 0:384]
                            act.wait_ge(S["masked"], i * 4 + (k + 1))
                            act.activation(stick[:, k, 1, :], z, ACT.Exp).then_inc(S["stick_w"], 1)

                    def store(pr):
                        act.wait_ge(S["pv_ready"], i * 2 + (pr + 1))
                        for h in range(2):
                            rows = slice(64 * h, 64 * h + 64)
                            act.activation(mixT[rows, i * 2 + (UT + pr), :], psum[rows, 2, h * SEQ:(h + 1) * SEQ],
                                           ACT.Copy).then_inc(S["o_copied"], 1)

                    step.enter(i, 8)
                    take(0)
                    logs(0)
                    take(1)
                    weights(0)
                    logs(1)
                    store(0)
                    weights(1)
                    store(1)

                turn(0)
                step.leave(1)
                with act.Fori(1, SB_PAIRS // 2) as i:
                    turn(i)
                step.leave(SB_PAIRS // 2 - 1)
                act.wait_ge(S["s5_y_in"], 1)
                act.activation(yT[:, 1, :, :], yT[:, 0, :, :], ACT.Gelu_apprx_tanh).then_inc(S["s5_gelu"], 1)
                act.wait_ge(S["s5_z"], 1)
                for c in range(UT):
                    act.activation(yT[:, 2, c, :], psum[:, 2, c * SEQ:(c + 1) * SEQ], ACT.Sigmoid,
                                   bias=s5_par[:, 3 * ST + UT + c:3 * ST + UT + c + 1]).then_inc(S["s5_gate"], 1)

            def odd_mixer(layer):
                b = base(layer)
                for n in range(4):
                    copy_proj((b + n + 1, n % 2), kvc[:, n, :])
                act.wait_ge(S["cmp_ready"], 4)
                for f in range(2):
                    step(act.activation(cmp_bias[:, :, f], psum[:, 3 * f, 480:482], ACT.Copy))
                step.wait()
                for n in range(2):
                    for f in range(2):
                        c = n * 2 * NCMP
                        act.activation(cmp_hid[:, n, f, :, :].rearrange("p g m -> p (g m)"),
                                       psum[:, 3 * f, c:c + 2 * NCMP], ACT.Gelu_apprx_tanh,
                                       bias=cmp_bias[:, n, f:f + 1]).then_inc(S["cmp_hidden"], 1)
                act.wait_ge(S["cmp_kv"], 1)
                for f in range(2):
                    rows = slice(64 * f, 64 * f + 64)
                    act.activation(kcT[rows, :, :].rearrange("p g m -> p (g m)"),
                                   psum[rows, 1, f * 2 * NCMP:(f + 1) * 2 * NCMP], ACT.Copy).then_inc(S["cmp_kv_copied"], 1)
                    act.activation(vc[0:NCMP, f, :], psum[0:NCMP, 1, 128 + f * P:256 + f * P],
                                   ACT.Copy).then_inc(S["cmp_kv_copied"], 1)
                act.wait_ge(S["gate_ready"], 1)
                act.activation(gates[:, :, :, :].rearrange("p t g n -> p (t g n)"), psum[:, 2, 0:96],
                               ACT.Sigmoid).then_inc(S["gate_done"], 1)
                act.wait_ge(S["cmp_kv_copied"], 4)
                def turn(i):
                    act.wait_ge(S["sel_out"], i * 16)
                    act.activation(kc_now[:, :], kcT[:, i, :], ACT.Copy).then_inc(S["cmp_staged"], 1)
                    act.activation(vc_now[0:NCMP, :], vc[0:NCMP, i, :], ACT.Copy).then_inc(S["cmp_staged"], 1)
                    for m in range(8):
                        n = (i * 8 + (b + 4 + m + 1), m % 2)
                        if m < 2:
                            copy_proj(n, kT[:, m, :])
                        elif m < 4:
                            copy_proj(n, vN[:, m - 2, :, :], natural=1)
                        else:
                            copy_proj(n, qT[:, m - 4, :], SCALE)
                    act.wait_ge(S["cmp_shifted"], i + 1)
                    act.activation(pc[:, :, :, :], pc[:, :, :, :], ACT.Exp).then_inc(S["cmp_exp"], 1)

                    def exps(s):
                        t = s % 2
                        n = P * (t + 1)
                        act.wait_ge(S["sel_biased"], i * 16 + (s + 1))
                        for br in range(2):
                            x = prob[:, s % 2, br * n:(br + 1) * n]
                            act.activation(x, x, ACT.Exp, bias=red[:, s % 2, br:br + 1],
                                           accum_out=red[:, s % 2, 2 + br:3 + br]).then_inc(S["sel_exp"], 1)

                    def turned_copy(s):
                        t = s % 2
                        act.wait_ge(S["sel_turned"], i * 16 + (s + 1))
                        n = 2 * P * (t + 1)
                        step(act.activation(pcT[0:NCMP, s % 2, :],
                                            psum[0:NCMP, 3, 256 + P * (s % 2):256 + P * (s % 2) + P], ACT.Copy))
                        step.wait()
                        act.activation(probT[:, s % 2, 0:n], psum[:, s % 2, 0:n], ACT.Copy).then_inc(S["sel_copied"], 1)

                    def store(s):
                        act.wait_ge(S["sel_out"], i * 16 + (s + 1))
                        for half in range(2):
                            rows = slice(64 * half, 64 * half + 64)
                            act.activation(mixT[rows, i * 4 + s // 4, :], psum[rows, 2, half * SEQ:(half + 1) * SEQ],
                                           ACT.Copy).then_inc(S["sel_stored"], 1)

                    step.enter(i, 16)
                    exps(0)
                    for s in range(16):
                        if s + 1 < 16:
                            exps(s + 1)
                        turned_copy(s)
                        if s % 4 == 3:
                            store(s)

                turn(0)
                step.leave(1)
                with act.Fori(1, 2) as i:
                    turn(i)
                step.leave(2 - 1)

            def route(layer):
                b = base(layer) + PROJ + OUTW
                def turn(i):
                    for s in range(RING):
                        if layer or s >= 2:
                            act.wait_ge(S["score_ready"], i * 4 + (layer * SUBS + s - 1))
                        else:
                            act.wait_ge(S["score_ready"], i * 4)
                        copy_proj((i * 4 + (b + s + 1), s % 2), sub_q[:, s % 2, :])

                turn(0)
                with act.Fori(1, WQ // RING) as i:
                    turn(i)
                for t in range(T):
                    act.wait_ge(S["route_exp_in"], layer * T + t + 1)
                    act.activation(pairs[:, 2, :], pairs[:, 2, :], ACT.Exp).then_inc(S["route_exp"], 1)
                def turn(i):
                    for q in range(2):
                        act.wait_ge(S["g_ready"], i * 2 + (layer * (SEQ // 4) + q + 1))
                        act.activation(G[:, :, bass.ds(i * 8 + 4 * q, 4)].rearrange("p e m -> p m e"),
                                       psum[:, 6 + q, :].rearrange("p (m e) -> p m e", m=4),
                                       ACT.Copy).then_inc(S["g_copied"], 1)

                turn(0)
                with act.Fori(1, SEQ // 8) as i:
                    turn(i)

            def experts(layer):
                b, w = base(layer) + PROJ + OUTW + WQ, layer * KEYS

                def high(slot, land, free):
                    act.wait_ge(slab_loaded[slot], land)
                    act.wait_ge(slab_done, free)
                    for n in range(2):
                        cols = slice(n * 512, (n + 1) * 512)
                        act.activation(slab_hi[:, slot % 2, cols], ring[:, slot, cols],
                                       ACT.Copy).then_inc(S["hi_done"], 1)

                def gelu(parity, done, free):
                    act.wait_ge(slab_done, done)
                    if free is not None:
                        act.wait_ge(S["weighted_ready"], free)
                    act.activation(hidden[:, parity, :], psum[:, 4 + parity, 0:SEQ],
                                   ACT.Gelu_apprx_tanh).then_inc(S["hidden_ready"], 1)

                land = (b // RING + 1) * 16
                high(0, land, b)
                high(1, land, b)
                high(2, land, b + 1)
                gelu(0, b + 1, None)

                def turn(k):
                    high(3, k * 16 + land, k * 4 + (b + 2))
                    gelu(1, k * 4 + (b + 2), k * 2 + w)
                    high(0, k * 16 + (land + 16), k * 4 + (b + 3))
                    high(1, k * 16 + (land + 16), k * 4 + (b + 4))
                    gelu(0, k * 4 + (b + 4), k * 2 + (w + 1))
                    high(2, k * 16 + (land + 16), k * 4 + (b + 5))

                turn(0)
                with act.Fori(1, KEYS // 2 - 1) as k:
                    turn(k)
                high(3, land + 16 * 63, b + 254)
                gelu(1, b + 254, w + 126)

            for layer in range(LAYERS):
                even_mixer() if layer == 0 else odd_mixer(layer)
                layer_norm(layer, 0)
                copy_hidden(2 * layer, True)
                route(layer)
                experts(layer)
                layer_norm(layer, 1)
                if layer + 1 < LAYERS:
                    copy_hidden(2 * layer + 1, False)

        @block.gpsimd
        def _(pool):
            step = Steps(pool, S["pool_steps"])
            pool.dma_start(const[:, :], a["const"]).then_inc(S["const_loaded"], 16)

            def load_ln(ln):
                for k in range(2):
                    pool.dma_start(ln_par[:, k, :], wide(a["ln"][2 * ln + k:2 * ln + k + 1, :], 0, P)).then_inc(
                        S["ln_loaded"], 16)

            def phases():
                pool.wait_ge(S["s5_sine"], 2)
                re, im = phase[:, 0, :, :], phase[:, 1, :, :]
                w = [s5_small[:, 16 + n, :] for n in range(4)]
                step(pool.memset(re[:, :, 0:1], 1.0))
                step(pool.memset(im[:, :, 0:1], 0.0))
                step(pool.tensor_copy(w[0], s5_small[:, 9, :]))
                step(pool.tensor_copy(w[1], s5_small[:, 8, :]))
                step.wait()
                n = 1
                while n < SEQ:
                    a0, b0 = re[:, :, 0:n], im[:, :, 0:n]
                    wr = wide(w[0][:, :].unsqueeze(2), 2, n)
                    wi = wide(w[1][:, :].unsqueeze(2), 2, n)
                    t0, t1 = temp[:, 0, :, 0:n], temp[:, 1, :, 0:n]
                    step(pool.tensor_tensor(t0, a0, wr, ALU.mult))
                    step(pool.tensor_tensor(t1, b0, wi, ALU.mult))
                    step.wait()
                    step(pool.tensor_tensor(re[:, :, n:2 * n], t0, t1, ALU.subtract))
                    step.wait()
                    step(pool.tensor_tensor(t0, a0, wi, ALU.mult))
                    step(pool.tensor_tensor(t1, b0, wr, ALU.mult))
                    step.wait()
                    step(pool.tensor_tensor(im[:, :, n:2 * n], t0, t1, ALU.add))
                    step(pool.tensor_tensor(w[2], w[0], w[0], ALU.mult))
                    step(pool.tensor_tensor(w[3], w[1], w[1], ALU.mult))
                    step(pool.tensor_tensor(w[1], w[0], w[1], ALU.mult))
                    step.wait()
                    step(pool.tensor_tensor(w[0], w[2], w[3], ALU.subtract))
                    step(pool.tensor_scalar(w[1], w[1], 2.0, None, ALU.mult))
                    step.wait()
                    n *= 2
                pool.memset(s5_small[:, 20, 0:1], 0.0).then_inc(S["s5_tables"], 1)

            phases()
            pool.wait_ge(proj_copied, 8)
            def turn(i):
                for pr in range(2):
                    pool.wait_ge(S["pv_ready"], i * 2)
                    pool.tensor_copy(v_pair[:, pr, :, :],
                                     v_nat[:, :, bass.ds(i * 2 * P + pr * P, P)]).then_inc(S["v_staged"], 1)

            turn(0)
            with pool.Fori(1, SB_PAIRS // 2) as i:
                turn(i)
            for layer in range(LAYERS):
                if layer:
                    pool.wait_ge(S["ln_done"], T * 2 * layer)
                    for dst, name in ((w1[0:64, 0], "w1k"), (w1[64:P, 0], "w1k"), (w1[0:64, 1], "w1v"),
                                      (w1[64:P, 1], "w1v"), (w2[:, :, :], "w2"), (peT[:, :, :], "pe"),
                                      (gate_w[:, :, :], "gate_w")):
                        pool.dma_start(dst, a[name]).then_inc(S["nsa_loaded"], 16)
                pool.wait_ge(slab_done, base(layer) + PROJ + 1)
                load_ln(2 * layer)
                pool.dma_start(keysT[:, :, :], a["keys"][layer]).then_inc(S["keys_loaded"], 16)
                pool.wait_ge(S["weighted_ready"], layer * KEYS + ln_rows[1])
                load_ln(2 * layer + 1)
            pool.wait_ge(S["ln_loaded"], 32 * 2 * LAYERS)
            pool.wait_ge(S["keys_loaded"], 16 * LAYERS)
            pool.wait_ge(S["nsa_loaded"], 7 * 16)

        @block.vector
        def _(dve):
            step = Steps(dve, S["dve_steps"])

            def run(ins):
                step(ins)
                step.wait()

            def layer_norm(layer, which):
                ln = 2 * layer + which
                done = base(layer) + (PROJ + OUTW if which == 0 else PER_LAYER)
                dve.wait_ge(slab_done, done)
                for t in range(T):
                    y = h_nat[:, t, :]
                    run(dve.scalar_tensor_tensor(out=y, in0=y, scalar=ALPHA,
                                                 in1=psum[:, 2 * t:2 * t + 2, :].rearrange("p a b -> p (a b)"),
                                                 op0=ALU.mult, op1=ALU.add, accum_out=small[:, 4 + t:5 + t]))
                    dve.tensor_scalar(small[:, 8 + t:9 + t], small[:, 4 + t:5 + t], -1.0 / D, None,
                                      ALU.mult).then_inc(S["ln_mean"], 1)
                for t in range(T):
                    dve.wait_ge(S["ln_square"], T * ln + t + 1)
                    run(dve.tensor_scalar(small[:, 16 + t:17 + t], small[:, 12 + t:13 + t], 1.0 / D, EPS,
                                          ALU.mult, ALU.add))
                    dve.reciprocal(small[:, 16 + t:17 + t], small[:, 16 + t:17 + t]).then_inc(S["ln_var"], 1)
                dve.wait_ge(S["ln_loaded"], 32 * (ln + 1))
                for t in range(T):
                    y = h_nat[:, t, :]
                    dve.wait_ge(S["ln_rstd"], T * ln + t + 1)
                    run(dve.tensor_scalar(y, y, small[:, 8 + t:9 + t], small[:, 20 + t:21 + t], ALU.add, ALU.mult))
                    run(dve.tensor_tensor(y, y, ln_par[:, 0, :], ALU.mult))
                    dve.tensor_tensor(y, y, ln_par[:, 1, :], ALU.add).then_inc(S["ln_done"], 1)
                dve.wait_ge(S["ln_done"], T * (ln + 1))

            def s5_rates():
                lr, li = s5_par[:, 0:ST], s5_par[:, ST:2 * ST]
                s = [s5_small[:, n, :] for n in range(24)]
                dt, rate, angle, mag, turns = s[0], s[1], s[2], s[3], s[4]
                dve.wait_ge(S["s5_dt"], 1)
                run(dve.tensor_tensor(angle, li, dt, ALU.mult))
                dve.tensor_tensor(rate, lr, dt, ALU.mult).then_inc(S["s5_rates"], 1)
                run(dve.tensor_scalar(turns, angle, 1.0 / TWO_PI, ROUND, ALU.mult, ALU.add))
                run(dve.tensor_scalar(turns, turns, -ROUND, None, ALU.add))
                for part_pi in (PI_A, PI_B, PI_C):
                    run(dve.scalar_tensor_tensor(out=angle, in0=turns, scalar=-part_pi, in1=angle, op0=ALU.mult,
                                                 op1=ALU.add))
                run(dve.tensor_scalar(s[6], angle, PI_IN, -PI_IN, ALU.min, ALU.max))
                run(dve.scalar_tensor_tensor(out=s[5], in0=s[6], scalar=-1.0, in1=s[6], op0=ALU.mult, op1=ALU.max))
                dve.tensor_scalar(s[7], s[5], -1.0, float(np.pi / 2), ALU.mult, ALU.add).then_inc(S["s5_angle"], 1)
                dve.wait_ge(S["s5_sine"], 2)
                sine, cosine, a_re, a_im, den, t0, f_re, f_im, nf = s[8], s[9], s[10], s[11], s[12], s[13], s[14], s[15], s[21]
                run(dve.tensor_tensor(a_re, mag, cosine, ALU.mult))
                run(dve.tensor_tensor(a_im, mag, sine, ALU.mult))
                run(dve.tensor_scalar(a_re, a_re, -1.0, None, ALU.add))
                run(dve.tensor_tensor(den, lr, lr, ALU.mult))
                run(dve.tensor_tensor(t0, li, li, ALU.mult))
                run(dve.tensor_tensor(den, den, t0, ALU.add))
                run(dve.reciprocal(den, den))
                run(dve.tensor_tensor(f_re, a_re, lr, ALU.mult))
                run(dve.tensor_tensor(t0, a_im, li, ALU.mult))
                run(dve.tensor_tensor(f_re, f_re, t0, ALU.add))
                run(dve.tensor_tensor(f_re, f_re, den, ALU.mult))
                run(dve.tensor_tensor(f_im, a_im, lr, ALU.mult))
                run(dve.tensor_tensor(t0, a_re, li, ALU.mult))
                run(dve.tensor_tensor(f_im, f_im, t0, ALU.subtract))
                run(dve.tensor_tensor(f_im, f_im, den, ALU.mult))
                run(dve.tensor_scalar(nf, f_im, -1.0, None, ALU.mult))
                return f_re, f_im, nf, mag

            def s5_scan():
                f_re, f_im, nf, mag = s5_rates()
                dve.wait_ge(S["s5_tables"], 1)
                for j in range(ST):
                    dve.wait_ge(S["s5_pq"], j + 1)
                    pq = psum[:, 6 + j % 2, :]
                    p, q = pq[:, 0:SEQ], pq[:, SEQ:2 * SEQ]
                    step(dve.tensor_scalar(temp[:, 0, j, :], q, nf[:, j:j + 1], None, ALU.mult))
                    run(dve.tensor_scalar(temp[:, 1, j, :], q, f_re[:, j:j + 1], None, ALU.mult))
                    step(dve.scalar_tensor_tensor(out=drive[:, 0, j, :], in0=p, scalar=f_re[:, j:j + 1],
                                                  in1=temp[:, 0, j, :], op0=ALU.mult, op1=ALU.add))
                    dve.scalar_tensor_tensor(out=drive[:, 1, j, :], in0=p, scalar=f_im[:, j:j + 1],
                                             in1=temp[:, 1, j, :], op0=ALU.mult, op1=ALU.add).then_inc(S["s5_pq_used"], 1)
                step.wait()
                dve.wait_ge(S["s5_pq_used"], ST)

                def flatten(x):
                    return x.rearrange("p j t -> p (j t)")

                pr, pi = flatten(phase[:, 0]), flatten(phase[:, 1])
                d_re, d_im = flatten(drive[:, 0]), flatten(drive[:, 1])
                z_re, z_im = flatten(turned[:, 0]), flatten(turned[:, 1])
                t0, t1 = flatten(temp[:, 0]), flatten(temp[:, 1])
                step(dve.tensor_tensor(z_re, pr, d_re, ALU.mult))
                step(dve.tensor_tensor(t0, pi, d_im, ALU.mult))
                step(dve.tensor_tensor(z_im, pr, d_im, ALU.mult))
                run(dve.tensor_tensor(t1, pi, d_re, ALU.mult))
                step(dve.tensor_tensor(z_re, z_re, t0, ALU.add))
                run(dve.tensor_tensor(z_im, z_im, t1, ALU.subtract))
                for j in range(ST):
                    for r in range(2):
                        step(dve.tensor_tensor_scan(drive[:, r, j, :], wide(mag[:, j:j + 1], 1, SEQ),
                                                    turned[:, r, j, :], 0.0, ALU.mult, ALU.add))
                step.wait()
                step(dve.tensor_tensor(z_re, pr, d_re, ALU.mult))
                step(dve.tensor_tensor(t0, pi, d_im, ALU.mult))
                step(dve.tensor_tensor(z_im, pr, d_im, ALU.mult))
                run(dve.tensor_tensor(t1, pi, d_re, ALU.mult))
                run(dve.tensor_tensor(z_re, z_re, t0, ALU.subtract))
                dve.scalar_tensor_tensor(out=z_im, in0=z_im, scalar=-1.0, in1=t1, op0=ALU.mult,
                                         op1=ALU.subtract).then_inc(S["s5_states"], 1)

            def even_mixer():
                dve.wait_ge(S["s5_loaded"], 5 * 16)
                dve.wait_ge(S["const_loaded"], 16)
                s5_scan()
                def turn(i):
                    def stick_sums(pr):
                        for h in range(2):
                            k = 2 * pr + h
                            z = psum[:, (6 if pr == 0 else 0) + h, 0:384]
                            s = stick[:, k, 0, :]
                            dve.wait_ge(S["z_log"], i * 4 + (k + 1))
                            run(dve.scalar_tensor_tensor(out=s, in0=z, scalar=0.0, in1=stick[:, k, 1, :],
                                                         op0=ALU.max, op1=ALU.add))
                            dve.tensor_tensor(s[:, 0:SEQ].rearrange("p (a b) -> p a b", a=2),
                                              s[:, 0:SEQ].rearrange("p (a b) -> p a b", a=2),
                                              wide(below.unsqueeze(1), 1, 2), ALU.mult).then_inc(
                                                  S["stick_ready"], 1)

                    def mask(pr):
                        for h in range(2):
                            k = 2 * pr + h
                            z = psum[:, (6 if pr == 0 else 0) + h, 0:SEQ].rearrange("p (a b) -> p a b", a=2)
                            dve.wait_ge(S["tails_ready"], i * 4 + (k + 1))
                            dve.tensor_tensor(z, z, wide(neg_diag.unsqueeze(1), 1, 2), ALU.add).then_inc(
                                S["masked"], 1)

                    step.enter(i, 4)
                    stick_sums(0)
                    mask(0)
                    stick_sums(1)
                    mask(1)

                turn(0)
                step.leave(1)
                with dve.Fori(1, SB_PAIRS // 2) as i:
                    turn(i)
                step.leave(SB_PAIRS // 2 - 1)
                dve.wait_ge(S["s5_y"], 1)
                for c in range(UT):
                    run(dve.scalar_tensor_tensor(out=yT[:, 0, c, :], in0=uT[:, c, :],
                                                 scalar=s5_par[:, 3 * ST + c:3 * ST + c + 1],
                                                 in1=psum[:, 3, c * SEQ:(c + 1) * SEQ], op0=ALU.mult, op1=ALU.add))
                dve.memset(small[:, 0:1], 0.0).then_inc(S["s5_y_in"], 1)
                for c in range(UT):
                    dve.wait_ge(S["s5_gate"], c + 1)
                    dve.tensor_tensor(mixT[:, c, :], yT[:, 1, c, :], yT[:, 2, c, :], ALU.mult).then_inc(S["s5_out"], 1)

            def odd_mixer():
                def turn(i):
                    step.enter(i, 8 + 16 * 6)
                    dve.wait_ge(S["gate_done"], 1)
                    dve.wait_ge(S["cmp_scores"], i + 1)
                    for t in range(T):
                        bias = const[:, bass.ds(i * (8 * NCMP) + (C_CMPBIAS + t * NSA_HEADS * NCMP), 8 * NCMP)]
                        bias = bias.rearrange("p (r f m) -> p r f m", r=4, f=2)
                        now = pc[:, t, :, :].rearrange("p (r f) m -> p r f m", f=2)
                        for f in range(2):
                            got = psum[:, 3 * f, t * 4 * NCMP:(t + 1) * 4 * NCMP].rearrange("p (r m) -> p r m", r=4)
                            step(dve.tensor_tensor(now[:, :, f, :], got, bias[:, :, f, :], ALU.add))
                    step.wait()
                    flat_pc = pc[:, :, :, :].rearrange("p t h m -> p (t h) m")
                    mx, sm = (pc_red[:, n, :, :].rearrange("p t h -> p (t h)") for n in range(2))
                    run(dve.tensor_reduce(mx, flat_pc, AX.X, ALU.max))
                    dve.tensor_tensor(flat_pc, flat_pc, wide(mx.unsqueeze(2), 2, NCMP),
                                      ALU.subtract).then_inc(S["cmp_shifted"], 1)
                    dve.wait_ge(S["cmp_exp"], i + 1)
                    for t in range(T):
                        keep = const[:, C_CMPMASK + t * NCMP:C_CMPMASK + (t + 1) * NCMP]
                        step(dve.tensor_tensor(pc[:, t, :, :], pc[:, t, :, :], wide(keep.unsqueeze(1), 1, 8),
                                               ALU.mult))
                    step.wait()
                    run(dve.tensor_reduce(sm, flat_pc, AX.X, ALU.add))
                    dve.tensor_scalar(sm, sm, 1e-30, None, ALU.max).then_inc(S["cmp_aux"], 1)
                    dve.wait_ge(S["cmp_aux"], i * 3 + 1)
                    dve.reciprocal(sm, sm).then_inc(S["cmp_aux"], 1)
                    dve.wait_ge(S["cmp_aux"], i * 3 + 2)
                    dve.tensor_tensor(pc_red[:, 1, :, :], pc_red[:, 1, :, :], gates[:, :, i, 0:8],
                                      ALU.mult).then_inc(S["cmp_aux"], 1)
                    dve.wait_ge(S["cmp_aux"], i * 3 + 3)
                    dve.tensor_tensor(flat_pc, flat_pc, wide(sm.unsqueeze(2), 2, NCMP),
                                      ALU.mult).then_inc(S["cmp_probs"], 1)

                    def biased(s):
                        r, half, t = s // 4, s // 2 % 2, s % 2
                        n = P * (t + 1)
                        dve.wait_ge(S["sel_scores"], i * 16 + (s + 1))
                        if s >= 2:
                            dve.wait_ge(S["sel_turned"], i * 16 + (s - 1))
                        d = C_DIST + (P if t else 0)
                        x = prob[:, s % 2, 0:2 * n].rearrange("p (b n) -> p b n", b=2)
                        h = 2 * r + half
                        run(dve.scalar_tensor_tensor(
                            out=x, in0=wide(const[:, d:d + n].unsqueeze(1), 1, 2),
                            scalar=const[:, bass.ds(i * 8 + (C_SLOPE + h), 1)],
                            in1=psum[:, 6 + s % 2, 0:2 * n].rearrange("p (b n) -> p b n", b=2),
                            op0=ALU.mult, op1=ALU.add))
                        dve.tensor_reduce(red[:, s % 2, 0:2], x, AX.X, ALU.max, negate=True).then_inc(
                            S["sel_biased"], 1)

                    def scaled(s):
                        r, half, t = s // 4, s // 2 % 2, s % 2
                        n, h = P * (t + 1), 2 * r + half
                        sums = red[:, s % 2, 2:4]
                        dve.wait_ge(S["sel_exp"], i * 32 + 2 * (s + 1))
                        run(dve.tensor_scalar(sums, sums, 1e-30, None, ALU.max))
                        run(dve.reciprocal(sums, sums))
                        for br in range(2):
                            g = 8 * (br + 1) + h
                            step(dve.tensor_tensor(sums[:, br:br + 1], sums[:, br:br + 1], gates[:, t, i, g:g + 1],
                                                   ALU.mult))
                        step.wait()
                        x = prob[:, s % 2, :]
                        run(dve.tensor_scalar(x[:, 0:n], x[:, 0:n], sums[:, 0:1], None, ALU.mult))
                        dve.tensor_scalar(x[:, n:2 * n], x[:, n:2 * n], sums[:, 1:2], None,
                                          ALU.mult).then_inc(S["sel_prob"], 1)

                    biased(0)
                    for s in range(16):
                        if s + 1 < 16:
                            biased(s + 1)
                        scaled(s)

                turn(0)
                step.leave(1)
                with dve.Fori(1, 2) as i:
                    turn(i)
                step.leave(2 - 1)

            def top16(rows):
                for values, best_out, index_out in rows:
                    step(dve.max(best_out[:, 0:8], values))
                step.wait()
                for values, best_out, index_out in rows:
                    step(dve.max_index(index_out[:, 0:8].bitcast(U32), best_out[:, 0:8], values))
                step.wait()
                for values, best_out, index_out in rows:
                    step(dve.match_replace(values, best_out[:, 0:8], values, NEG * 1e8))
                step.wait()
                for values, best_out, index_out in rows:
                    step(dve.max(best_out[:, 8:16], values))
                step.wait()
                for values, best_out, index_out in rows:
                    step(dve.max_index(index_out[:, 8:16].bitcast(U32), best_out[:, 8:16], values))
                step.wait()

            def route(layer):
                for b in range(4):
                    dve.wait_ge(S["hidden_hi"], 4 * layer + b + 1)
                    dve.tensor_tensor(hT_lo[:, 2 * b:2 * b + 2, :], hT[:, 2 * b:2 * b + 2, :],
                                      hT_hi[:, 2 * b:2 * b + 2, :].bitcast(F32), ALU.subtract).then_inc(
                                          S["hidden_lo"], 1)
                for h in range(PEER_HEADS):
                    for j in (2 * h, 2 * h + 1):
                        dve.wait_ge(S["score_ready"], layer * SUBS + j + 1)
                        dve.tensor_copy(scores[:, :, j, :], psum[:, 6 + j % 2, 0:SEQ].rearrange(
                            "p (t k) -> p t k", t=T)).then_inc(S["score_copied"], 1)
                        dve.wait_ge(S["score_copied"], layer * SUBS + j + 1)
                        top16([(scores[:, t, j, :], sub_top[:, t, j, :], sub_idx[:, t, j, :]) for t in range(T)])
                    for t in range(T):
                        step(dve.tensor_tensor(cand[:, t, :].rearrange("p (a b) -> p a b", a=TOPK),
                                               wide(sub_top[:, t, 2 * h, :].unsqueeze(2), 2, TOPK),
                                               wide(sub_top[:, t, 2 * h + 1, :].unsqueeze(1), 1, TOPK), ALU.add))
                    step.wait()
                    top16([(cand[:, t, :], best[:, t, h, :], flat[:, t, h, :]) for t in range(T)])
                run(dve.tensor_copy(sub_idf[:, :, :, :], sub_idx[:, :, :, :].bitcast(U32)))
                for t in range(T):
                    if t:
                        dve.wait_ge(S["route_turned"], layer * T + t)
                    g = pairs[:, 2, :].rearrange("p (h k) -> p h k", h=PEER_HEADS)
                    dve.tensor_tensor(g, best[:, t, :, :], wide(best[:, t, :, 0:1], 2, TOPK),
                                      ALU.subtract).then_inc(S["route_exp_in"], 1)
                    chosen = flat[:, t, :, :].rearrange("p h k -> p (h k)").bitcast(U32)
                    step(dve.tensor_scalar(part[:, 0, :].bitcast(U32), chosen, 4, None, ALU.logical_shift_right))
                    run(dve.tensor_scalar(part[:, 1, :].bitcast(U32), chosen, TOPK - 1, None, ALU.bitwise_and))
                    run(dve.tensor_copy(partf[:, :, :], part[:, :, :].bitcast(U32)))
                    idf = sub_idf[:, t, :, :].rearrange("p (h s) k -> p h s k", s=2)
                    for s in range(2):
                        m3 = match[:, :, :, :].rearrange("p h k c -> p (h k) c")
                        run(dve.tensor_tensor(m3, wide(partf[:, s, :].unsqueeze(2), 2, TOPK),
                                              wide(iota16.unsqueeze(1), 1, PEER_HEADS * TOPK), ALU.is_equal))
                        run(dve.tensor_tensor(match[:, :, :, :], match[:, :, :, :],
                                              wide(idf[:, :, s, :].unsqueeze(2), 2, TOPK), ALU.mult))
                        run(dve.tensor_reduce(pairs[:, s, :], m3, AX.X, ALU.add))
                    dve.wait_ge(S["route_exp"], layer * T + t + 1)
                    run(dve.tensor_reduce(soft_red[:, 0, :], g, AX.X, ALU.add))
                    run(dve.reciprocal(soft_red[:, 1, :], soft_red[:, 0, :]))
                    dve.tensor_tensor(g, g, wide(soft_red[:, 1, :].unsqueeze(2), 2, TOPK),
                                      ALU.mult).then_inc(S["route_out"], 1)
                for t in range(T):
                    dve.wait_ge(S["route_turned"], layer * T + t + 1)
                    run(dve.tensor_copy(pairsT[:, :, t * P:(t + 1) * P],
                                        psum[:, 6 + t, 0:3 * P].rearrange("p (n c) -> p n c", n=3)))
                def turn(i):
                    step.enter(i, 14)
                    for q in range(2):
                        k = layer * (SEQ // 4) + q
                        if layer or q:
                            dve.wait_ge(S["g_ready"], i * 2 + (k - 1))
                        else:
                            dve.wait_ge(S["g_ready"], i * 2)
                        for m in range(4):
                            tok = i * 8 + (4 * q + m)
                            step(dve.tensor_scalar(hot2[:, 4 * q + m, :], iota, pairsT[:, 1, bass.ds(tok, 1)], None,
                                                   ALU.is_equal))
                            ins = dve.tensor_scalar(hot1[:, 4 * q + m, :], iota, pairsT[:, 0, bass.ds(tok, 1)],
                                                    pairsT[:, 2, bass.ds(tok, 1)], ALU.is_equal, ALU.mult)
                            if m < 3:
                                step(ins)
                        ins.then_inc(S["hot_ready"], 1)

                turn(0)
                step.leave(1)
                with dve.Fori(1, SEQ // 8) as i:
                    turn(i)
                step.leave(SEQ // 8 - 1)

            def experts(layer):
                b, w = base(layer) + PROJ + OUTW + WQ, layer * KEYS
                dve.wait_ge(S["g_copied"], (layer + 1) * (SEQ // 4))

                def low(slot, high):
                    for n in range(2):
                        cols = slice(n * 512, (n + 1) * 512)
                        dve.wait_ge(S["hi_done"], high + 1 + n)
                        dve.tensor_tensor(slab_lo[:, slot % 2, cols], ring[:, slot, cols],
                                          slab_hi[:, slot % 2, cols].bitcast(F32), ALU.subtract).then_inc(
                                              split_done, 1)

                def weigh(parity, e, ready, free):
                    dve.wait_ge(S["hidden_ready"], ready)
                    if free is not None:
                        dve.wait_ge(slab_done, free)
                    x = hidden[:, parity, :]
                    dve.tensor_tensor(x, x, G[:, e, :], ALU.mult).then_inc(S["raw_weighted"], 1)
                    dve.wait_ge(S["raw_weighted"], ready)
                    step(dve.tensor_copy(weighted_hi[:, parity, :], x))
                    step.wait()
                    dve.tensor_tensor(weighted_lo[:, parity, :], x, weighted_hi[:, parity, :].bitcast(F32),
                                      ALU.subtract).then_inc(S["weighted_ready"], 1)

                z = 2 * layer * EXP
                low(0, z)
                low(1, z + 2)
                low(2, z + 4)
                weigh(0, 0, w + 1, None)

                def turn(k):
                    step.enter(k, 2)
                    low(3, k * 8 + (z + 6))
                    weigh(1, k * 2 + 1, k * 2 + (w + 2), k * 4 + (b + 1))
                    low(0, k * 8 + (z + 8))
                    low(1, k * 8 + (z + 10))
                    weigh(0, k * 2 + 2, k * 2 + (w + 3), k * 4 + (b + 3))
                    low(2, k * 8 + (z + 12))

                turn(0)
                step.leave(1)
                with dve.Fori(1, KEYS // 2 - 1) as k:
                    turn(k)
                step.leave(KEYS // 2 - 2)
                low(3, z + 510)
                weigh(1, KEYS - 1, w + KEYS, b + 253)

            for layer in range(LAYERS):
                even_mixer() if layer == 0 else odd_mixer()
                layer_norm(layer, 0)
                route(layer)
                experts(layer)
                layer_norm(layer, 1)


def _cols(w, order=None):
    w = w if order is None else w[:, order]
    return w.reshape(KC, P, -1, P).transpose(2, 1, 0, 3).reshape(-1, P, D)


def _rows(w):
    return w.reshape(-1, P, D)


def lay_out(x):
    even, odd = x["even_w_in"][0], x["odd_w_in"][0]
    c, n = GROUPS * CH, SB_PAIRS * P
    u, q, k, v = even[:, :c], even[:, c:c + n], even[:, c + n:c + 2 * n], even[:, c + 2 * n:]
    qk = np.stack([_cols(q), _cols(k)], 1).reshape(-1, P, D)
    even_slabs = [_cols(u), _cols(v), qk, _rows(x["even_w_out"][0])]
    order = np.array([((2 * p + half) * 4 + r) * HEAD + d for p in range(2) for r in range(4) for half in range(2)
                      for d in range(HEAD)])
    kv = [_cols(odd[:, D + 256 * m:D + 256 * (m + 1)]) for m in range(6)]
    qs = _cols(odd[:, order])
    kc, vc, ks, vs, kw, vw = kv
    odd_slabs = [kc, vc]
    for p in range(2):
        odd_slabs += [ks[p:p + 1], kw[p:p + 1], vs[p:p + 1], vw[p:p + 1], qs[4 * p:4 * p + 4]]
    odd_slabs.append(_rows(x["odd_w_out"][0][order]))
    slabs = []
    for layer, mixer in ((0, even_slabs), (1, odd_slabs)):
        slabs += mixer
        slabs.append(_cols(x["peer_w_q"][layer]))
        up = x["peer_u"][layer].reshape(KEYS, P, KC, P).transpose(0, 3, 2, 1).reshape(KEYS, P, D)
        down = _rows(x["peer_v"][layer])
        both = np.empty((EXP, P, D), np.float32)
        ups = [0] + [4 * k + 1 if e % 2 else 4 * k + 3 for e in range(1, KEYS) for k in [(e - 1) // 2]]
        downs = [4 * (e // 2) + 2 if e % 2 == 0 else 4 * ((e + 1) // 2) for e in range(KEYS)]
        ups[KEYS - 1], downs[KEYS - 1] = EXP - 3, EXP - 1
        both[ups], both[downs] = up, down
        slabs.append(both)
    lam = [x["even_lam_re"][0], x["even_lam_im"][0], np.repeat(x["even_log_dt"][0][:, None], STATE, 1)]
    lam = [m.reshape(ST, P).T for m in lam]
    par = np.concatenate(lam + [x["even_d"][0].reshape(UT, P).T, x["even_b_glu"][0].reshape(UT, P).T], 1)
    b_lay = np.zeros((P, ST, 2, P), np.float32)
    c_lay = np.zeros((P, ST, 2, P), np.float32)
    for g in range(GROUPS):
        j, s, ch = g // 2, (g % 2) * STATE, (g % 8) * CH
        for r, (bm, cm) in enumerate((("even_b_re", "even_c_re"), ("even_b_im", "even_c_im"))):
            b_lay[ch:ch + CH, j, r, s:s + STATE] = x[bm][0, g].T
            c_lay[s:s + STATE, j, r, ch:ch + CH] = x[cm][0, g].T
    gate = odd[:, D + 6 * 256:].reshape(D, NBR, 2, 2, 4).transpose(0, 2, 1, 4, 3).reshape(KC, P, 48).transpose(1, 0, 2)

    def dup(m):
        return np.concatenate([m, m], 0)

    w1 = {n: x[f"odd_w1_{n}"][0].reshape(CMP_BLOCK, HEAD, P).transpose(1, 0, 2) for n in "kv"}
    w2 = np.stack([np.concatenate([x[f"odd_w2_{n}"][0]] * 2, 1) for n in "kv"], 1)
    pe = np.stack([dup(x[f"odd_pe_{n}"][0].T) for n in "kv"], 1)
    keys = x["peer_sub_keys"].reshape(LAYERS, SUBS, KEYS, P).transpose(0, 3, 1, 2)
    ln = np.stack([x[n][layer] for layer in range(LAYERS) for k in (1, 2) for n in (f"ln{k}_g", f"ln{k}_b")])
    xs = x["x"][0]
    out = {
        "slabs": np.concatenate(slabs), "x": xs.reshape(T, P, D).transpose(1, 0, 2),
        "xT": xs.T.reshape(KC, P, SEQ).transpose(1, 0, 2), "s5_par": par, "s5_b": b_lay, "s5_c": c_lay,
        "glu_w": x["even_w_glu"][0].reshape(UT, P, UT * P).transpose(1, 0, 2), "gate_w": gate,
        "w1k": w1["k"], "w1v": w1["v"], "w2": w2, "pe": pe, "keys": keys, "ln": ln, "const": constants(),
    }
    return {n: np.ascontiguousarray(m) for n, m in out.items()}


def kernel(**inputs):
    import concourse.bacc as bacc
    from concourse.bass_utils import run_bass_kernel_spmd

    arrays = lay_out({n: np.asarray(m) for n, m in inputs.items()})
    nc = bacc.Bacc("TRN2", target_bir_lowering=False, num_devices=1)
    aps = {n: nc.dram_tensor(f"in_{n}", m.shape, F32, kind="ExternalInput").ap() for n, m in arrays.items()}
    aps["out"] = nc.dram_tensor("out", (SEQ, D), F32, kind="ExternalOutput").ap()
    build(nc, aps)
    r = run_bass_kernel_spmd(nc, [{f"in_{n}": m for n, m in arrays.items()}], core_ids=[0])
    return r.results[0]["out"].reshape(1, SEQ, D)
```

```python
from contextlib import ExitStack

import numpy as np

import concourse.bass as bass
from concourse import mybir

ALU = mybir.AluOpType
ACT = mybir.ActivationFunctionType
AX = mybir.AxisListType
F32 = mybir.dt.float32
F32R = mybir.dt.float32r
U32 = mybir.dt.uint32

P = 128
SEQ = 256
D = 1024
T = SEQ // P
KC = D // P
LAYERS = 2
RING = 4

GROUPS, STATE, CH = 16, 64, 16
UT = GROUPS * CH // P
ST = GROUPS * STATE // P
SB_PAIRS = 6
HEAD = 64
SCALE = HEAD ** -0.5
CMP_BLOCK, CMP_STRIDE = 32, 16
NCMP = (SEQ - CMP_BLOCK) // CMP_STRIDE + 1
CMP_ROWS = 2 * NCMP + 1
NSA_HEADS = 16
NBR = 3
EPS = 1e-5
ALPHA = (2 * LAYERS) ** 0.25
PEER_HEADS, KEYS, TOPK = 8, 128, 16
HALF = PEER_HEADS // 2
SUBS = 2 * PEER_HEADS
NEG = -1e30

CAND_ROWS = ((0, 1, 16), (1, 4, 8), (4, 8, 4), (8, 16, 1))
CAND_START = [0]
for _from, _to, _width in CAND_ROWS:
    CAND_START += [CAND_START[-1] + _width * (n + 1) for n in range(_to - _from)]
CANDS = CAND_START.pop()

PROJ, OUTW, WQ, EXP = 20, 8, 16, 2 * KEYS
SCORE_BANKS = (6, 7, 4, 5)
PER_LAYER = PROJ + OUTW + WQ + EXP
SLABS = LAYERS * PER_LAYER
PROJ_PER_LAYER = PROJ + WQ

TWO_PI = 2 * np.pi
PI_A = 6.28125
PI_B = float(np.float32(TWO_PI - PI_A))
PI_C = float(np.float32(TWO_PI - PI_A - PI_B))
ROUND = 1.5 * 2.0 ** 23
PI_IN = float(np.nextafter(np.float32(np.pi), np.float32(0)))

C_IDENT, C_TRI, C_ONES, C_BELOW, C_NEGDIAG = 0, 128, 256, 384, 512
C_IOTA, C_IOTA16, C_DIST, C_SLOPE = 640, 768, 784, 784 + 384
C_CMPBIAS = C_SLOPE + NSA_HEADS
C_CMPMASK = C_CMPBIAS + T * NSA_HEADS * NCMP
C_START = C_CMPMASK + T * NCMP
C_ALL = C_START + TOPK


def constants():
    c = np.zeros((P, C_ALL), np.float32)
    i = np.arange(P)
    c[:, C_IDENT:C_IDENT + P] = np.eye(P)
    c[:, C_TRI:C_TRI + P] = -1.0 * (i[:, None] >= i[None, :])
    c[:, C_ONES:C_ONES + P] = -1
    c[:, C_BELOW:C_BELOW + P] = i[:, None] < i[None, :]
    c[:, C_NEGDIAG:C_NEGDIAG + P] = np.where(i[:, None] < i[None, :], 0, NEG)
    c[:, C_IOTA:C_IOTA + P] = i[None, :]
    c[:, C_IOTA16:C_IOTA16 + TOPK] = np.arange(TOPK)[None, :]
    col = C_DIST
    for t in range(T):
        n = P * (t + 1)
        dist = (t * P + i[:, None]) - np.arange(n)[None, :]
        c[:, col:col + n] = np.where(dist >= 0, -dist, NEG)
        col += n
    head = np.arange(NSA_HEADS)
    order = np.array([(2 * p + half) * 4 + r for p in range(2) for r in range(4) for half in range(2)])
    slope = (2.0 ** (-8.0 * (head + 1) / NSA_HEADS)).astype(np.float32)[order]
    c[:, C_SLOPE:C_SLOPE + NSA_HEADS] = slope
    ends = np.arange(NCMP) * CMP_STRIDE + CMP_BLOCK - 1
    for t in range(T):
        dist = ((t * P + i[:, None]) - ends[None, :]).astype(np.float32)
        bias = np.where(dist[:, None, :] >= 0, -slope[None, :, None] * dist[:, None, :], np.float32(NEG))
        a = C_CMPBIAS + t * NSA_HEADS * NCMP
        c[:, a:a + NSA_HEADS * NCMP] = bias.reshape(P, -1)
        a = C_CMPMASK + t * NCMP
        c[:, a:a + NCMP] = dist >= 0
    c[:, C_START:C_START + TOPK] = CAND_START
    return c


def wide(ap, axis, n):
    shape = list(ap.shape)
    shape[axis] = n
    return ap.broadcast_to(tuple(shape))


def free(eng, sem, count):
    if not isinstance(count, int) or count > 0:
        eng.wait_ge(sem, count)


class Steps:

    def __init__(self, eng, sem):
        self.eng, self.sem, self.n, self.turn = eng, sem, 0, 0

    def __call__(self, ins):
        self.n += 1
        ins.then_inc(self.sem, 1)

    def wait(self, behind=0):
        self.eng.wait_ge(self.sem, self.turn + self.n - behind)

    def enter(self, i, per):
        self.turn = 0 if isinstance(i, int) else (i - 1) * per
        self.start, self.per = self.n, per

    def leave(self, turns):
        assert self.n - self.start == self.per, (self.n - self.start, self.per)
        self.n, self.turn = self.n + (turns - 1) * self.per, 0


def build(nc, a):
    with ExitStack() as ctx:
        def sb(name, shape, dt=F32):
            return ctx.enter_context(nc.sbuf_tensor(name, shape, dt))

        def sem(name):
            return ctx.enter_context(nc.semaphore(name))

        psum = ctx.enter_context(nc.psum_tensor("psum", [P, 8, 512], F32))
        ring = sb("ring", [P, RING, D])
        h_nat = sb("h_nat", [P, T, D])
        hT_hi = sb("hT_hi", [P, KC, SEQ], F32R)
        hT_lo = sb("hT_lo", [P, KC, SEQ], F32R)
        slab_hi = sb("slab_hi", [P, 2, D], F32R)
        slab_lo = sb("slab_lo", [P, 2, D], F32R)
        weighted_hi = sb("weighted_hi", [P, 2, SEQ], F32R)
        weighted_lo = sb("weighted_lo", [P, 2, SEQ], F32R)
        big = sb("big", [P, SEQ * KEYS])
        const = sb("const", [P, C_ALL])
        hidden = sb("hidden", [P, 2, SEQ])
        pairsT = sb("pairsT", [P, SEQ // 4, 3, 4])
        hot = sb("hot", [P, 2, 2, 4, KEYS])
        small = sb("small", [P, 32])

        used = [0]

        def view(n):
            used[0] += n
            assert used[0] <= SEQ * KEYS
            return big[:, used[0] - n:used[0]]

        G = big[:, :].rearrange("p (e t) -> p e t", t=SEQ)
        mixT = view(KC * SEQ).rearrange("p (c t) -> p c t", c=KC)
        hT = view(KC * SEQ).rearrange("p (c t) -> p c t", c=KC)
        shared = used[0]
        uT = view(UT * SEQ).rearrange("p (c t) -> p c t", c=UT)
        v_nat = view(T * SB_PAIRS * P).rearrange("p (t n) -> p t n", t=T)
        b_lay = view(ST * 2 * P).rearrange("p (j r n) -> p j r n", j=ST, r=2)
        c_lay = view(ST * 2 * P).rearrange("p (j r n) -> p j r n", j=ST, r=2)
        glu_w = view(UT * UT * P).rearrange("p (c n) -> p c n", c=UT)
        s5_par = view(3 * ST + 2 * UT)
        phase = view(2 * ST * SEQ).rearrange("p (r j t) -> p r j t", r=2, j=ST)
        drive = view(2 * ST * SEQ).rearrange("p (r j t) -> p r j t", r=2, j=ST)
        turned = view(2 * ST * SEQ).rearrange("p (r j t) -> p r j t", r=2, j=ST)
        temp = view(2 * ST * SEQ).rearrange("p (r j t) -> p r j t", r=2, j=ST)
        s5_small = view(24 * ST).rearrange("p (n j) -> p n j", j=ST)
        qk = view(4 * SEQ).rearrange("p (n t) -> p n t", n=4)
        v_pair = view(2 * T * P).rearrange("p (n t d) -> p n t d", n=2, t=T)
        stick_flat = view(4 * 2 * 384)
        stick = stick_flat.rearrange("p (h n c) -> p h n c", h=4, n=2)
        yT = stick_flat[:, 0:3 * UT * SEQ].rearrange("p (n c t) -> p n c t", n=3, c=UT)
        used[0] = shared
        kvc = view(4 * SEQ).rearrange("p (n t) -> p n t", n=4)
        blocks = view(2 * 2 * 2 * SEQ).rearrange("p (n b c) -> p n b c", n=2, b=2)
        w1 = view(2 * CMP_BLOCK * P).rearrange("p (n o m) -> p n o m", n=2, o=CMP_BLOCK)
        w2 = view(2 * P).rearrange("p (n m) -> p n m", n=2)
        peT = view(2 * CMP_BLOCK).rearrange("p (n o) -> p n o", n=2)
        gate_w = view(KC * 48).rearrange("p (c n) -> p c n", c=KC)
        gates = view(T * 48).rearrange("p (t g n) -> p t g n", t=T, g=2)
        cmp_hid = view(2 * 2 * 2 * NCMP).rearrange("p (n f g m) -> p n f g m", n=2, f=2, g=2)
        cmp_act = view(4 * P).rearrange("p (n f m) -> p n f m", n=2, f=2)
        kcT = view(2 * NCMP).rearrange("p (g m) -> p g m", g=2)
        vc = view(2 * P).rearrange("p (g m) -> p g m", g=2)
        kc_now = view(NCMP)
        vc_now = view(P)
        kT = view(2 * SEQ).rearrange("p (n t) -> p n t", n=2)
        vN = view(2 * T * P).rearrange("p (n t d) -> p n t d", n=2, t=T)
        qT = view(4 * SEQ).rearrange("p (r t) -> p r t", r=4)
        pc = view(T * 8 * NCMP).rearrange("p (t h m) -> p t h m", t=T, h=8)
        pc_red = view(T * 8 * 2).rearrange("p (n t h) -> p n t h", n=2, t=T)
        prob = view(4 * 512).rearrange("p (s c) -> p s c", s=4)
        probT = view(2 * 512).rearrange("p (s c) -> p s c", s=2)
        pcT = view(2 * P).rearrange("p (s c) -> p s c", s=2)
        red = view(4 * 8).rearrange("p (s c) -> p s c", s=4)
        used[0] = shared
        scores = view(T * SUBS * KEYS).rearrange("p (t j k) -> p t j k", t=T, j=SUBS)
        sub_q = view(2 * SEQ).rearrange("p (s t) -> p s t", s=2)
        sub_top = view(T * SUBS * TOPK).rearrange("p (t j k) -> p t j k", t=T, j=SUBS)
        sub_idx = view(T * SUBS * TOPK).rearrange("p (t j k) -> p t j k", t=T, j=SUBS)
        sub_idf = view(T * SUBS * TOPK).rearrange("p (t j k) -> p t j k", t=T, j=SUBS)
        cand = view(T * CANDS).rearrange("p (t c) -> p t c", t=T)
        best = view(T * PEER_HEADS * TOPK).rearrange("p (t h k) -> p t h k", t=T, h=PEER_HEADS)
        flat = view(T * PEER_HEADS * TOPK).rearrange("p (t h k) -> p t h k", t=T, h=PEER_HEADS)
        place = view(6 * T * HALF * TOPK).rearrange("p (n t c) -> p n t c", n=6, t=T)
        spare = view(T * HALF * (TOPK - 1)).rearrange("p (t h k) -> p t h k", t=T, h=HALF)
        match = view(2 * T * HALF * TOPK * TOPK).rearrange("p (s t h k c) -> p s t h k c", s=2, t=T, h=HALF, k=TOPK)
        pairs = view(T * 3 * PEER_HEADS * TOPK).rearrange("p (t n c) -> p t n c", t=T, n=3)
        soft_red = view(2 * T * PEER_HEADS).rearrange("p (n t h) -> p n t h", n=2, t=T)
        keysT = view(SUBS * KEYS).rearrange("p (j k) -> p j k", j=SUBS)
        used[0] = shared
        squares = view(T * D).rearrange("p (t d) -> p t d", t=T)
        ln_rows = (used[0] // SEQ, used[0] // SEQ + 2 * D // SEQ)
        ln_par = view(2 * D).rearrange("p (k d) -> p k d", k=2)

        ident = const[:, C_IDENT:C_IDENT + P]
        neg_tri = const[:, C_TRI:C_TRI + P]
        neg_ones = const[:, C_ONES:C_ONES + P]
        below = const[:, C_BELOW:C_BELOW + P]
        neg_diag = const[:, C_NEGDIAG:C_NEGDIAG + P]
        iota = const[:, C_IOTA:C_IOTA + P]
        iota16 = const[:, C_IOTA16:C_IOTA16 + TOPK]
        cand_start = const[:, C_START:C_START + TOPK]

        names = """const_loaded x_loaded xT_loaded s5_par_loaded s5_b_loaded s5_loaded ln_loaded keys_loaded nsa_loaded out_stored dumped
            slab_done proj_copied hi_done split_done hidden_hi hidden_lo raw_weighted
            act_steps dve_steps pool_steps
            ln_sum ln_mean ln_square ln_var ln_rstd ln_done ln_turned ln_copied
            s5_dt s5_rates s5_mag s5_angle s5_sine s5_pq s5_pq_used s5_turned s5_scanned s5_states s5_y s5_y_in s5_gelu s5_z s5_gate s5_out
            v_staged z_ready z_log stick_ready tails_ready masked stick_w pv_ready o_copied
            cmp_blocks cmp_ready cmp_act_ready cmp_turned cmp_hidden cmp_kv cmp_kv_copied gate_ready gate_done cmp_staged cmp_scores cmp_shifted cmp_exp cmp_aux cmp_probs
            sel_scores sel_biased sel_exp sel_prob sel_turned sel_copied sel_out sel_stored
            score_ready score_copied match_ready match_taken route_exp_in route_exp route_out route_turned route_copied
            pairs_turned apart hot_rows hot_ready g_ready g_copied hidden_ready weighted_ready""".split()
        S = {n: sem(n) for n in names}
        slab_loaded = [sem(f"slab_loaded{s}") for s in range(RING)]
        slab_done, proj_copied, split_done = S["slab_done"], S["proj_copied"], S["split_done"]
        block = ctx.enter_context(nc.Block())

        def base(layer):
            return layer * PER_LAYER

        TAKEN_BY_POOL = (((0, 0), (1, 0), (0, 1), (1, 1)), ((0, 0),))
        POOL_TAKES = sum(len(x) for x in TAKEN_BY_POOL)

        def taken_indices(s, t, some):
            idf = sub_idf[:, t, some * SUBS // 2:(some + 1) * SUBS // 2, :].rearrange("p (h s) k -> p h s k", s=2)
            return wide(idf[:, :, s, :].unsqueeze(2), 2, TOPK)

        @block.sync
        def _(sp):
            sp.dma_start(hT[:, :, :], a["xT"]).then_inc(S["xT_loaded"], 16)
            for s in range(RING):
                sp.dma_start(ring[:, s, :], a["slabs"][s]).then_inc(slab_loaded[s], 16)
            for layer in range(LAYERS):
                first, experts = layer * PER_LAYER // RING, (PER_LAYER - EXP) // RING
                if layer:
                    for s in range(RING):
                        sp.wait_ge(split_done, 2 * (layer * EXP + s + 1 - RING))
                        sp.dma_start(ring[:, s, :], a["slabs"][first * RING + s]).then_inc(slab_loaded[s], 16)
                with sp.Fori(first + 1, first + experts + 1) as r:
                    for s in range(RING):
                        sp.wait_ge(slab_done, r * RING + (s + 1 - RING))
                        sp.dma_start(ring[:, s, :], a["slabs"][r * RING + s]).then_inc(slab_loaded[s], 16)
                with sp.Fori(1, EXP // RING) as r:
                    for s in range(RING):
                        sp.wait_ge(split_done, r * (2 * RING) + 2 * (layer * EXP + s + 1 - RING))
                        sp.dma_start(ring[:, s, :], a["slabs"][r * RING + ((first + experts) * RING + s)]).then_inc(
                            slab_loaded[s], 16)
            for t in range(T):
                sp.wait_ge(S["ln_done"], 2 * LAYERS * T - T + t + 1)
                sp.dma_start(a["out"][t * P:(t + 1) * P, :], h_nat[:, t, :]).then_inc(S["out_stored"], 16)
            sp.wait_ge(S["out_stored"], 16 * T)

        @block.tensor
        def _(pe):
            def landed(n):
                return (n // RING + 1) * 16

            def slab(slot, count):
                pe.wait_ge(slab_loaded[slot], count)
                return ring[:, slot, :]

            def project(n, slot, turn, pi):
                w = slab(slot, turn * 16 + landed(n))
                w = w.rearrange("p (c n) -> p c n", c=KC)
                free(pe, proj_copied, pi - 1)
                out = psum[:, 4 + slot % 2, 0:SEQ]
                for c in range(KC):
                    last = pe.matmul(out, w[:, c, :], hT[:, c, :], start=(c == 0), stop=(c == KC - 1))
                last.then_inc(slab_done, 1)

            def project_natural(n, slot, turn, pi):
                slab(slot, turn * 16 + landed(n))
                slab(slot + 1, turn * 16 + landed(n + 1))
                w = ring[:, slot:slot + 2, :].rearrange("p s (c n) -> p s c n", c=KC)
                free(pe, proj_copied, pi)
                for t in range(T):
                    for c in range(KC):
                        last = pe.matmul(psum[:, 4 + t, 0:2 * P], hT[:, c, t * P:(t + 1) * P], w[:, :, c, :],
                                         start=(c == 0), stop=(c == KC - 1))
                last.then_inc(slab_done, 2)

            def accumulate(w, rows, first, last):
                for t in range(T):
                    for n in range(2):
                        mm = pe.matmul(psum[:, 2 * t + n, :], rows[:, t * P:(t + 1) * P], w[:, n * 512:(n + 1) * 512],
                                       start=first, stop=last)
                mm.then_inc(slab_done, 1)

            def turn_hidden(ln):
                pe.wait_ge(S["ln_done"], T * (ln + 1))
                for b in range(4):
                    for k in range(2):
                        for t in range(T):
                            mm = pe.transpose(psum[:, b, k * SEQ + t * P:k * SEQ + (t + 1) * P],
                                              h_nat[:, t, (2 * b + k) * P:(2 * b + k + 1) * P], ident)
                    mm.then_inc(S["ln_turned"], 1)

            def s5_inputs():
                pe.wait_ge(S["s5_b_loaded"], 16)
                pe.wait_ge(proj_copied, UT)
                for j in range(ST):
                    free(pe, S["s5_pq_used"], j - 1)
                    for r in range(2):
                        mm = pe.matmul(psum[:, 6 + j % 2, r * SEQ:(r + 1) * SEQ], b_lay[:, j, r, :], uT[:, j // 4, :],
                                       start=(r == 0), stop=True, skip_group_check=True)
                    mm.then_inc(S["s5_pq"], 1)

            def s5_outputs():
                pe.wait_ge(S["s5_loaded"], 3 * 16)
                pe.wait_ge(S["s5_states"], 1)
                first = True
                for c in range(UT):
                    for j in range(4 * c, 4 * c + 4):
                        for r in range(2):
                            mm = pe.matmul(psum[:, 3, c * SEQ:(c + 1) * SEQ], c_lay[:, j, r, :], turned[:, r, j, :],
                                           start=first, stop=(j == 4 * c + 3 and r == 1), skip_group_check=True)
                            first = False
                mm.then_inc(S["s5_y"], 1)
                pe.wait_ge(S["s5_gelu"], 1)
                first = True
                for c in range(UT):
                    for k in range(UT):
                        mm = pe.matmul(psum[:, 2, c * SEQ:(c + 1) * SEQ], glu_w[:, k, c * P:(c + 1) * P],
                                       yT[:, 1, k, :], start=first, stop=(k == UT - 1), skip_group_check=True)
                        first = False
                mm.then_inc(S["s5_z"], 1)

            def stick_logits(i, pr):
                pe.wait_ge(proj_copied, i * 4 + (8 + 2 * pr + 2))
                for h in range(2):
                    z = psum[:, (6 if pr == 0 else 0) + h, :]
                    lo, hi = 64 * h, 64 * h + 64
                    q, k = qk[lo:hi, 2 * pr, :], qk[lo:hi, 2 * pr + 1, :]
                    pe.matmul(z[:, 0:2 * P], k[:, 0:P], q, start=True, stop=False, skip_group_check=True)
                    pe.matmul(z[:, 2 * P:3 * P], k[:, P:SEQ], q[:, P:SEQ], start=False, stop=False,
                              skip_group_check=True).then_inc(S["z_ready"], 1)

            def stick_tails(i, pr):
                for h in range(2):
                    pe.wait_ge(S["stick_ready"], i * 4 + (2 * pr + h + 1))
                    z = psum[:, (6 if pr % 2 == 0 else 0) + h, :]
                    s = stick[:, 2 * (pr % 2) + h, 0, :]
                    pe.matmul(z[:, 0:3 * P], neg_tri, s[:, 0:3 * P], start=False, stop=False, skip_group_check=True)
                    pe.matmul(z[:, P:2 * P], neg_ones, s[:, 2 * P:3 * P], start=False, stop=True,
                              skip_group_check=True).then_inc(S["tails_ready"], 1)

            def stick_values(i, pr):
                pe.wait_ge(S["v_staged"], i * 2 + (pr + 1))
                for h in range(2):
                    pe.wait_ge(S["stick_w"], i * 4 + (2 * pr + h + 1))
                    w = stick[:, 2 * (pr % 2) + h, 1, :]
                    o = psum[:, 2, h * SEQ:(h + 1) * SEQ]
                    pe.matmul(o, v_pair[:, pr % 2, 0, :], w[:, 0:2 * P], start=(h == 0), stop=False,
                              skip_group_check=True)
                    mm = pe.matmul(o[:, P:SEQ], v_pair[:, pr % 2, 1, :], w[:, 2 * P:3 * P], start=False, stop=True,
                                   skip_group_check=True)
                mm.then_inc(S["pv_ready"], 1)

            def even_mixer():
                pe.wait_ge(S["xT_loaded"], 16)
                for n in range(UT):
                    project(n, n % RING, 0, n)
                project_natural(2, 2, 0, 2)
                s5_inputs()
                for n in (4, 6):
                    project_natural(n, n % RING, 0, n)
                pe.wait_ge(S["s5_pq_used"], ST)

                def turn(i):
                    for pr in range(2):
                        for m in range(2):
                            n = 8 + 2 * pr + m
                            project(n, n % RING, i, i * 4 + n)
                        if not isinstance(i, int):
                            stick_values(i, pr - 2)
                        stick_logits(i, pr)
                        if not isinstance(i, int) or pr:
                            stick_tails(i, pr - 1)

                turn(0)
                with pe.Fori(1, SB_PAIRS // 2) as i:
                    turn(i)
                stick_values(SB_PAIRS // 2, -2)
                stick_tails(SB_PAIRS // 2, -1)
                stick_values(SB_PAIRS // 2, -1)
                pe.wait_ge(S["o_copied"], 2 * SB_PAIRS)
                s5_outputs()
                pe.wait_ge(S["s5_out"], UT)

            def compress():
                pe.wait_ge(S["nsa_loaded"], 7 * 16)
                for n in range(2):
                    pe.wait_ge(S["cmp_blocks"], 2 * (n + 1))
                    for f in range(2):
                        rows, bank = slice(64 * f, 64 * f + 64), 3 * f
                        for o in range(CMP_BLOCK):
                            b = o // CMP_STRIDE
                            x = blocks[rows, n, b, :].rearrange("p (m o) -> p m o", o=CMP_STRIDE)
                            mm = pe.matmul(psum[0:CMP_ROWS, bank, n * P:(n + 1) * P],
                                           x[:, b:b + CMP_ROWS, o % CMP_STRIDE], w1[rows, n, o, :],
                                           start=(n == 0 and o == 0), stop=(o == CMP_BLOCK - 1), skip_group_check=True)
                        mm.then_inc(S["cmp_ready"], 1)
                pe.wait_ge(S["cmp_act_ready"], 4)
                for n in range(2):
                    for f in range(2):
                        mm = pe.transpose(psum[:, 1, (2 * n + f) * 32:(2 * n + f) * 32 + CMP_ROWS],
                                          cmp_act[0:CMP_ROWS, n, f, :], ident[0:CMP_ROWS, 0:CMP_ROWS])
                mm.then_inc(S["cmp_turned"], 1)
                pe.wait_ge(S["cmp_hidden"], 4)
                pe.matmul(psum[:, 2, 128:128 + 4 * NCMP], w2[:, 0, :],
                          cmp_hid[:, 0, :, :, :].rearrange("p f g m -> p (f g m)"), start=True, stop=True,
                          skip_group_check=True)
                for f in range(2):
                    for g in range(2):
                        mm = pe.matmul(psum[0:NCMP, 2, 256 + g * P + 64 * f:256 + g * P + 64 * f + 64],
                                       cmp_hid[:, 1, f, g, :], w2[:, 1, 0:64], start=False, stop=True,
                                       skip_group_check=True)
                mm.then_inc(S["cmp_kv"], 1)
                for t in range(T):
                    for c in range(KC):
                        mm = pe.matmul(psum[:, 1, 48 * t:48 * t + 48], hT[:, c, t * P:(t + 1) * P], gate_w[:, c, :],
                                       start=(c == 0 and t == 0), stop=(c == KC - 1), skip_group_check=True)
                mm.then_inc(S["gate_ready"], 1)

            def nsa_scores(i, s):
                r, half, t = s // 4, s // 2 % 2, s % 2
                if s >= 4:
                    pe.wait_ge(S["sel_biased"], i * 16 + (s - 3))
                rows, n = slice(64 * half, 64 * half + 64), P * (t + 1)
                for br in range(2):
                    mm = pe.matmul(psum[:, SCORE_BANKS[s % 4], br * n:(br + 1) * n], qT[rows, r, t * P:(t + 1) * P],
                                   kT[rows, br, 0:n], start=(br == 0), stop=True, skip_group_check=True)
                mm.then_inc(S["sel_scores"], 1)

            def nsa_turn(i, s):
                r, half, t = s // 4, s // 2 % 2, s % 2
                pe.wait_ge(S["sel_prob"], i * 16 + (s + 1))
                if s >= 2:
                    pe.wait_ge(S["sel_copied"], i * 16 + (s - 1))
                if s == 0:
                    pe.wait_ge(S["cmp_probs"], i + 1)
                pe.transpose(psum[0:NCMP, 3 * t, 256:256 + P], pc[:, t, 2 * r + half, :], ident)
                for m in range(2 * (t + 1)):
                    mm = pe.transpose(psum[:, s % 2, m * P:(m + 1) * P], prob[:, s % 4, m * P:(m + 1) * P], ident)
                mm.then_inc(S["sel_turned"], 1)

            def nsa_values(i, s):
                r, half, t = s // 4, s // 2 % 2, s % 2
                pe.wait_ge(S["sel_copied"], i * 16 + (s + 1))
                if s % 4 == 0:
                    free(pe, S["sel_stored"], i * 8 + 2 * (s // 4))
                out = psum[:, 2, half * SEQ + t * P:half * SEQ + (t + 1) * P]
                first = s % 4 == 0
                for br in range(2):
                    for k in range(t + 1):
                        m = br * (t + 1) + k
                        pe.matmul(out, vN[:, br, k, :], probT[:, s % 2, m * P:(m + 1) * P], start=first, stop=False,
                                  skip_group_check=True)
                        first = False
                pe.matmul(out, vc_now[0:NCMP, :], pcT[0:NCMP, s % 2, :], start=False, stop=True,
                          skip_group_check=True).then_inc(S["sel_out"], 1)

            def odd_mixer(layer):
                b, p = base(layer), layer * PROJ_PER_LAYER
                for n in range(4):
                    project(b + n, n % RING, 0, p + n)
                compress()
                pe.wait_ge(S["gate_done"], 1)
                pe.wait_ge(S["cmp_kv_copied"], 4)
                def turn(i):
                    free(pe, S["sel_biased"], i * 16)
                    for m in (0, 1, 2, 4, 5, 6, 7):
                        n = 4 + m
                        (project_natural if m == 2 else project)(b + n, n % RING, i * 2, i * 8 + (p + n))
                    pe.wait_ge(proj_copied, i * 8 + (p + 12))
                    pe.wait_ge(S["cmp_staged"], i * 2 + 2)
                    free(pe, S["sel_copied"], i * 16)
                    for t in range(T):
                        for r in range(4):
                            for half in range(2):
                                rows = slice(64 * half, 64 * half + 64)
                                c = (t * 4 + r) * NCMP
                                mm = pe.matmul(psum[:, 3 * half, c:c + NCMP], qT[rows, r, t * P:(t + 1) * P],
                                               kc_now[rows, :], start=(c == 0), stop=True, skip_group_check=True)
                    mm.then_inc(S["cmp_scores"], 1)
                    for s in range(3):
                        nsa_scores(i, s)
                    for s in range(16):
                        if s + 3 < 16:
                            nsa_scores(i, s + 3)
                        nsa_turn(i, s)
                        if s:
                            nsa_values(i, s - 1)
                    nsa_values(i, 15)

                turn(0)
                with pe.Fori(1, 2) as i:
                    turn(i)
                pe.wait_ge(S["sel_stored"], 16)

            def out_projection(layer):
                b = base(layer) + PROJ
                for c in range(OUTW):
                    accumulate(slab((b + c) % RING, landed(b + c)), mixT[:, c, :], c == 0, c == OUTW - 1)

            def route_scores(layer):
                b, p = base(layer) + PROJ + OUTW, layer * PROJ_PER_LAYER + PROJ
                pe.wait_ge(S["ln_copied"], (2 * layer + 1) * 4)
                pe.wait_ge(S["keys_loaded"], 16 * (layer + 1))
                def turn(i):
                    for pr in range(2):
                        for m in range(2):
                            s = 2 * pr + m
                            project(b + s, s, i, i * 4 + (p + s))
                        for m in range(2):
                            s = 2 * pr + m
                            pe.wait_ge(proj_copied, i * 4 + (p + s + 1))
                            free(pe, S["score_copied"], i * 4 + (SUBS * layer + s - 1))
                            for t in range(T):
                                mm = pe.matmul(psum[:, 6 + m, t * P:(t + 1) * P], sub_q[:, m, t * P:(t + 1) * P],
                                               keysT[:, i * 4 + s, :], start=(t == 0), stop=True,
                                               skip_group_check=True)
                            mm.then_inc(S["score_ready"], 1)

                turn(0)
                with pe.Fori(1, WQ // RING) as i:
                    turn(i)

            def spread(layer):
                for t in range(T):
                    pe.wait_ge(S["route_out"], layer * T + t + 1)
                    for n in range(3):
                        mm = pe.transpose(psum[:, 6 + t, n * P:(n + 1) * P], pairs[:, t, n, :], ident)
                    mm.then_inc(S["route_turned"], 1)
                def turn(i):
                    for q in range(2):
                        k = layer * (SEQ // 4) + q
                        pe.wait_ge(S["hot_rows"], i * 8 + 4 * (k + 1))
                        pe.wait_ge(S["hot_ready"], i * 2 + (k + 1))
                        free(pe, S["g_copied"], i * 2 + (k - 1))
                        for m in range(4):
                            mm = pe.matmul(psum[:, 6 + q, m * KEYS:(m + 1) * KEYS], hot[:, q, 1, m, :],
                                           hot[:, q, 0, m, :], start=(m == 0), stop=True, skip_group_check=True)
                        mm.then_inc(S["g_ready"], 1)

                turn(0)
                with pe.Fori(1, SEQ // 8) as i:
                    turn(i)

            def experts(layer):
                b, w = base(layer) + PROJ + OUTW + WQ, layer * KEYS

                def up(slot, split, e):
                    out = psum[:, 4 + e[0], 0:SEQ]
                    if e[1] is not None:
                        pe.wait_ge(S["hidden_ready"], e[1])
                    hi = slab_hi[:, slot % 2, :].rearrange("p (c n) -> p c n", c=KC)
                    lo = slab_lo[:, slot % 2, :].rearrange("p (c n) -> p c n", c=KC)
                    for c in range(KC):
                        if c % (KC // 2) == 0:
                            pe.wait_ge(split_done, split + 1 + 2 * c // KC)
                        pe.matmul(out, hi[:, c, :], hT_hi[:, c, :], start=(c == 0), stop=False)
                        pe.matmul(out, hi[:, c, :], hT_lo[:, c, :], start=False, stop=False)
                        mm = pe.matmul(out, lo[:, c, :], hT_hi[:, c, :], start=False, stop=(c == KC - 1))
                    mm.then_inc(slab_done, 1)

                def down(slot, split, parity, e, first=False, last=False):
                    pe.wait_ge(S["weighted_ready"], e)
                    for n in range(2):
                        pe.wait_ge(split_done, split + 1 + n)
                        hi = slab_hi[:, slot % 2, n * 512:(n + 1) * 512]
                        lo = slab_lo[:, slot % 2, n * 512:(n + 1) * 512]
                        for t in range(T):
                            out, tok = psum[:, 2 * t + n, :], slice(t * P, (t + 1) * P)
                            pe.matmul(out, weighted_hi[:, parity, tok], hi, start=first, stop=False)
                            pe.matmul(out, weighted_hi[:, parity, tok], lo, start=False, stop=False)
                            mm = pe.matmul(out, weighted_lo[:, parity, tok], hi, start=False, stop=last)
                    mm.then_inc(slab_done, 1)

                z = 2 * layer * EXP
                pe.wait_ge(S["hidden_lo"], 4 * (layer + 1))
                up(0, z, (0, None))
                up(1, z + 2, (1, None))
                down(2, z + 4, 0, w + 1, first=True)
                up(3, z + 6, (0, w + 1))
                with pe.Fori(1, EXP // RING - 1) as k:
                    down(0, k * 8 + z, 1, k * 2 + w)
                    up(1, k * 8 + (z + 2), (1, k * 2 + w))
                    down(2, k * 8 + (z + 4), 0, k * 2 + (w + 1))
                    up(3, k * 8 + (z + 6), (0, k * 2 + (w + 1)))
                down(0, z + 504, 1, w + 126)
                up(1, z + 506, (1, w + 126))
                down(2, z + 508, 0, w + 127)
                down(3, z + 510, 1, w + 128, last=True)

            pe.wait_ge(S["const_loaded"], 16)
            for layer in range(LAYERS):
                even_mixer() if layer == 0 else odd_mixer(layer)
                out_projection(layer)
                turn_hidden(2 * layer)
                route_scores(layer)
                spread(layer)
                experts(layer)
                if layer + 1 < LAYERS:
                    turn_hidden(2 * layer + 1)
                    pe.wait_ge(S["ln_copied"], (2 * layer + 2) * 4)

        @block.scalar
        def _(act):
            step = Steps(act, S["act_steps"])

            def copy_proj(n, dst, scale=1.0):
                act.wait_ge(slab_done, n[0])
                src = psum[:, 4 + n[1], 0:SEQ]
                if len(dst.shape) == 3:
                    src = src.rearrange("p (a b) -> p a b", a=2)
                act.activation(dst, src, ACT.Copy, scale=scale).then_inc(proj_copied, 1)

            def layer_norm(layer, which):
                ln = 2 * layer + which
                for t in range(T):
                    act.wait_ge(S["ln_mean"], T * ln + t + 1)
                    act.activation(squares[:, t, :], h_nat[:, t, :], ACT.Square, bias=small[:, 8 + t:9 + t],
                                   accum_out=small[:, 12 + t:13 + t]).then_inc(S["ln_square"], 1)
                for t in range(T):
                    act.wait_ge(S["ln_var"], T * ln + t + 1)
                    act.activation(small[:, 20 + t:21 + t], small[:, 16 + t:17 + t],
                                   ACT.Sqrt).then_inc(S["ln_rstd"], 1)

            def copy_hidden(ln, split):
                for b in range(4):
                    act.wait_ge(S["ln_turned"], 4 * ln + b + 1)
                    act.activation(hT[:, 2 * b:2 * b + 2, :], psum[:, b, :].rearrange("p (k t) -> p k t", k=2),
                                   ACT.Copy).then_inc(S["ln_copied"], 1)
                if split:
                    act.wait_ge(S["ln_copied"], 4 * (ln + 1))
                    for b in range(4):
                        act.activation(hT_hi[:, 2 * b:2 * b + 2, :], hT[:, 2 * b:2 * b + 2, :],
                                       ACT.Copy).then_inc(S["hidden_hi"], 1)

            def even_mixer():
                act.dma_start(s5_par[:, :], a["s5_par"]).then_inc(S["s5_par_loaded"], 16)
                act.dma_start(b_lay[:, :, :, :], a["s5_b"]).then_inc(S["s5_b_loaded"], 16)
                act.dma_start(c_lay[:, :, :, :], a["s5_c"]).then_inc(S["s5_loaded"], 16)
                act.dma_start(glu_w[:, :, :], a["glu_w"]).then_inc(S["s5_loaded"], 16)
                act.dma_start(h_nat[:, :, :], a["x"]).then_inc(S["s5_loaded"], 16)
                act.wait_ge(S["s5_par_loaded"], 16)
                act.activation(s5_small[:, 0, :], s5_par[:, 2 * ST:3 * ST], ACT.Exp).then_inc(S["s5_dt"], 1)
                act.wait_ge(S["s5_rates"], 1)
                act.activation(s5_small[:, 3, :], s5_small[:, 1, :], ACT.Exp).then_inc(S["s5_mag"], 1)
                act.wait_ge(S["s5_angle"], 1)
                act.activation(s5_small[:, 8, :], s5_small[:, 6, :], ACT.Sin).then_inc(S["s5_sine"], 1)
                act.activation(s5_small[:, 9, :], s5_small[:, 7, :], ACT.Sin).then_inc(S["s5_sine"], 1)
                for n in range(UT):
                    copy_proj((n + 1, n % 2), uT[:, n, :])
                for n in range(UT, 8):
                    c = (n - UT) // 2 * 2 * P
                    copy_proj((n // 2 * 2 + 2, n % 2), v_nat[:, n % 2, c:c + 2 * P])
                def take(i, pr):
                    copy_proj((i * 4 + (9 + 2 * pr), 0), qk[:, 2 * pr, :], SCALE)
                    copy_proj((i * 4 + (10 + 2 * pr), 1), qk[:, 2 * pr + 1, :])

                def logs(i, pr):
                    for h in range(2):
                        k = 2 * pr + h
                        z = psum[:, (6 if pr == 0 else 0) + h, 0:384]
                        s1 = stick[:, k, 1, :]
                        act.wait_ge(S["z_ready"], i * 4 + (k + 1))
                        step(act.activation(s1, z, ACT.Abs))
                        step.wait()
                        step(act.activation(s1, s1, ACT.Exp, scale=-1.0))
                        step.wait()
                        act.activation(s1, s1, ACT.Ln, bias=1.0).then_inc(S["z_log"], 1)

                def weights(i, pr):
                    for h in range(2):
                        z = psum[:, (6 if pr % 2 == 0 else 0) + h, 0:384]
                        act.wait_ge(S["masked"], i * 4 + (2 * pr + h + 1))
                        act.activation(stick[:, 2 * (pr % 2) + h, 1, :], z, ACT.Exp).then_inc(S["stick_w"], 1)

                def store(i, pr):
                    act.wait_ge(S["pv_ready"], i * 2 + (pr + 1))
                    for h in range(2):
                        rows = slice(64 * h, 64 * h + 64)
                        act.activation(mixT[rows, i * 2 + (UT + pr), :], psum[rows, 2, h * SEQ:(h + 1) * SEQ],
                                       ACT.Copy).then_inc(S["o_copied"], 1)

                def turn(i):
                    step.enter(i, 8)
                    for pr in range(2):
                        take(i, pr)
                        if not isinstance(i, int):
                            store(i, pr - 2)
                        logs(i, pr)
                        if not isinstance(i, int) or pr:
                            weights(i, pr - 1)

                turn(0)
                step.leave(1)
                with act.Fori(1, SB_PAIRS // 2) as i:
                    turn(i)
                step.leave(SB_PAIRS // 2 - 1)
                store(SB_PAIRS // 2, -2)
                weights(SB_PAIRS // 2, -1)
                store(SB_PAIRS // 2, -1)
                act.wait_ge(S["s5_y_in"], 1)
                act.activation(yT[:, 1, :, :], yT[:, 0, :, :], ACT.Gelu_apprx_tanh).then_inc(S["s5_gelu"], 1)
                act.wait_ge(S["s5_z"], 1)
                for c in range(UT):
                    act.activation(yT[:, 2, c, :], psum[:, 2, c * SEQ:(c + 1) * SEQ], ACT.Sigmoid,
                                   bias=s5_par[:, 3 * ST + UT + c:3 * ST + UT + c + 1]).then_inc(S["s5_gate"], 1)

            def odd_mixer(layer):
                b = base(layer)
                for n in range(4):
                    copy_proj((b + n + 1, n % 2), kvc[:, n, :])
                act.wait_ge(S["cmp_ready"], 4)
                for n in range(2):
                    for f in range(2):
                        act.activation(cmp_act[0:CMP_ROWS, n, f, :], psum[0:CMP_ROWS, 3 * f, n * P:(n + 1) * P],
                                       ACT.Gelu_apprx_tanh).then_inc(S["cmp_act_ready"], 1)
                act.wait_ge(S["cmp_turned"], 1)
                for n in range(2):
                    for f in range(2):
                        c = (2 * n + f) * 32
                        act.activation(cmp_hid[:, n, f, :, :],
                                       psum[:, 1, c:c + 32].rearrange("p (g m) -> p g m", g=2)[:, :, 0:NCMP], ACT.Copy).then_inc(S["cmp_hidden"], 1)
                act.wait_ge(S["cmp_kv"], 1)
                for f in range(2):
                    rows = slice(64 * f, 64 * f + 64)
                    act.activation(kcT[rows, :, :].rearrange("p g m -> p (g m)"),
                                   psum[rows, 2, 128 + f * 2 * NCMP:128 + (f + 1) * 2 * NCMP],
                                   ACT.Copy).then_inc(S["cmp_kv_copied"], 1)
                    act.activation(vc[0:NCMP, f, :], psum[0:NCMP, 2, 256 + f * P:256 + (f + 1) * P],
                                   ACT.Copy).then_inc(S["cmp_kv_copied"], 1)
                act.wait_ge(S["gate_ready"], 1)
                act.activation(gates[:, :, :, :].rearrange("p t g n -> p (t g n)"), psum[:, 1, 0:96],
                               ACT.Sigmoid).then_inc(S["gate_done"], 1)
                act.wait_ge(S["cmp_kv_copied"], 4)
                def turn(i):
                    free(act, S["sel_out"], i * 16)
                    act.activation(kc_now[:, :], kcT[:, i, :], ACT.Copy).then_inc(S["cmp_staged"], 1)
                    act.activation(vc_now[0:NCMP, :], vc[0:NCMP, i, :], ACT.Copy).then_inc(S["cmp_staged"], 1)
                    for m in range(8):
                        n = (i * 8 + (b + 4 + m + 1), m % 2)
                        if m < 2:
                            copy_proj(n, kT[:, m, :])
                        elif m < 4:
                            copy_proj((i * 8 + (b + 8), m % 2), vN[:, :, m - 2, :])
                        else:
                            copy_proj(n, qT[:, m - 4, :], SCALE)
                    act.wait_ge(S["cmp_shifted"], i + 1)
                    act.activation(pc[:, :, :, :], pc[:, :, :, :], ACT.Exp).then_inc(S["cmp_exp"], 1)

                    def exps(s):
                        t = s % 2
                        n = P * (t + 1)
                        act.wait_ge(S["sel_biased"], i * 16 + (s + 1))
                        for br in range(2):
                            x = prob[:, s % 4, br * n:(br + 1) * n]
                            act.activation(x, x, ACT.Exp, bias=red[:, s % 4, br:br + 1],
                                           accum_out=red[:, s % 4, 2 + br:3 + br]).then_inc(S["sel_exp"], 1)

                    def turned_copy(s):
                        t = s % 2
                        act.wait_ge(S["sel_turned"], i * 16 + (s + 1))
                        n = 2 * P * (t + 1)
                        step(act.activation(pcT[0:NCMP, s % 2, :],
                                            psum[0:NCMP, 3 * t, 256:256 + P], ACT.Copy))
                        step.wait()
                        act.activation(probT[:, s % 2, 0:n], psum[:, s % 2, 0:n], ACT.Copy).then_inc(S["sel_copied"], 1)

                    def store(s):
                        act.wait_ge(S["sel_out"], i * 16 + (s + 1))
                        for half in range(2):
                            rows = slice(64 * half, 64 * half + 64)
                            act.activation(mixT[rows, i * 4 + s // 4, :], psum[rows, 2, half * SEQ:(half + 1) * SEQ],
                                           ACT.Copy).then_inc(S["sel_stored"], 1)

                    step.enter(i, 16)
                    exps(0)
                    exps(1)
                    for s in range(16):
                        if s + 2 < 16:
                            exps(s + 2)
                        turned_copy(s)
                        if s and s % 4 == 0:
                            store(s - 1)
                    store(15)

                turn(0)
                step.leave(1)
                with act.Fori(1, 2) as i:
                    turn(i)
                step.leave(2 - 1)

            def route(layer):
                b = base(layer) + PROJ + OUTW
                def turn(i):
                    for pr in range(2):
                        for s in (2 * pr, 2 * pr + 1):
                            free(act, S["score_ready"], i * 4 + (layer * SUBS + s - 1))
                            copy_proj((i * 4 + (b + s + 1), s % 2), sub_q[:, s % 2, :])
                        for s in (2 * pr, 2 * pr + 1):
                            act.wait_ge(S["score_ready"], i * 4 + (layer * SUBS + s + 1))
                            act.activation(scores[:, :, i * 4 + s, :], psum[:, 6 + s % 2, 0:SEQ].rearrange(
                                "p (t k) -> p t k", t=T), ACT.Copy).then_inc(S["score_copied"], 1)

                turn(0)
                with act.Fori(1, WQ // RING) as i:
                    turn(i)
                for t in range(T):
                    act.wait_ge(S["route_exp_in"], layer * T + t + 1)
                    act.activation(pairs[:, t, 2, :], pairs[:, t, 2, :], ACT.Exp).then_inc(S["route_exp"], 1)
                def turn(i):
                    for q in range(2):
                        act.wait_ge(S["g_ready"], i * 2 + (layer * (SEQ // 4) + q + 1))
                        act.activation(G[:, :, bass.ds(i * 8 + 4 * q, 4)].rearrange("p e m -> p m e"),
                                       psum[:, 6 + q, :].rearrange("p (m e) -> p m e", m=4),
                                       ACT.Copy).then_inc(S["g_copied"], 1)

                turn(0)
                with act.Fori(1, SEQ // 8) as i:
                    turn(i)

            def experts(layer):
                b, w = base(layer) + PROJ + OUTW + WQ, layer * KEYS

                def high(slot, land, free):
                    act.wait_ge(slab_loaded[slot], land)
                    act.wait_ge(slab_done, free)
                    for n in range(2):
                        cols = slice(n * 512, (n + 1) * 512)
                        act.activation(slab_hi[:, slot % 2, cols], ring[:, slot, cols],
                                       ACT.Copy).then_inc(S["hi_done"], 1)

                def gelu(parity, done, free):
                    act.wait_ge(slab_done, done)
                    if free is not None:
                        act.wait_ge(S["weighted_ready"], free)
                    act.activation(hidden[:, parity, :], psum[:, 4 + parity, 0:SEQ],
                                   ACT.Gelu_apprx_tanh).then_inc(S["hidden_ready"], 1)

                land = (b // RING + 1) * 16
                high(0, land, b)
                high(1, land, b)
                high(2, land, b + 1)
                gelu(0, b + 1, None)

                def turn(k):
                    high(3, k * 16 + land, k * 4 + (b + 2))
                    gelu(1, k * 4 + (b + 2), k * 2 + w)
                    high(0, k * 16 + (land + 16), k * 4 + (b + 3))
                    high(1, k * 16 + (land + 16), k * 4 + (b + 4))
                    gelu(0, k * 4 + (b + 4), k * 2 + (w + 1))
                    high(2, k * 16 + (land + 16), k * 4 + (b + 5))

                turn(0)
                with act.Fori(1, KEYS // 2 - 1) as k:
                    turn(k)
                high(3, land + 16 * 63, b + 254)
                gelu(1, b + 254, w + 126)

            for layer in range(LAYERS):
                even_mixer() if layer == 0 else odd_mixer(layer)
                layer_norm(layer, 0)
                copy_hidden(2 * layer, True)
                route(layer)
                experts(layer)
                layer_norm(layer, 1)
                if layer + 1 < LAYERS:
                    copy_hidden(2 * layer + 1, False)

        @block.gpsimd
        def _(pool):
            step = Steps(pool, S["pool_steps"])
            pool.dma_start(const[:, :], a["const"]).then_inc(S["const_loaded"], 16)

            def load_ln(ln):
                for k in range(2):
                    pool.dma_start(ln_par[:, k, :], wide(a["ln"][2 * ln + k:2 * ln + k + 1, :], 0, P)).then_inc(
                        S["ln_loaded"], 16)

            def phases():
                pool.wait_ge(S["s5_sine"], 2)
                re, im = phase[:, 0, :, :], phase[:, 1, :, :]
                w = [s5_small[:, 16 + n, :] for n in range(4)]
                step(pool.memset(re[:, :, 0:1], 1.0))
                step(pool.memset(im[:, :, 0:1], 0.0))
                step(pool.tensor_copy(w[0], s5_small[:, 9, :]))
                step(pool.tensor_copy(w[1], s5_small[:, 8, :]))
                step.wait()
                n = 1
                while n < SEQ:
                    a0, b0 = re[:, :, 0:n], im[:, :, 0:n]
                    wr = wide(w[0][:, :].unsqueeze(2), 2, n)
                    wi = wide(w[1][:, :].unsqueeze(2), 2, n)
                    t0, t1 = temp[:, 0, :, 0:n], temp[:, 1, :, 0:n]
                    step(pool.tensor_tensor(t0, a0, wr, ALU.mult))
                    step(pool.tensor_tensor(t1, b0, wi, ALU.mult))
                    step.wait()
                    step(pool.tensor_tensor(re[:, :, n:2 * n], t0, t1, ALU.subtract))
                    step.wait()
                    step(pool.tensor_tensor(t0, a0, wi, ALU.mult))
                    step(pool.tensor_tensor(t1, b0, wr, ALU.mult))
                    step.wait()
                    step(pool.tensor_tensor(im[:, :, n:2 * n], t0, t1, ALU.add))
                    step(pool.tensor_tensor(w[2], w[0], w[0], ALU.mult))
                    step(pool.tensor_tensor(w[3], w[1], w[1], ALU.mult))
                    step(pool.tensor_tensor(w[1], w[0], w[1], ALU.mult))
                    step.wait()
                    step(pool.tensor_tensor(w[0], w[2], w[3], ALU.subtract))
                    step(pool.tensor_scalar(w[1], w[1], 2.0, None, ALU.mult))
                    step.wait()
                    n *= 2
            def flatten(x):
                return x.rearrange("p j t -> p (j t)")

            pr, pi = flatten(phase[:, 0]), flatten(phase[:, 1])
            d_re, d_im = flatten(drive[:, 0]), flatten(drive[:, 1])
            z_re, z_im = flatten(turned[:, 0]), flatten(turned[:, 1])
            t0, t1 = flatten(temp[:, 0]), flatten(temp[:, 1])

            def products():
                step(pool.tensor_tensor(z_re, pr, d_re, ALU.mult))
                step(pool.tensor_tensor(t0, pi, d_im, ALU.mult))
                step(pool.tensor_tensor(z_im, pr, d_im, ALU.mult))
                step(pool.tensor_tensor(t1, pi, d_re, ALU.mult))
                step.wait()

            phases()
            pool.wait_ge(S["s5_pq_used"], ST)
            products()
            step(pool.tensor_tensor(z_re, z_re, t0, ALU.add))
            pool.tensor_tensor(z_im, z_im, t1, ALU.subtract).then_inc(S["s5_turned"], 1)
            pool.wait_ge(S["s5_scanned"], 2 * ST)
            products()
            step(pool.tensor_tensor(z_re, z_re, t0, ALU.subtract))
            step(pool.tensor_tensor(z_im, z_im, t1, ALU.add))
            step.wait()
            pool.tensor_scalar(z_im, z_im, -1.0, None, ALU.mult).then_inc(S["s5_states"], 1)

            def take_indices(layer, some):
                for s, t in TAKEN_BY_POOL[some]:
                    pool.wait_ge(S["match_ready"], (2 * layer + some) * 4 + 2 * t + s + 1)
                    pool.tensor_tensor(match[:, s, t], match[:, s, t], taken_indices(s, t, some), ALU.mult).then_inc(
                        S["match_taken"], 1)

            def distances(layer):
                pool.wait_ge(S["pairs_turned"], T * (layer + 1))

                def columns(i, q):
                    return wide(pairsT[:, bass.ds(i * 2 + q, 1), 1, :].rearrange("p a m -> p (a m)").unsqueeze(2), 2, KEYS)

                def turn(i):
                    for q in range(2):
                        k = layer * (SEQ // 4) + q
                        free(pool, S["g_ready"], i * 2 + (k - 1))
                        pool.tensor_tensor(hot[:, q, 1, :, :], wide(iota.unsqueeze(1), 1, 4), columns(i, q),
                                           ALU.subtract).then_inc(S["apart"], 1)

                turn(0)
                with pool.Fori(1, SEQ // 8) as i:
                    turn(i)

            for layer in range(LAYERS):
                if layer:
                    pool.wait_ge(S["ln_done"], T * 2 * layer)
                    for dst, name in ((w1[0:64, 0], "w1k"), (w1[64:P, 0], "w1k"), (w1[0:64, 1], "w1v"),
                                      (w1[64:P, 1], "w1v"), (w2[:, :, :], "w2"), (peT[:, :, :], "pe"),
                                      (gate_w[:, :, :], "gate_w")):
                        pool.dma_start(dst, a[name]).then_inc(S["nsa_loaded"], 16)
                pool.wait_ge(slab_done, base(layer) + PROJ + 1)
                load_ln(2 * layer)
                pool.dma_start(keysT[:, :, :], a["keys"][layer]).then_inc(S["keys_loaded"], 16)
                for some in range(2):
                    take_indices(layer, some)
                distances(layer)
                pool.wait_ge(S["weighted_ready"], layer * KEYS + ln_rows[1])
                load_ln(2 * layer + 1)
            pool.wait_ge(S["ln_loaded"], 32 * 2 * LAYERS)
            pool.wait_ge(S["keys_loaded"], 16 * LAYERS)
            pool.wait_ge(S["nsa_loaded"], 7 * 16)

        @block.vector
        def _(dve):
            step = Steps(dve, S["dve_steps"])

            def run(ins):
                step(ins)
                step.wait()

            def layer_norm(layer, which):
                ln = 2 * layer + which
                done = base(layer) + (PROJ + OUTW if which == 0 else PER_LAYER)
                dve.wait_ge(slab_done, done)
                for t in range(T):
                    y = h_nat[:, t, :]
                    run(dve.scalar_tensor_tensor(out=y, in0=y, scalar=ALPHA,
                                                 in1=psum[:, 2 * t:2 * t + 2, :].rearrange("p a b -> p (a b)"),
                                                 op0=ALU.mult, op1=ALU.add, accum_out=small[:, 4 + t:5 + t]))
                    dve.tensor_scalar(small[:, 8 + t:9 + t], small[:, 4 + t:5 + t], -1.0 / D, None,
                                      ALU.mult).then_inc(S["ln_mean"], 1)
                for t in range(T):
                    dve.wait_ge(S["ln_square"], T * ln + t + 1)
                    run(dve.tensor_scalar(small[:, 16 + t:17 + t], small[:, 12 + t:13 + t], 1.0 / D, EPS,
                                          ALU.mult, ALU.add))
                    dve.reciprocal(small[:, 16 + t:17 + t], small[:, 16 + t:17 + t]).then_inc(S["ln_var"], 1)
                dve.wait_ge(S["ln_loaded"], 32 * (ln + 1))
                for t in range(T):
                    y = h_nat[:, t, :]
                    dve.wait_ge(S["ln_rstd"], T * ln + t + 1)
                    run(dve.tensor_scalar(y, y, small[:, 8 + t:9 + t], small[:, 20 + t:21 + t], ALU.add, ALU.mult))
                    run(dve.tensor_tensor(y, y, ln_par[:, 0, :], ALU.mult))
                    dve.tensor_tensor(y, y, ln_par[:, 1, :], ALU.add).then_inc(S["ln_done"], 1)
                dve.wait_ge(S["ln_done"], T * (ln + 1))

            def s5_rates():
                lr, li = s5_par[:, 0:ST], s5_par[:, ST:2 * ST]
                s = [s5_small[:, n, :] for n in range(24)]
                dt, rate, angle, mag, turns = s[0], s[1], s[2], s[3], s[4]
                dve.wait_ge(S["s5_dt"], 1)
                run(dve.tensor_tensor(angle, li, dt, ALU.mult))
                dve.tensor_tensor(rate, lr, dt, ALU.mult).then_inc(S["s5_rates"], 1)
                run(dve.tensor_scalar(turns, angle, 1.0 / TWO_PI, ROUND, ALU.mult, ALU.add))
                run(dve.tensor_scalar(turns, turns, -ROUND, None, ALU.add))
                for part_pi in (PI_A, PI_B, PI_C):
                    run(dve.scalar_tensor_tensor(out=angle, in0=turns, scalar=-part_pi, in1=angle, op0=ALU.mult,
                                                 op1=ALU.add))
                run(dve.tensor_scalar(s[6], angle, PI_IN, -PI_IN, ALU.min, ALU.max))
                run(dve.scalar_tensor_tensor(out=s[5], in0=s[6], scalar=-1.0, in1=s[6], op0=ALU.mult, op1=ALU.max))
                dve.tensor_scalar(s[7], s[5], -1.0, float(np.pi / 2), ALU.mult, ALU.add).then_inc(S["s5_angle"], 1)
                dve.wait_ge(S["s5_sine"], 2)
                sine, cosine, a_re, a_im, den, t0, f_re, f_im, nf = s[8], s[9], s[10], s[11], s[12], s[13], s[14], s[15], s[21]
                run(dve.tensor_tensor(a_re, mag, cosine, ALU.mult))
                run(dve.tensor_tensor(a_im, mag, sine, ALU.mult))
                run(dve.tensor_scalar(a_re, a_re, -1.0, None, ALU.add))
                run(dve.tensor_tensor(den, lr, lr, ALU.mult))
                run(dve.tensor_tensor(t0, li, li, ALU.mult))
                run(dve.tensor_tensor(den, den, t0, ALU.add))
                run(dve.reciprocal(den, den))
                run(dve.tensor_tensor(f_re, a_re, lr, ALU.mult))
                run(dve.tensor_tensor(t0, a_im, li, ALU.mult))
                run(dve.tensor_tensor(f_re, f_re, t0, ALU.add))
                run(dve.tensor_tensor(f_re, f_re, den, ALU.mult))
                run(dve.tensor_tensor(f_im, a_im, lr, ALU.mult))
                run(dve.tensor_tensor(t0, a_re, li, ALU.mult))
                run(dve.tensor_tensor(f_im, f_im, t0, ALU.subtract))
                run(dve.tensor_tensor(f_im, f_im, den, ALU.mult))
                run(dve.tensor_scalar(nf, f_im, -1.0, None, ALU.mult))
                return f_re, f_im, nf, mag

            def s5_drive():
                f_re, f_im, nf, mag = s5_rates()
                for j in range(ST):
                    dve.wait_ge(S["s5_pq"], j + 1)
                    pq = psum[:, 6 + j % 2, :]
                    p, q = pq[:, 0:SEQ], pq[:, SEQ:2 * SEQ]
                    step(dve.tensor_scalar(turned[:, 0, j, :], q, nf[:, j:j + 1], None, ALU.mult))
                    run(dve.tensor_scalar(turned[:, 1, j, :], q, f_re[:, j:j + 1], None, ALU.mult))
                    step(dve.scalar_tensor_tensor(out=drive[:, 0, j, :], in0=p, scalar=f_re[:, j:j + 1],
                                                  in1=turned[:, 0, j, :], op0=ALU.mult, op1=ALU.add))
                    dve.scalar_tensor_tensor(out=drive[:, 1, j, :], in0=p, scalar=f_im[:, j:j + 1],
                                             in1=turned[:, 1, j, :], op0=ALU.mult, op1=ALU.add).then_inc(S["s5_pq_used"], 1)

            def s5_scan():
                mag = s5_small[:, 3, :]
                dve.wait_ge(S["s5_turned"], 1)
                for j in range(ST):
                    for r in range(2):
                        dve.tensor_tensor_scan(drive[:, r, j, :], wide(mag[:, j:j + 1], 1, SEQ), turned[:, r, j, :],
                                               0.0, ALU.mult, ALU.add).then_inc(S["s5_scanned"], 1)

            def even_mixer():
                dve.wait_ge(S["s5_par_loaded"], 16)
                s5_drive()
                dve.wait_ge(S["const_loaded"], 16)
                dve.wait_ge(proj_copied, 8)
                def stick_sums(i, pr):
                    for h in range(2):
                        k = 2 * pr + h
                        s = stick[:, k, 0, :]
                        dve.wait_ge(S["z_log"], i * 4 + (k + 1))
                        run(dve.scalar_tensor_tensor(out=s, in0=psum[:, (6 if pr == 0 else 0) + h, 0:384], scalar=0.0,
                                                     in1=stick[:, k, 1, :], op0=ALU.max, op1=ALU.add))
                        step(dve.tensor_tensor(s[:, 0:P], s[:, 0:P], below, ALU.mult))
                        dve.tensor_tensor(s[:, 2 * P:3 * P], s[:, 2 * P:3 * P], below,
                                          ALU.mult).then_inc(S["stick_ready"], 1)

                def mask(i, pr):
                    for h in range(2):
                        z = psum[:, (6 if pr % 2 == 0 else 0) + h, :].rearrange("p (a b) -> p a b", a=2)[:, :, 0:P]
                        dve.wait_ge(S["tails_ready"], i * 4 + (2 * pr + h + 1))
                        dve.tensor_tensor(z, z, wide(neg_diag.unsqueeze(1), 1, 2), ALU.add).then_inc(S["masked"], 1)

                def turn(i):
                    step.enter(i, 8)
                    for pr in range(2):
                        free(dve, S["pv_ready"], i * 2 + (pr - 1))
                        dve.tensor_copy(v_pair[:, pr, :, :],
                                        v_nat[:, :, bass.ds(i * 2 * P + pr * P, P)]).then_inc(S["v_staged"], 1)
                        stick_sums(i, pr)
                        if not isinstance(i, int) or pr:
                            mask(i, pr - 1)

                turn(0)
                step.leave(1)
                s5_scan()
                with dve.Fori(1, SB_PAIRS // 2) as i:
                    turn(i)
                step.leave(SB_PAIRS // 2 - 1)
                mask(SB_PAIRS // 2, -1)
                dve.wait_ge(S["s5_loaded"], 3 * 16)
                dve.wait_ge(S["s5_y"], 1)
                for c in range(UT):
                    run(dve.scalar_tensor_tensor(out=yT[:, 0, c, :], in0=uT[:, c, :],
                                                 scalar=s5_par[:, 3 * ST + c:3 * ST + c + 1],
                                                 in1=psum[:, 3, c * SEQ:(c + 1) * SEQ], op0=ALU.mult, op1=ALU.add))
                dve.memset(small[:, 0:1], 0.0).then_inc(S["s5_y_in"], 1)
                for c in range(UT):
                    dve.wait_ge(S["s5_gate"], c + 1)
                    dve.tensor_tensor(mixT[:, c, :], yT[:, 1, c, :], yT[:, 2, c, :], ALU.mult).then_inc(S["s5_out"], 1)

            def odd_mixer():
                dve.wait_ge(S["nsa_loaded"], 7 * 16)
                dve.wait_ge(proj_copied, PROJ_PER_LAYER + 4)
                for n in range(2):
                    for b in range(2):
                        dve.tensor_tensor(blocks[:, n, b, :].rearrange("p (m o) -> p m o", o=CMP_STRIDE),
                                          kvc[:, 2 * n:2 * n + 2, :].rearrange("p g (m o) -> p (g m) o", o=CMP_STRIDE),
                                          wide(peT[:, n, b * CMP_STRIDE:(b + 1) * CMP_STRIDE].unsqueeze(1), 1,
                                               2 * SEQ // CMP_STRIDE), ALU.add).then_inc(S["cmp_blocks"], 1)

                def turn(i):
                    step.enter(i, 8 + 16 * 6)
                    dve.wait_ge(S["gate_done"], 1)
                    dve.wait_ge(S["cmp_scores"], i + 1)
                    for t in range(T):
                        bias = const[:, bass.ds(i * (8 * NCMP) + (C_CMPBIAS + t * NSA_HEADS * NCMP), 8 * NCMP)]
                        bias = bias.rearrange("p (r f m) -> p r f m", r=4, f=2)
                        now = pc[:, t, :, :].rearrange("p (r f) m -> p r f m", f=2)
                        for f in range(2):
                            got = psum[:, 3 * f, t * 4 * NCMP:(t + 1) * 4 * NCMP].rearrange("p (r m) -> p r m", r=4)
                            step(dve.tensor_tensor(now[:, :, f, :], got, bias[:, :, f, :], ALU.add))
                    step.wait()
                    flat_pc = pc[:, :, :, :].rearrange("p t h m -> p (t h) m")
                    mx, sm = (pc_red[:, n, :, :].rearrange("p t h -> p (t h)") for n in range(2))
                    run(dve.tensor_reduce(mx, flat_pc, AX.X, ALU.max))
                    dve.tensor_tensor(flat_pc, flat_pc, wide(mx.unsqueeze(2), 2, NCMP),
                                      ALU.subtract).then_inc(S["cmp_shifted"], 1)
                    dve.wait_ge(S["cmp_exp"], i + 1)
                    for t in range(T):
                        keep = const[:, C_CMPMASK + t * NCMP:C_CMPMASK + (t + 1) * NCMP]
                        step(dve.tensor_tensor(pc[:, t, :, :], pc[:, t, :, :], wide(keep.unsqueeze(1), 1, 8),
                                               ALU.mult))
                    step.wait()
                    run(dve.tensor_reduce(sm, flat_pc, AX.X, ALU.add))
                    dve.tensor_scalar(sm, sm, 1e-30, None, ALU.max).then_inc(S["cmp_aux"], 1)
                    dve.wait_ge(S["cmp_aux"], i * 3 + 1)
                    dve.reciprocal(sm, sm).then_inc(S["cmp_aux"], 1)
                    dve.wait_ge(S["cmp_aux"], i * 3 + 2)
                    dve.tensor_tensor(pc_red[:, 1, :, :], pc_red[:, 1, :, :], gates[:, :, i, 0:8],
                                      ALU.mult).then_inc(S["cmp_aux"], 1)
                    dve.wait_ge(S["cmp_aux"], i * 3 + 3)
                    dve.tensor_tensor(flat_pc, flat_pc, wide(sm.unsqueeze(2), 2, NCMP),
                                      ALU.mult).then_inc(S["cmp_probs"], 1)

                    def biased(s):
                        r, half, t = s // 4, s // 2 % 2, s % 2
                        n = P * (t + 1)
                        dve.wait_ge(S["sel_scores"], i * 16 + (s + 1))
                        if s >= 4:
                            dve.wait_ge(S["sel_turned"], i * 16 + (s - 3))
                        d = C_DIST + (P if t else 0)
                        x = prob[:, s % 4, 0:2 * n].rearrange("p (b n) -> p b n", b=2)
                        h = 2 * r + half
                        run(dve.scalar_tensor_tensor(
                            out=x, in0=wide(const[:, d:d + n].unsqueeze(1), 1, 2),
                            scalar=const[:, bass.ds(i * 8 + (C_SLOPE + h), 1)],
                            in1=psum[:, SCORE_BANKS[s % 4], 0:2 * n].rearrange("p (b n) -> p b n", b=2),
                            op0=ALU.mult, op1=ALU.add))
                        dve.tensor_reduce(red[:, s % 4, 0:2], x, AX.X, ALU.max, negate=True).then_inc(
                            S["sel_biased"], 1)

                    def scaled(s):
                        r, half, t = s // 4, s // 2 % 2, s % 2
                        n, h = P * (t + 1), 2 * r + half
                        sums = red[:, s % 4, 2:4]
                        dve.wait_ge(S["sel_exp"], i * 32 + 2 * (s + 1))
                        run(dve.tensor_scalar(sums, sums, 1e-30, None, ALU.max))
                        run(dve.reciprocal(sums, sums))
                        for br in range(2):
                            g = 8 * (br + 1) + h
                            step(dve.tensor_tensor(sums[:, br:br + 1], sums[:, br:br + 1], gates[:, t, i, g:g + 1],
                                                   ALU.mult))
                        step.wait()
                        x = prob[:, s % 4, :]
                        run(dve.tensor_scalar(x[:, 0:n], x[:, 0:n], sums[:, 0:1], None, ALU.mult))
                        dve.tensor_scalar(x[:, n:2 * n], x[:, n:2 * n], sums[:, 1:2], None,
                                          ALU.mult).then_inc(S["sel_prob"], 1)

                    biased(0)
                    biased(1)
                    for s in range(16):
                        if s + 2 < 16:
                            biased(s + 2)
                        scaled(s)

                turn(0)
                step.leave(1)
                with dve.Fori(1, 2) as i:
                    turn(i)
                step.leave(2 - 1)

            def top16(rows):
                stages = (lambda v, b, x: dve.max(b[:, 0:8], v),
                          lambda v, b, x: dve.max_index(x[:, 0:8].bitcast(U32), b[:, 0:8], v),
                          lambda v, b, x: dve.match_replace(v, b[:, 0:8], v, NEG * 1e8),
                          lambda v, b, x: dve.max(b[:, 8:16], v),
                          lambda v, b, x: dve.max_index(x[:, 8:16].bitcast(U32), b[:, 8:16], v))
                for n, stage in enumerate(stages):
                    for values, best_out, index_out in rows:
                        if n:
                            step.wait(len(rows) - 1)
                        step(stage(values, best_out, index_out))

            def ranks(some):
                c, b, m, mi = place[:, 0], place[:, 1], place[:, 2:5], place[:, 5]
                step.wait()
                heads = slice(some * HALF, (some + 1) * HALF)
                at = flat[:, :, heads, :].rearrange("p t h k -> p t (h k)").bitcast(U32)
                step(dve.tensor_copy(c, at))
                idf = sub_idf[:, :, some * SUBS // 2:(some + 1) * SUBS // 2, :]
                step(dve.tensor_copy(idf, sub_idx[:, :, some * SUBS // 2:(some + 1) * SUBS // 2, :].bitcast(U32)))
                step.wait(1)
                width = CAND_ROWS[0][2]
                for n, (first, _, now) in enumerate(CAND_ROWS[1:]):
                    low_bits = now - 1
                    step(dve.tensor_scalar(m[:, n], c, float(CAND_START[first]), float(low_bits - (width - 1)),
                                           ALU.is_ge, ALU.mult))
                    width = now
                step.wait(1)
                step(dve.scalar_tensor_tensor(out=m[:, 0], in0=m[:, 0], scalar=float(TOPK - 1), in1=m[:, 1],
                                              op0=ALU.add, op1=ALU.add))
                step.wait()
                step(dve.tensor_tensor(m[:, 0], m[:, 0], m[:, 2], ALU.add))
                both = sub_idf.rearrange("p t (h s) k -> p t h s k", s=2)[:, :, heads, 0, :]
                step.wait()
                step(dve.tensor_copy(mi.bitcast(U32), m[:, 0]))
                for t in range(T):
                    x = both[:, t]
                    y = spare[:, t]
                    step(dve.tensor_tensor(y, x[:, :, 1:TOPK], x[:, :, 0:TOPK - 1], ALU.subtract))
                step.wait()
                for t in range(T):
                    step(dve.tensor_copy(both[:, t, :, 1:TOPK], spare[:, t]))
                step(dve.tensor_tensor(mi.bitcast(U32), mi.bitcast(U32), at, ALU.bitwise_and))
                step.wait()
                step(dve.tensor_copy(b, mi.bitcast(U32)))
                step.wait()
                for t in range(T):
                    for s in range(2):
                        of = wide(place[:, s, t, :].unsqueeze(2), 2, TOPK)
                        against = wide((cand_start, iota16)[s].unsqueeze(1), 1, HALF * TOPK)
                        dve.tensor_tensor(match[:, s, t].rearrange("p h k c -> p (h k) c"), of, against,
                                          (ALU.is_ge, ALU.is_equal)[s]).then_inc(S["match_ready"], 1)

            def sums(layer, some, s, t):
                step(dve.tensor_reduce(pairs[:, t, s, some * HALF * TOPK:(some + 1) * HALF * TOPK],
                                       match[:, s, t].rearrange("p h k c -> p (h k) c"), AX.X, ALU.add))

            def route(layer):
                for b in range(4):
                    dve.wait_ge(S["hidden_hi"], 4 * layer + b + 1)
                    dve.tensor_tensor(hT_lo[:, 2 * b:2 * b + 2, :], hT[:, 2 * b:2 * b + 2, :],
                                      hT_hi[:, 2 * b:2 * b + 2, :].bitcast(F32), ALU.subtract).then_inc(
                                          S["hidden_lo"], 1)
                for h in range(PEER_HEADS):
                    for j in (2 * h, 2 * h + 1):
                        dve.wait_ge(S["score_copied"], layer * SUBS + j + 1)
                        top16([(scores[:, t, j, :], sub_top[:, t, j, :], sub_idx[:, t, j, :]) for t in range(T)])
                    step.wait(T)
                    for t in range(T):
                        for first, to, width in CAND_ROWS:
                            at, n = CAND_START[first], to - first
                            step(dve.tensor_tensor(cand[:, t, at:at + n * width].rearrange("p (a b) -> p a b", a=n),
                                                   wide(sub_top[:, t, 2 * h, first:to].unsqueeze(2), 2, width),
                                                   wide(sub_top[:, t, 2 * h + 1, 0:width].unsqueeze(1), 1, n), ALU.add))
                    step.wait()
                    top16([(cand[:, t, :], best[:, t, h, :], flat[:, t, h, :]) for t in range(T)])
                    if h == HALF - 1:
                        ranks(0)
                    if h == HALF + 1:
                        for n, (s, t) in enumerate(TAKEN_BY_POOL[0]):
                            dve.wait_ge(S["match_taken"], layer * POOL_TAKES + n + 1)
                            sums(layer, 0, s, t)
                for t in range(T):
                    g = pairs[:, t, 2, :].rearrange("p (h k) -> p h k", h=PEER_HEADS)
                    dve.tensor_tensor(g, best[:, t, :, :], wide(best[:, t, :, 0:1], 2, TOPK),
                                      ALU.subtract).then_inc(S["route_exp_in"], 1)
                ranks(1)
                dve.wait_ge(S["match_ready"], 8 * (layer + 1))
                for t in range(T):
                    g = pairs[:, t, 2, :].rearrange("p (h k) -> p h k", h=PEER_HEADS)
                    own = [s for s in range(2) if (s, t) not in TAKEN_BY_POOL[1]]
                    for s in own:
                        step(dve.tensor_tensor(match[:, s, t], match[:, s, t], taken_indices(s, t, 1), ALU.mult))
                    dve.wait_ge(S["route_exp"], layer * T + t + 1)
                    step(dve.tensor_reduce(soft_red[:, 0, t, :], g, AX.X, ALU.add))
                    step.wait()
                    step(dve.reciprocal(soft_red[:, 1, t, :], soft_red[:, 0, t, :]))
                    for s in own:
                        sums(layer, 1, s, t)
                    if len(own) < 2:
                        dve.wait_ge(S["match_taken"], (layer + 1) * POOL_TAKES)
                        sums(layer, 1, 0, t)
                    step.wait()
                    dve.tensor_tensor(g, g, wide(soft_red[:, 1, t, :].unsqueeze(2), 2, TOPK),
                                      ALU.mult).then_inc(S["route_out"], 1)
                for t in range(T):
                    dve.wait_ge(S["route_turned"], layer * T + t + 1)
                    dve.tensor_copy(pairsT[:, t * P // 4:(t + 1) * P // 4, :, :].rearrange("p g n m -> p n g m"),
                                    psum[:, 6 + t, 0:3 * P].rearrange("p (n g m) -> p n g m", n=3, m=4)).then_inc(
                                        S["pairs_turned"], 1)
                dve.wait_ge(S["pairs_turned"], T * (layer + 1))
                def turn(i):
                    for q in range(2):
                        k = layer * (SEQ // 4) + q
                        free(dve, S["g_ready"], i * 2 + (k - 1))
                        for m in range(4):
                            of = [pairsT[:, bass.ds(i * 2 + q, 1), n, m:m + 1].rearrange("p a m -> p (a m)")
                                  for n in (0, 2)]
                            dve.tensor_scalar(hot[:, q, 0, m, :], iota, of[0], of[1], ALU.is_equal,
                                              ALU.mult).then_inc(S["hot_rows"], 1)
                        dve.wait_ge(S["apart"], i * 2 + (k + 1))
                        x = hot[:, q, 1, :, :]
                        dve.tensor_scalar(x, x, 0.0, None, ALU.is_equal).then_inc(S["hot_ready"], 1)

                turn(0)
                with dve.Fori(1, SEQ // 8) as i:
                    turn(i)

            def experts(layer):
                b, w = base(layer) + PROJ + OUTW + WQ, layer * KEYS
                dve.wait_ge(S["g_copied"], (layer + 1) * (SEQ // 4))

                def low(slot, high):
                    for n in range(2):
                        cols = slice(n * 512, (n + 1) * 512)
                        dve.wait_ge(S["hi_done"], high + 1 + n)
                        dve.tensor_tensor(slab_lo[:, slot % 2, cols], ring[:, slot, cols],
                                          slab_hi[:, slot % 2, cols].bitcast(F32), ALU.subtract).then_inc(
                                              split_done, 1)

                def weigh(parity, e, ready, free):
                    dve.wait_ge(S["hidden_ready"], ready)
                    if free is not None:
                        dve.wait_ge(slab_done, free)
                    x = hidden[:, parity, :]
                    dve.tensor_tensor(x, x, G[:, e, :], ALU.mult).then_inc(S["raw_weighted"], 1)
                    dve.wait_ge(S["raw_weighted"], ready)
                    step(dve.tensor_copy(weighted_hi[:, parity, :], x))
                    step.wait()
                    dve.tensor_tensor(weighted_lo[:, parity, :], x, weighted_hi[:, parity, :].bitcast(F32),
                                      ALU.subtract).then_inc(S["weighted_ready"], 1)

                z = 2 * layer * EXP
                low(0, z)
                low(1, z + 2)
                low(2, z + 4)
                weigh(0, 0, w + 1, None)

                def turn(k):
                    step.enter(k, 2)
                    low(3, k * 8 + (z + 6))
                    weigh(1, k * 2 + 1, k * 2 + (w + 2), k * 4 + (b + 1))
                    low(0, k * 8 + (z + 8))
                    low(1, k * 8 + (z + 10))
                    weigh(0, k * 2 + 2, k * 2 + (w + 3), k * 4 + (b + 3))
                    low(2, k * 8 + (z + 12))

                turn(0)
                step.leave(1)
                with dve.Fori(1, KEYS // 2 - 1) as k:
                    turn(k)
                step.leave(KEYS // 2 - 2)
                low(3, z + 510)
                weigh(1, KEYS - 1, w + KEYS, b + 253)

            for layer in range(LAYERS):
                even_mixer() if layer == 0 else odd_mixer()
                layer_norm(layer, 0)
                route(layer)
                experts(layer)
                layer_norm(layer, 1)


def _cols(w, order=None):
    w = w if order is None else w[:, order]
    return w.reshape(KC, P, -1, P).transpose(2, 1, 0, 3).reshape(-1, P, D)


def _rows(w):
    return w.reshape(-1, P, D)


def lay_out(x):
    even, odd = x["even_w_in"][0], x["odd_w_in"][0]
    c, n = GROUPS * CH, SB_PAIRS * P
    u, q, k, v = even[:, :c], even[:, c:c + n], even[:, c + n:c + 2 * n], even[:, c + 2 * n:]
    qk = np.stack([_cols(q), _cols(k)], 1).reshape(-1, P, D)
    even_slabs = [_cols(u), _cols(v), qk, _rows(x["even_w_out"][0])]
    order = np.array([((2 * p + half) * 4 + r) * HEAD + d for p in range(2) for r in range(4) for half in range(2)
                      for d in range(HEAD)])
    kv = [_cols(odd[:, D + 256 * m:D + 256 * (m + 1)]) for m in range(6)]
    qs = _cols(odd[:, order])
    kc, vc, ks, vs, kw, vw = kv
    odd_slabs = [kc, vc]
    for p in range(2):
        odd_slabs += [ks[p:p + 1], kw[p:p + 1], vs[p:p + 1], vw[p:p + 1], qs[4 * p:4 * p + 4]]
    odd_slabs.append(_rows(x["odd_w_out"][0][order]))
    slabs = []
    for layer, mixer in ((0, even_slabs), (1, odd_slabs)):
        slabs += mixer
        slabs.append(_cols(x["peer_w_q"][layer]))
        up = x["peer_u"][layer].reshape(KEYS, P, KC, P).transpose(0, 3, 2, 1).reshape(KEYS, P, D)
        down = _rows(x["peer_v"][layer])
        both = np.empty((EXP, P, D), np.float32)
        ups = [0] + [4 * k + 1 if e % 2 else 4 * k + 3 for e in range(1, KEYS) for k in [(e - 1) // 2]]
        downs = [4 * (e // 2) + 2 if e % 2 == 0 else 4 * ((e + 1) // 2) for e in range(KEYS)]
        ups[KEYS - 1], downs[KEYS - 1] = EXP - 3, EXP - 1
        both[ups], both[downs] = up, down
        slabs.append(both)
    lam = [x["even_lam_re"][0], x["even_lam_im"][0], np.repeat(x["even_log_dt"][0][:, None], STATE, 1)]
    lam = [m.reshape(ST, P).T for m in lam]
    par = np.concatenate(lam + [x["even_d"][0].reshape(UT, P).T, x["even_b_glu"][0].reshape(UT, P).T], 1)
    b_lay = np.zeros((P, ST, 2, P), np.float32)
    c_lay = np.zeros((P, ST, 2, P), np.float32)
    for g in range(GROUPS):
        j, s, ch = g // 2, (g % 2) * STATE, (g % 8) * CH
        for r, (bm, cm) in enumerate((("even_b_re", "even_c_re"), ("even_b_im", "even_c_im"))):
            b_lay[ch:ch + CH, j, r, s:s + STATE] = x[bm][0, g].T
            c_lay[s:s + STATE, j, r, ch:ch + CH] = x[cm][0, g].T
    gate = odd[:, D + 6 * 256:].reshape(D, NBR, 2, 2, 4).transpose(0, 2, 1, 4, 3).reshape(KC, P, 48).transpose(1, 0, 2)

    def dup(m):
        return np.concatenate([m, m], 0)

    w1 = {n: x[f"odd_w1_{n}"][0].reshape(CMP_BLOCK, HEAD, P).transpose(1, 0, 2) for n in "kv"}
    w2 = np.stack([np.concatenate([x[f"odd_w2_{n}"][0]] * 2, 1) for n in "kv"], 1)
    pe = np.stack([dup(x[f"odd_pe_{n}"][0].T) for n in "kv"], 1)
    keys = x["peer_sub_keys"].reshape(LAYERS, SUBS, KEYS, P).transpose(0, 3, 1, 2)
    ln = np.stack([x[n][layer] for layer in range(LAYERS) for k in (1, 2) for n in (f"ln{k}_g", f"ln{k}_b")])
    xs = x["x"][0]
    out = {
        "slabs": np.concatenate(slabs), "x": xs.reshape(T, P, D).transpose(1, 0, 2),
        "xT": xs.T.reshape(KC, P, SEQ).transpose(1, 0, 2), "s5_par": par, "s5_b": b_lay, "s5_c": c_lay,
        "glu_w": x["even_w_glu"][0].reshape(UT, P, UT * P).transpose(1, 0, 2), "gate_w": gate,
        "w1k": w1["k"], "w1v": w1["v"], "w2": w2, "pe": pe, "keys": keys, "ln": ln, "const": constants(),
    }
    return {n: np.ascontiguousarray(m) for n, m in out.items()}


def kernel(**inputs):
    import concourse.bacc as bacc
    from concourse.bass_utils import run_bass_kernel_spmd

    arrays = lay_out({n: np.asarray(m) for n, m in inputs.items()})
    nc = bacc.Bacc("TRN2", target_bir_lowering=False, num_devices=1)
    aps = {n: nc.dram_tensor(f"in_{n}", m.shape, F32, kind="ExternalInput").ap() for n, m in arrays.items()}
    aps["out"] = nc.dram_tensor("out", (SEQ, D), F32, kind="ExternalOutput").ap()
    build(nc, aps)
    r = run_bass_kernel_spmd(nc, [{f"in_{n}": m for n, m in arrays.items()}], core_ids=[0])
    return r.results[0]["out"].reshape(1, SEQ, D)
```

```python
from contextlib import ExitStack

import numpy as np

import concourse.bass as bass
from concourse import mybir

ALU = mybir.AluOpType
ACT = mybir.ActivationFunctionType
AX = mybir.AxisListType
F32 = mybir.dt.float32
F32R = mybir.dt.float32r
U32 = mybir.dt.uint32

P = 128
SEQ = 256
D = 1024
T = SEQ // P
KC = D // P
LAYERS = 2
RING = 4

GROUPS, STATE, CH = 16, 64, 16
UT = GROUPS * CH // P
ST = GROUPS * STATE // P
SB_PAIRS = 6
HEAD = 64
SCALE = HEAD ** -0.5
CMP_BLOCK, CMP_STRIDE = 32, 16
NCMP = (SEQ - CMP_BLOCK) // CMP_STRIDE + 1
GROUP_ROWS = SEQ // CMP_STRIDE
CMP_ROWS = 4 * GROUP_ROWS - 1
NSA_HEADS = 16
NBR = 3
EPS = 1e-5
ALPHA = (2 * LAYERS) ** 0.25
PEER_HEADS, KEYS, TOPK = 8, 128, 16
SHARE = 2
SHARES = PEER_HEADS // SHARE
SUBS = 2 * PEER_HEADS
NEG = -1e30

CAND_ROWS = ((0, 1, 16), (1, 4, 8), (4, 8, 4), (8, 16, 1))
CAND_START = [0]
for _from, _to, _width in CAND_ROWS:
    CAND_START += [CAND_START[-1] + _width * (n + 1) for n in range(_to - _from)]
CANDS = CAND_START.pop()

PROJ, OUTW, WQ, EXP = 20, 8, 16, 2 * KEYS
SCORE_BANKS = (6, 7, 4, 5)
PER_LAYER = PROJ + OUTW + WQ + EXP
SLABS = LAYERS * PER_LAYER
PROJ_PER_LAYER = PROJ + WQ
HOT, HOT_GROUPS, HOT_SCALED = 4, SEQ // 4, 2
HOT_TURNS = HOT_GROUPS // HOT

TWO_PI = 2 * np.pi
PI_A = 6.28125
PI_B = float(np.float32(TWO_PI - PI_A))
PI_C = float(np.float32(TWO_PI - PI_A - PI_B))
ROUND = 1.5 * 2.0 ** 23
PI_IN = float(np.nextafter(np.float32(np.pi), np.float32(0)))

C_IDENT, C_TRI, C_ONES, C_BELOW, C_NEGDIAG = 0, 128, 256, 384, 512
C_IOTA, C_IOTA16, C_DIST, C_SLOPE = 640, 768, 784, 784 + 384
C_CMPBIAS = C_SLOPE + NSA_HEADS
C_CMPMASK = C_CMPBIAS + T * NSA_HEADS * NCMP
C_START = C_CMPMASK + T * NCMP
C_ALL = C_START + TOPK


def constants():
    c = np.zeros((P, C_ALL), np.float32)
    i = np.arange(P)
    c[:, C_IDENT:C_IDENT + P] = np.eye(P)
    c[:, C_TRI:C_TRI + P] = -1.0 * (i[:, None] >= i[None, :])
    c[:, C_ONES:C_ONES + P] = -1
    c[:, C_BELOW:C_BELOW + P] = i[:, None] < i[None, :]
    c[:, C_NEGDIAG:C_NEGDIAG + P] = np.where(i[:, None] < i[None, :], 0, NEG)
    c[:, C_IOTA:C_IOTA + P] = i[None, :]
    c[:, C_IOTA16:C_IOTA16 + TOPK] = np.arange(TOPK)[None, :]
    col = C_DIST
    for t in range(T):
        n = P * (t + 1)
        dist = (t * P + i[:, None]) - np.arange(n)[None, :]
        c[:, col:col + n] = np.where(dist >= 0, -dist, NEG)
        col += n
    head = np.arange(NSA_HEADS)
    order = np.array([(2 * p + half) * 4 + r for p in range(2) for r in range(4) for half in range(2)])
    slope = (2.0 ** (-8.0 * (head + 1) / NSA_HEADS)).astype(np.float32)[order]
    c[:, C_SLOPE:C_SLOPE + NSA_HEADS] = slope
    ends = np.arange(NCMP) * CMP_STRIDE + CMP_BLOCK - 1
    for t in range(T):
        dist = ((t * P + i[:, None]) - ends[None, :]).astype(np.float32)
        bias = np.where(dist[:, None, :] >= 0, -slope[None, :, None] * dist[:, None, :], np.float32(NEG))
        a = C_CMPBIAS + t * NSA_HEADS * NCMP
        c[:, a:a + NSA_HEADS * NCMP] = bias.reshape(P, -1)
        a = C_CMPMASK + t * NCMP
        c[:, a:a + NCMP] = dist >= 0
    c[:, C_START:C_START + TOPK] = CAND_START
    return c


def wide(ap, axis, n):
    shape = list(ap.shape)
    shape[axis] = n
    return ap.broadcast_to(tuple(shape))


def free(eng, sem, count):
    if not isinstance(count, int) or count > 0:
        eng.wait_ge(sem, count)


class Steps:

    def __init__(self, eng, sem):
        self.eng, self.sem, self.n, self.turn = eng, sem, 0, 0

    def __call__(self, ins):
        self.n += 1
        ins.then_inc(self.sem, 1)

    def wait(self, behind=0):
        self.eng.wait_ge(self.sem, self.turn + self.n - behind)

    def enter(self, i, per):
        self.turn = 0 if isinstance(i, int) else (i - 1) * per
        self.start, self.per = self.n, per

    def leave(self, turns):
        assert self.n - self.start == self.per, (self.n - self.start, self.per)
        self.n, self.turn = self.n + (turns - 1) * self.per, 0


def build(nc, a):
    with ExitStack() as ctx:
        def sb(name, shape, dt=F32):
            return ctx.enter_context(nc.sbuf_tensor(name, shape, dt))

        def sem(name):
            return ctx.enter_context(nc.semaphore(name))

        psum = ctx.enter_context(nc.psum_tensor("psum", [P, 8, 512], F32))
        ring = sb("ring", [P, RING, D])
        h_nat = sb("h_nat", [P, T, D])
        hT_hi = sb("hT_hi", [P, KC, SEQ], F32R)
        hT_lo = sb("hT_lo", [P, KC, SEQ], F32R)
        slab_hi = sb("slab_hi", [P, 2, D], F32R)
        slab_lo = sb("slab_lo", [P, 2, D], F32R)
        weighted_hi = sb("weighted_hi", [P, 2, SEQ], F32R)
        weighted_lo = sb("weighted_lo", [P, 2, SEQ], F32R)
        big = sb("big", [P, SEQ * KEYS])
        const = sb("const", [P, C_ALL])
        hidden = sb("hidden", [P, 2, SEQ])
        pairsT = sb("pairsT", [P, SEQ // 4, 3, 4])
        hot_own = sb("hot_own", [P, 2, D])
        hot = [x.rearrange("p (r m k) -> p r m k", r=2, m=4)
               for x in (hot_own[:, 0, :], hot_own[:, 1, :], ring[:, RING - 2, :], ring[:, RING - 1, :])]
        small = sb("small", [P, 32])

        used = [0]

        def view(n):
            used[0] += n
            assert used[0] <= SEQ * KEYS
            return big[:, used[0] - n:used[0]]

        G = big[:, :].rearrange("p (e t) -> p e t", t=SEQ)
        mixT = view(KC * SEQ).rearrange("p (c t) -> p c t", c=KC)
        hT = view(KC * SEQ).rearrange("p (c t) -> p c t", c=KC)
        shared = used[0]
        uT = view(UT * SEQ).rearrange("p (c t) -> p c t", c=UT)
        v_nat = view(T * SB_PAIRS * P).rearrange("p (t n) -> p t n", t=T)
        b_lay = view(ST * 2 * P).rearrange("p (j r n) -> p j r n", j=ST, r=2)
        c_lay = view(ST * 2 * P).rearrange("p (j r n) -> p j r n", j=ST, r=2)
        glu_w = view(UT * UT * P).rearrange("p (c n) -> p c n", c=UT)
        s5_par = view(3 * ST + 2 * UT)
        phase = view(2 * ST * SEQ).rearrange("p (r j t) -> p r j t", r=2, j=ST)
        drive = view(2 * ST * SEQ).rearrange("p (r j t) -> p r j t", r=2, j=ST)
        turned = view(2 * ST * SEQ).rearrange("p (r j t) -> p r j t", r=2, j=ST)
        temp = view(2 * ST * SEQ).rearrange("p (r j t) -> p r j t", r=2, j=ST)
        s5_small = view(24 * ST).rearrange("p (n j) -> p n j", j=ST)
        qk = view(4 * SEQ).rearrange("p (n t) -> p n t", n=4)
        v_pair = view(2 * T * P).rearrange("p (n t d) -> p n t d", n=2, t=T)
        stick_flat = view(4 * 2 * 384)
        stick = stick_flat.rearrange("p (h n c) -> p h n c", h=4, n=2)
        yT = temp.rearrange("p r j t -> p (r j t)")[:, 0:3 * UT * SEQ].rearrange("p (n c t) -> p n c t", n=3, c=UT)
        used[0] = shared
        kvc = view(4 * SEQ).rearrange("p (n t) -> p n t", n=4)
        blocks = view(2 * 4 * SEQ).rearrange("p (n c) -> p n c", n=2)
        moving = view(2 * 2 * SEQ).rearrange("p (n c) -> p n c", n=2)
        nsa_from = used[0]
        w1 = view(2 * CMP_STRIDE * P).rearrange("p (n o m) -> p n o m", n=2, o=CMP_STRIDE)
        w2 = view(2 * P).rearrange("p (n m) -> p n m", n=2)
        peT = view(2 * 2 * CMP_STRIDE).rearrange("p (n w o) -> p n w o", n=2, w=2)
        gate_w = view(KC * 48).rearrange("p (c n) -> p c n", c=KC)
        nsa_rows = -(-used[0] // SEQ)
        gates = view(T * 48).rearrange("p (t g n) -> p t g n", t=T, g=2)
        cmp_hid = view(2 * 2 * 2 * NCMP).rearrange("p (n f g m) -> p n f g m", n=2, f=2, g=2)
        cmp_act = view(2 * P).rearrange("p (n m) -> p n m", n=2)
        kcT = view(2 * NCMP).rearrange("p (g m) -> p g m", g=2)
        vc = view(2 * P).rearrange("p (g m) -> p g m", g=2)
        kc_now = view(NCMP)
        vc_now = view(P)
        kT = view(2 * SEQ).rearrange("p (n t) -> p n t", n=2)
        vN = view(2 * T * P).rearrange("p (n t d) -> p n t d", n=2, t=T)
        qT = view(4 * SEQ).rearrange("p (r t) -> p r t", r=4)
        pc = view(T * 8 * NCMP).rearrange("p (t h m) -> p t h m", t=T, h=8)
        pc_red = view(T * 8 * 2).rearrange("p (n t h) -> p n t h", n=2, t=T)
        prob = view(4 * 512).rearrange("p (s c) -> p s c", s=4)
        probT = view(2 * 512).rearrange("p (s c) -> p s c", s=2)
        pcT = view(2 * P).rearrange("p (s c) -> p s c", s=2)
        red = view(4 * 8).rearrange("p (s c) -> p s c", s=4)
        used[0] = shared
        scores = view(T * SUBS * KEYS).rearrange("p (t j k) -> p t j k", t=T, j=SUBS)
        sub_q = view(2 * SEQ).rearrange("p (s t) -> p s t", s=2)
        sub_top = view(T * SUBS * TOPK).rearrange("p (t j k) -> p t j k", t=T, j=SUBS)
        sub_idx = view(T * SUBS * TOPK).rearrange("p (t j k) -> p t j k", t=T, j=SUBS)
        sub_idf = view(T * SUBS * TOPK).rearrange("p (t j k) -> p t j k", t=T, j=SUBS)
        cand = view(2 * T * CANDS).rearrange("p (n t c) -> p n t c", n=2, t=T)
        best = view(T * PEER_HEADS * TOPK).rearrange("p (t h k) -> p t h k", t=T, h=PEER_HEADS)
        flat = view(T * PEER_HEADS * TOPK).rearrange("p (t h k) -> p t h k", t=T, h=PEER_HEADS)
        place = view(6 * T * SHARE * TOPK).rearrange("p (n t c) -> p n t c", n=6, t=T)
        spare = view(T * SHARE * (TOPK - 1)).rearrange("p (t h k) -> p t h k", t=T, h=SHARE)
        match = view(2 * T * SHARE * TOPK * TOPK).rearrange("p (s t h k c) -> p s t h k c", s=2, t=T, h=SHARE, k=TOPK)
        pairs = view(T * 3 * PEER_HEADS * TOPK).rearrange("p (t n c) -> p t n c", t=T, n=3)
        soft_red = view(2 * T * PEER_HEADS).rearrange("p (n t h) -> p n t h", n=2, t=T)
        keysT = view(SUBS * KEYS).rearrange("p (j k) -> p j k", j=SUBS)
        used[0] = shared
        squares = view(T * D).rearrange("p (t d) -> p t d", t=T)
        ln_rows = (used[0] // SEQ, used[0] // SEQ + 2 * D // SEQ)
        ln_par = view(2 * D).rearrange("p (k d) -> p k d", k=2)
        assert used[0] <= nsa_from

        centred = big[:, SEQ * KEYS - T * D:].rearrange("p (t d) -> p t d", t=T)

        ident = const[:, C_IDENT:C_IDENT + P]
        neg_tri = const[:, C_TRI:C_TRI + P]
        neg_ones = const[:, C_ONES:C_ONES + P]
        below = const[:, C_BELOW:C_BELOW + P]
        neg_diag = const[:, C_NEGDIAG:C_NEGDIAG + P]
        iota = const[:, C_IOTA:C_IOTA + P]
        iota16 = const[:, C_IOTA16:C_IOTA16 + TOPK]
        cand_start = const[:, C_START:C_START + TOPK]

        names = """const_loaded xT_loaded s5_par_loaded s5_b_loaded s5_loaded ln_loaded keys_loaded nsa_loaded out_stored 
            slab_done proj_copied hi_done split_done hidden_hi hidden_lo raw_weighted
            act_steps dve_steps pool_steps
            ln_mean ln_square ln_var ln_rstd ln_done ln_turned ln_copied
            s5_dt s5_rates s5_mag s5_angle s5_sine s5_pq s5_pq_used s5_turned s5_scanned s5_states s5_y s5_y_in s5_gelu s5_z s5_gate s5_out
            v_staged z_ready z_log stick_ready tails_ready masked stick_w pv_ready o_copied
            cmp_staying cmp_leaving cmp_moved_k cmp_moved_v cmp_ready cmp_act_ready cmp_turned cmp_hidden cmp_kv cmp_kv_copied gate_ready gate_done cmp_staged cmp_scores cmp_shifted cmp_exp cmp_aux cmp_probs
            sel_scores sel_biased sel_exp sel_prob sel_turned sel_copied sel_out sel_stored
            score_ready score_copied sub_ranked cand_ready cand_ranked match_ready match_taken route_exp_in route_exp route_out route_turned 
            pairs_turned apart hot_equal hot_scaled hot_rows hot_ready g_ready g_copied hidden_ready weighted_ready""".split()
        S = {n: sem(n) for n in names}
        slab_loaded = [sem(f"slab_loaded{s}") for s in range(RING)]
        slab_done, proj_copied, split_done = S["slab_done"], S["proj_copied"], S["split_done"]
        block = ctx.enter_context(nc.Block())

        def base(layer):
            return layer * PER_LAYER

        def pair_column(i, q, n, m):
            return pairsT[:, bass.ds(i * HOT + q, 1), n, m:m + 1].rearrange("p a m -> p (a m)")

        def group_of(i, q, n, count):
            return wide(pairsT[:, bass.ds(i * HOT + q, 1), n, 0:count].rearrange("p a m -> p (a m)").unsqueeze(2), 2, KEYS)

        TAKEN_BY_POOL = (((0, 0), (1, 0), (0, 1), (1, 1)),) * (SHARES - 1) + (((0, 0),),)
        POOL_TAKES = sum(len(x) for x in TAKEN_BY_POOL)

        def taken_indices(s, t, some):
            idf = sub_idf[:, t, 2 * some * SHARE:2 * (some + 1) * SHARE, :].rearrange("p (h s) k -> p h s k", s=2)
            return wide(idf[:, :, s, :].unsqueeze(2), 2, TOPK)

        @block.sync
        def _(sp):
            sp.dma_start(hT[:, :, :], a["xT"]).then_inc(S["xT_loaded"], 16)
            for s in range(RING):
                sp.dma_start(ring[:, s, :], a["slabs"][s]).then_inc(slab_loaded[s], 16)
            for layer in range(LAYERS):
                first, experts = layer * PER_LAYER // RING, (PER_LAYER - EXP) // RING
                if layer:
                    for s in range(RING):
                        sp.wait_ge(split_done, 2 * (layer * EXP + s + 1 - RING))
                        sp.dma_start(ring[:, s, :], a["slabs"][first * RING + s]).then_inc(slab_loaded[s], 16)
                with sp.Fori(first + 1, first + experts) as r:
                    for s in range(RING):
                        sp.wait_ge(slab_done, r * RING + (s + 1 - RING))
                        sp.dma_start(ring[:, s, :], a["slabs"][r * RING + s]).then_inc(slab_loaded[s], 16)
                for s in range(RING):
                    r = first + experts
                    sp.wait_ge(slab_done, r * RING + (s + 1 - RING))
                    if s >= RING - 2:
                        sp.wait_ge(S["g_ready"], (layer + 1) * HOT_GROUPS)
                    sp.dma_start(ring[:, s, :], a["slabs"][r * RING + s]).then_inc(slab_loaded[s], 16)
                with sp.Fori(1, EXP // RING) as r:
                    for s in range(RING):
                        sp.wait_ge(split_done, r * (2 * RING) + 2 * (layer * EXP + s + 1 - RING))
                        sp.dma_start(ring[:, s, :], a["slabs"][r * RING + ((first + experts) * RING + s)]).then_inc(
                            slab_loaded[s], 16)
            for t in range(T):
                sp.wait_ge(S["ln_done"], 2 * LAYERS * T - T + t + 1)
                sp.dma_start(a["out"][t * P:(t + 1) * P, :], h_nat[:, t, :]).then_inc(S["out_stored"], 16)
            sp.wait_ge(S["out_stored"], 16 * T)

        @block.tensor
        def _(pe):
            def landed(n):
                return (n // RING + 1) * 16

            def slab(slot, count):
                pe.wait_ge(slab_loaded[slot], count)
                return ring[:, slot, :]

            def project(n, slot, turn, pi, after_ln=None):
                w = slab(slot, turn * 16 + landed(n))
                w = w.rearrange("p (c n) -> p c n", c=KC)
                free(pe, proj_copied, pi - 1)
                out = psum[:, 4 + slot % 2, 0:SEQ]
                for c in range(KC):
                    if after_ln is not None and c % 4 == 0:
                        pe.wait_ge(S["ln_copied"], 4 * after_ln + 3 + c // 4)
                    last = pe.matmul(out, w[:, c, :], hT[:, c, :], start=(c == 0), stop=(c == KC - 1))
                last.then_inc(slab_done, 1)

            def project_natural(n, slot, turn, pi):
                slab(slot, turn * 16 + landed(n))
                slab(slot + 1, turn * 16 + landed(n + 1))
                w = ring[:, slot:slot + 2, :].rearrange("p s (c n) -> p s c n", c=KC)
                free(pe, proj_copied, pi)
                for t in range(T):
                    for c in range(KC):
                        last = pe.matmul(psum[:, 4 + t, 0:2 * P], hT[:, c, t * P:(t + 1) * P], w[:, :, c, :],
                                         start=(c == 0), stop=(c == KC - 1))
                last.then_inc(slab_done, 2)

            def accumulate(w, rows, first, last):
                for t in range(T):
                    for n in range(2):
                        mm = pe.matmul(psum[:, 2 * t + n, :], rows[:, t * P:(t + 1) * P], w[:, n * 512:(n + 1) * 512],
                                       start=first, stop=last)
                mm.then_inc(slab_done, 1)

            def turn_hidden(ln):
                for t in range(T):
                    pe.wait_ge(S["ln_done"], T * ln + t + 1)
                    for b in range(2):
                        for c in range(4):
                            mm = pe.transpose(psum[:, 2 * t + b, c * P:(c + 1) * P],
                                              h_nat[:, t, (4 * b + c) * P:(4 * b + c + 1) * P], ident)
                        mm.then_inc(S["ln_turned"], 1)

            def s5_inputs(states):
                for j in states:
                    free(pe, S["s5_pq_used"], j - 1)
                    for r in range(2):
                        mm = pe.matmul(psum[:, 6 + j % 2, r * SEQ:(r + 1) * SEQ], b_lay[:, j, r, :], uT[:, j // 4, :],
                                       start=(r == 0), stop=True, skip_group_check=True)
                    mm.then_inc(S["s5_pq"], 1)

            def s5_outputs():
                pe.wait_ge(S["s5_loaded"], 3 * 16)
                pe.wait_ge(S["s5_states"], 2)
                first = True
                for c in range(UT):
                    for j in range(4 * c, 4 * c + 4):
                        for r in range(2):
                            mm = pe.matmul(psum[:, 3, c * SEQ:(c + 1) * SEQ], c_lay[:, j, r, :], turned[:, r, j, :],
                                           start=first, stop=(j == 4 * c + 3 and r == 1), skip_group_check=True)
                            first = False
                mm.then_inc(S["s5_y"], 1)

            def s5_gates():
                pe.wait_ge(S["s5_gelu"], 1)
                first = True
                for c in range(UT):
                    for k in range(UT):
                        mm = pe.matmul(psum[:, 3, c * SEQ:(c + 1) * SEQ], glu_w[:, k, c * P:(c + 1) * P],
                                       yT[:, 1, k, :], start=first, stop=(k == UT - 1), skip_group_check=True)
                        first = False
                mm.then_inc(S["s5_z"], 1)

            def stick_logits(i, pr):
                pe.wait_ge(proj_copied, i * 4 + (8 + 2 * pr + 2))
                for h in range(2):
                    z = psum[:, (6 if pr == 0 else 0) + h, :]
                    lo, hi = 64 * h, 64 * h + 64
                    q, k = qk[lo:hi, 2 * pr, :], qk[lo:hi, 2 * pr + 1, :]
                    pe.matmul(z[:, 0:2 * P], k[:, 0:P], q, start=True, stop=False, skip_group_check=True)
                    pe.matmul(z[:, 2 * P:3 * P], k[:, P:SEQ], q[:, P:SEQ], start=False, stop=False,
                              skip_group_check=True).then_inc(S["z_ready"], 1)

            def stick_tails(i, pr):
                for h in range(2):
                    pe.wait_ge(S["stick_ready"], i * 4 + (2 * pr + h + 1))
                    z = psum[:, (6 if pr % 2 == 0 else 0) + h, :]
                    s = stick[:, 2 * (pr % 2) + h, 0, :]
                    pe.matmul(z[:, 0:3 * P], neg_tri, s[:, 0:3 * P], start=False, stop=False, skip_group_check=True)
                    pe.matmul(z[:, P:2 * P], neg_ones, s[:, 2 * P:3 * P], start=False, stop=True,
                              skip_group_check=True).then_inc(S["tails_ready"], 1)

            def stick_values(i, pr):
                pe.wait_ge(S["v_staged"], i * 2 + (pr + 1))
                for h in range(2):
                    pe.wait_ge(S["stick_w"], i * 4 + (2 * pr + h + 1))
                    w = stick[:, 2 * (pr % 2) + h, 1, :]
                    o = psum[:, 2, h * SEQ:(h + 1) * SEQ]
                    pe.matmul(o, v_pair[:, pr % 2, 0, :], w[:, 0:2 * P], start=(h == 0), stop=False,
                              skip_group_check=True)
                    mm = pe.matmul(o[:, P:SEQ], v_pair[:, pr % 2, 1, :], w[:, 2 * P:3 * P], start=False, stop=True,
                                   skip_group_check=True)
                mm.then_inc(S["pv_ready"], 1)

            def even_mixer():
                pe.wait_ge(S["xT_loaded"], 16)
                for n in range(UT):
                    project(n, n % RING, 0, n)
                project_natural(2, 2, 0, 2)
                pe.wait_ge(S["s5_b_loaded"], 16)
                pe.wait_ge(proj_copied, UT)
                s5_inputs(range(2))
                project_natural(4, 0, 0, 4)
                s5_inputs(range(2, 4))
                project_natural(6, 2, 0, 6)
                s5_inputs(range(4, ST))
                pe.wait_ge(S["const_loaded"], 16)
                pe.wait_ge(S["s5_pq_used"], ST)

                def turn(i):
                    for pr in range(2):
                        for m in range(2):
                            n = 8 + 2 * pr + m
                            project(n, n % RING, i, i * 4 + n)
                        if not isinstance(i, int):
                            stick_values(i, pr - 2)
                        stick_logits(i, pr)
                        if not isinstance(i, int) or pr:
                            stick_tails(i, pr - 1)

                turn(0)
                with pe.Fori(1, SB_PAIRS // 2) as i:
                    turn(i)
                s5_outputs()
                stick_values(SB_PAIRS // 2, -2)
                stick_tails(SB_PAIRS // 2, -1)
                stick_values(SB_PAIRS // 2, -1)
                s5_gates()
                pe.wait_ge(S["o_copied"], 2 * SB_PAIRS)
                pe.wait_ge(S["s5_out"], UT)

            def compress():
                pe.wait_ge(S["nsa_loaded"], 5 * 16)
                for t in range(T):
                    for c in range(KC):
                        mm = pe.matmul(psum[:, 7, 48 * t:48 * t + 48], hT[:, c, t * P:(t + 1) * P], gate_w[:, c, :],
                                       start=(c == 0 and t == 0), stop=(c == KC - 1), skip_group_check=True)
                mm.then_inc(S["gate_ready"], 1)
                for n in range(2):
                    pe.wait_ge(S["cmp_staying"], 2 * (n + 1))
                    pe.wait_ge(S["cmp_moved_" + "kv"[n]], 2 * 16)
                    x = blocks[:, n, :].rearrange("p (m o) -> p m o", o=CMP_STRIDE)
                    for o in range(CMP_STRIDE):
                        mm = pe.matmul(psum[0:CMP_ROWS, 3 * n, 0:P], x[:, 0:CMP_ROWS, o], w1[:, n, o, :],
                                       start=(o == 0), stop=(o == CMP_STRIDE - 1))
                    mm.then_inc(S["cmp_ready"], 1)
                pe.wait_ge(S["cmp_act_ready"], 2)
                for n in range(2):
                    mm = pe.transpose(psum[:, 1, n * 64:n * 64 + CMP_ROWS],
                                      cmp_act[0:CMP_ROWS, n, :], ident[0:CMP_ROWS, 0:CMP_ROWS])
                mm.then_inc(S["cmp_turned"], 1)
                pe.wait_ge(S["cmp_hidden"], 2)
                pe.matmul(psum[:, 2, 128:128 + 4 * NCMP], w2[:, 0, :],
                          cmp_hid[:, 0, :, :, :].rearrange("p f g m -> p (f g m)"), start=True, stop=True,
                          skip_group_check=True)
                for f in range(2):
                    for g in range(2):
                        mm = pe.matmul(psum[0:NCMP, 2, 256 + g * P + 64 * f:256 + g * P + 64 * f + 64],
                                       cmp_hid[:, 1, f, g, :], w2[:, 1, 0:64], start=False, stop=True,
                                       skip_group_check=True)
                mm.then_inc(S["cmp_kv"], 1)

            def nsa_scores(i, s):
                r, half, t = s // 4, s // 2 % 2, s % 2
                if s >= 4:
                    pe.wait_ge(S["sel_biased"], i * 16 + (s - 3))
                rows, n = slice(64 * half, 64 * half + 64), P * (t + 1)
                for br in range(2):
                    mm = pe.matmul(psum[:, SCORE_BANKS[s % 4], br * n:(br + 1) * n], qT[rows, r, t * P:(t + 1) * P],
                                   kT[rows, br, 0:n], start=(br == 0), stop=True, skip_group_check=True)
                mm.then_inc(S["sel_scores"], 1)

            def nsa_turn(i, s):
                r, half, t = s // 4, s // 2 % 2, s % 2
                pe.wait_ge(S["sel_prob"], i * 16 + (s + 1))
                if s >= 2:
                    pe.wait_ge(S["sel_copied"], i * 16 + (s - 1))
                if s == 0:
                    pe.wait_ge(S["cmp_probs"], i + 1)
                pe.transpose(psum[0:NCMP, 3 * t, 256:256 + P], pc[:, t, 2 * r + half, :], ident)
                for m in range(2 * (t + 1)):
                    mm = pe.transpose(psum[:, s % 2, m * P:(m + 1) * P], prob[:, s % 4, m * P:(m + 1) * P], ident)
                mm.then_inc(S["sel_turned"], 1)

            def nsa_values(i, s):
                r, half, t = s // 4, s // 2 % 2, s % 2
                pe.wait_ge(S["sel_copied"], i * 16 + (s + 1))
                if s % 4 == 0:
                    free(pe, S["sel_stored"], i * 8 + 2 * (s // 4))
                out = psum[:, 2, half * SEQ + t * P:half * SEQ + (t + 1) * P]
                first = s % 4 == 0
                for br in range(2):
                    for k in range(t + 1):
                        m = br * (t + 1) + k
                        pe.matmul(out, vN[:, br, k, :], probT[:, s % 2, m * P:(m + 1) * P], start=first, stop=False,
                                  skip_group_check=True)
                        first = False
                pe.matmul(out, vc_now[0:NCMP, :], pcT[0:NCMP, s % 2, :], start=False, stop=True,
                          skip_group_check=True).then_inc(S["sel_out"], 1)

            def odd_mixer(layer):
                b, p = base(layer), layer * PROJ_PER_LAYER
                for n in range(4):
                    project(b + n, n % RING, 0, p + n, 2 * layer - 1 if n == 0 else None)
                compress()
                pe.wait_ge(S["gate_done"], 1)
                pe.wait_ge(S["cmp_kv_copied"], 4)
                def turn(i):
                    free(pe, S["sel_biased"], i * 16)
                    for m in (0, 1, 2, 4, 5, 6, 7):
                        n = 4 + m
                        (project_natural if m == 2 else project)(b + n, n % RING, i * 2, i * 8 + (p + n))
                    pe.wait_ge(proj_copied, i * 8 + (p + 12))
                    pe.wait_ge(S["cmp_staged"], i * 2 + 2)
                    free(pe, S["sel_copied"], i * 16)
                    for t in range(T):
                        for r in range(4):
                            for half in range(2):
                                rows = slice(64 * half, 64 * half + 64)
                                c = (t * 4 + r) * NCMP
                                mm = pe.matmul(psum[:, 3 * half, c:c + NCMP], qT[rows, r, t * P:(t + 1) * P],
                                               kc_now[rows, :], start=(c == 0), stop=True, skip_group_check=True)
                    mm.then_inc(S["cmp_scores"], 1)
                    for s in range(3):
                        nsa_scores(i, s)
                    for s in range(16):
                        if s + 3 < 16:
                            nsa_scores(i, s + 3)
                        nsa_turn(i, s)
                        if s:
                            nsa_values(i, s - 1)
                    nsa_values(i, 15)

                turn(0)
                with pe.Fori(1, 2) as i:
                    turn(i)
                pe.wait_ge(S["sel_stored"], 16)

            def out_projection(layer):
                b = base(layer) + PROJ
                for c in range(OUTW):
                    accumulate(slab((b + c) % RING, landed(b + c)), mixT[:, c, :], c == 0, c == OUTW - 1)

            def route_scores(layer):
                b, p = base(layer) + PROJ + OUTW, layer * PROJ_PER_LAYER + PROJ
                pe.wait_ge(S["keys_loaded"], 16 * (layer + 1))
                def turn(i):
                    for pr in range(2):
                        for m in range(2):
                            s = 2 * pr + m
                            project(b + s, s, i, i * 4 + (p + s), 2 * layer if isinstance(i, int) and s == 0 else None)
                        for m in range(2):
                            s = 2 * pr + m
                            pe.wait_ge(proj_copied, i * 4 + (p + s + 1))
                            free(pe, S["score_copied"], i * 4 + (SUBS * layer + s - 1))
                            for t in range(T):
                                mm = pe.matmul(psum[:, 6 + m, t * P:(t + 1) * P], sub_q[:, m, t * P:(t + 1) * P],
                                               keysT[:, i * 4 + s, :], start=(t == 0), stop=True,
                                               skip_group_check=True)
                            mm.then_inc(S["score_ready"], 1)

                turn(0)
                with pe.Fori(1, WQ // RING) as i:
                    turn(i)

            def spread(layer):
                for t in range(T):
                    pe.wait_ge(S["route_out"], layer * T + t + 1)
                    for n in range(3):
                        mm = pe.transpose(psum[:, 6 + t, n * P:(n + 1) * P], pairs[:, t, n, :], ident)
                    mm.then_inc(S["route_turned"], 1)
                def turn(i):
                    for q in range(HOT):
                        k = layer * HOT_GROUPS + q
                        pe.wait_ge(S["hot_scaled"], i * (HOT * HOT_SCALED) + HOT_SCALED * (k + 1))
                        pe.wait_ge(S["hot_rows"], i * (HOT * (4 - HOT_SCALED)) + (4 - HOT_SCALED) * (k + 1))
                        pe.wait_ge(S["hot_ready"], i * HOT + (k + 1))
                        free(pe, S["g_copied"], i * HOT + (k + 1 - HOT))
                        for m in range(4):
                            mm = pe.matmul(psum[:, 4 + q, m * KEYS:(m + 1) * KEYS], hot[q][:, 1, m, :],
                                           hot[q][:, 0, m, :], start=(m == 0), stop=True, skip_group_check=True)
                        mm.then_inc(S["g_ready"], 1)

                turn(0)
                with pe.Fori(1, HOT_TURNS) as i:
                    turn(i)

            def experts(layer):
                b, w = base(layer) + PROJ + OUTW + WQ, layer * KEYS

                def up(slot, split, e):
                    out = psum[:, 4 + e[0], 0:SEQ]
                    if e[1] is not None:
                        pe.wait_ge(S["hidden_ready"], e[1])
                    hi = slab_hi[:, slot % 2, :].rearrange("p (c n) -> p c n", c=KC)
                    lo = slab_lo[:, slot % 2, :].rearrange("p (c n) -> p c n", c=KC)
                    for c in range(KC):
                        if c % (KC // 2) == 0:
                            pe.wait_ge(split_done, split + 1 + 2 * c // KC)
                        pe.matmul(out, hi[:, c, :], hT_hi[:, c, :], start=(c == 0), stop=False)
                        pe.matmul(out, hi[:, c, :], hT_lo[:, c, :], start=False, stop=False)
                        mm = pe.matmul(out, lo[:, c, :], hT_hi[:, c, :], start=False, stop=(c == KC - 1))
                    mm.then_inc(slab_done, 1)

                def down(slot, split, parity, e, first=False, last=False):
                    pe.wait_ge(S["weighted_ready"], e)
                    for n in range(2):
                        pe.wait_ge(split_done, split + 1 + n)
                        hi = slab_hi[:, slot % 2, n * 512:(n + 1) * 512]
                        lo = slab_lo[:, slot % 2, n * 512:(n + 1) * 512]
                        for t in range(T):
                            out, tok = psum[:, 2 * t + n, :], slice(t * P, (t + 1) * P)
                            pe.matmul(out, weighted_hi[:, parity, tok], hi, start=first, stop=False)
                            pe.matmul(out, weighted_hi[:, parity, tok], lo, start=False, stop=False)
                            mm = pe.matmul(out, weighted_lo[:, parity, tok], hi, start=False, stop=last)
                    mm.then_inc(slab_done, 1)

                z = 2 * layer * EXP
                pe.wait_ge(S["hidden_lo"], 4 * (layer + 1))
                up(0, z, (0, None))
                up(1, z + 2, (1, None))
                down(2, z + 4, 0, w + 1, first=True)
                up(3, z + 6, (0, w + 1))
                with pe.Fori(1, EXP // RING - 1) as k:
                    down(0, k * 8 + z, 1, k * 2 + w)
                    up(1, k * 8 + (z + 2), (1, k * 2 + w))
                    down(2, k * 8 + (z + 4), 0, k * 2 + (w + 1))
                    up(3, k * 8 + (z + 6), (0, k * 2 + (w + 1)))
                down(0, z + 504, 1, w + 126)
                up(1, z + 506, (1, w + 126))
                down(2, z + 508, 0, w + 127)
                down(3, z + 510, 1, w + 128, last=True)

            for layer in range(LAYERS):
                even_mixer() if layer == 0 else odd_mixer(layer)
                out_projection(layer)
                turn_hidden(2 * layer)
                route_scores(layer)
                spread(layer)
                experts(layer)
                if layer + 1 < LAYERS:
                    turn_hidden(2 * layer + 1)

        @block.scalar
        def _(act):
            step = Steps(act, S["act_steps"])

            def copy_proj(n, dst, scale=1.0):
                act.wait_ge(slab_done, n[0])
                src = psum[:, 4 + n[1], 0:SEQ]
                if len(dst.shape) == 3:
                    src = src.rearrange("p (a b) -> p a b", a=2)
                act.activation(dst, src, ACT.Copy, scale=scale).then_inc(proj_copied, 1)

            def layer_norm(layer, which):
                ln = 2 * layer + which
                for t in range(T):
                    act.wait_ge(S["ln_mean"], T * ln + t + 1)
                    act.activation(squares[:, t, :], h_nat[:, t, :], ACT.Square, bias=small[:, 8 + t:9 + t],
                                   accum_out=small[:, 12 + t:13 + t]).then_inc(S["ln_square"], 1)
                for t in range(T):
                    act.wait_ge(S["ln_var"], T * ln + t + 1)
                    act.activation(small[:, 20 + t:21 + t], small[:, 16 + t:17 + t],
                                   ACT.Sqrt).then_inc(S["ln_rstd"], 1)

            def copy_hidden(ln, split):
                for t in range(T):
                    for b in range(2):
                        act.wait_ge(S["ln_turned"], 4 * ln + 2 * t + b + 1)
                        act.activation(hT[:, 4 * b:4 * b + 4, t * P:(t + 1) * P],
                                       psum[:, 2 * t + b, :].rearrange("p (c t) -> p c t", c=4),
                                       ACT.Copy).then_inc(S["ln_copied"], 1)
                if split:
                    act.wait_ge(S["ln_copied"], 4 * (ln + 1))
                    for b in range(4):
                        act.activation(hT_hi[:, 2 * b:2 * b + 2, :], hT[:, 2 * b:2 * b + 2, :],
                                       ACT.Copy).then_inc(S["hidden_hi"], 1)

            def even_mixer():
                act.dma_start(s5_par[:, :], a["s5_par"]).then_inc(S["s5_par_loaded"], 16)
                act.wait_ge(S["s5_par_loaded"], 16)
                act.activation(s5_small[:, 0, :], s5_par[:, 2 * ST:3 * ST], ACT.Exp).then_inc(S["s5_dt"], 1)
                act.wait_ge(S["s5_rates"], 1)
                act.activation(s5_small[:, 3, :], s5_small[:, 1, :], ACT.Exp).then_inc(S["s5_mag"], 1)
                act.wait_ge(S["s5_angle"], 1)
                act.activation(s5_small[:, 8, :], s5_small[:, 6, :], ACT.Sin).then_inc(S["s5_sine"], 1)
                act.activation(s5_small[:, 9, :], s5_small[:, 7, :], ACT.Sin).then_inc(S["s5_sine"], 1)
                act.dma_start(b_lay[:, :, :, :], a["s5_b"]).then_inc(S["s5_b_loaded"], 16)
                for n in range(UT):
                    copy_proj((n + 1, n % 2), uT[:, n, :])
                for n in range(UT, 8):
                    c = (n - UT) // 2 * 2 * P
                    copy_proj((n // 2 * 2 + 2, n % 2), v_nat[:, n % 2, c:c + 2 * P])
                act.dma_start(c_lay[:, :, :, :], a["s5_c"]).then_inc(S["s5_loaded"], 16)
                act.dma_start(glu_w[:, :, :], a["glu_w"]).then_inc(S["s5_loaded"], 16)
                act.dma_start(h_nat[:, :, :], a["x"]).then_inc(S["s5_loaded"], 16)

                def take(i, pr):
                    copy_proj((i * 4 + (9 + 2 * pr), 0), qk[:, 2 * pr, :], SCALE)
                    copy_proj((i * 4 + (10 + 2 * pr), 1), qk[:, 2 * pr + 1, :])

                def logs(i, pr):
                    parts = [stick[:, 2 * pr + h, 1, :] for h in range(2)]
                    for h in range(2):
                        act.wait_ge(S["z_ready"], i * 4 + (2 * pr + h + 1))
                        step(act.activation(parts[h], psum[:, (6 if pr == 0 else 0) + h, 0:384], ACT.Abs))
                    for h in range(2):
                        step.wait(1)
                        step(act.activation(parts[h], parts[h], ACT.Exp, scale=-1.0))
                    for h in range(2):
                        step.wait(1 - h)
                        act.activation(parts[h], parts[h], ACT.Ln, bias=1.0).then_inc(S["z_log"], 1)

                def weights(i, pr):
                    for h in range(2):
                        z = psum[:, (6 if pr % 2 == 0 else 0) + h, 0:384]
                        act.wait_ge(S["masked"], i * 4 + (2 * pr + h + 1))
                        act.activation(stick[:, 2 * (pr % 2) + h, 1, :], z, ACT.Exp).then_inc(S["stick_w"], 1)

                def store(i, pr):
                    act.wait_ge(S["pv_ready"], i * 2 + (pr + 1))
                    for h in range(2):
                        rows = slice(64 * h, 64 * h + 64)
                        act.activation(mixT[rows, i * 2 + (UT + pr), :], psum[rows, 2, h * SEQ:(h + 1) * SEQ],
                                       ACT.Copy).then_inc(S["o_copied"], 1)

                def turn(i):
                    step.enter(i, 8)
                    for pr in range(2):
                        take(i, pr)
                        if not isinstance(i, int):
                            store(i, pr - 2)
                        logs(i, pr)
                        if not isinstance(i, int) or pr:
                            weights(i, pr - 1)

                turn(0)
                step.leave(1)
                with act.Fori(1, SB_PAIRS // 2) as i:
                    turn(i)
                step.leave(SB_PAIRS // 2 - 1)
                store(SB_PAIRS // 2, -2)
                weights(SB_PAIRS // 2, -1)
                act.wait_ge(S["s5_y_in"], 1)
                act.activation(yT[:, 1, :, :], yT[:, 0, :, :], ACT.Gelu_apprx_tanh).then_inc(S["s5_gelu"], 1)
                store(SB_PAIRS // 2, -1)
                act.wait_ge(S["s5_z"], 1)
                for c in range(UT):
                    act.activation(yT[:, 2, c, :], psum[:, 3, c * SEQ:(c + 1) * SEQ], ACT.Sigmoid,
                                   bias=s5_par[:, 3 * ST + UT + c:3 * ST + UT + c + 1]).then_inc(S["s5_gate"], 1)

            def odd_mixer(layer):
                b = base(layer)
                for n in range(4):
                    copy_proj((b + n + 1, n % 2), kvc[:, n, :])
                act.wait_ge(S["gate_ready"], 1)
                act.activation(gates[:, :, :, :].rearrange("p t g n -> p (t g n)"), psum[:, 7, 0:96],
                               ACT.Sigmoid).then_inc(S["gate_done"], 1)
                for n in range(2):
                    act.wait_ge(S["cmp_ready"], n + 1)
                    act.activation(cmp_act[0:CMP_ROWS, n, :], psum[0:CMP_ROWS, 3 * n, 0:P],
                                   ACT.Gelu_apprx_tanh).then_inc(S["cmp_act_ready"], 1)
                act.wait_ge(S["cmp_turned"], 1)
                for n in range(2):
                    act.activation(cmp_hid[:, n, :, :, :].rearrange("p f g m -> p (f g) m"),
                                   psum[:, 1, n * 64:(n + 1) * 64].rearrange("p (g m) -> p g m", g=4)[:, :, 0:NCMP],
                                   ACT.Copy).then_inc(S["cmp_hidden"], 1)
                act.wait_ge(S["cmp_kv"], 1)
                for f in range(2):
                    rows = slice(64 * f, 64 * f + 64)
                    act.activation(kcT[rows, :, :].rearrange("p g m -> p (g m)"),
                                   psum[rows, 2, 128 + f * 2 * NCMP:128 + (f + 1) * 2 * NCMP],
                                   ACT.Copy).then_inc(S["cmp_kv_copied"], 1)
                    act.activation(vc[0:NCMP, f, :], psum[0:NCMP, 2, 256 + f * P:256 + (f + 1) * P],
                                   ACT.Copy).then_inc(S["cmp_kv_copied"], 1)
                act.wait_ge(S["cmp_kv_copied"], 4)
                def turn(i):
                    free(act, S["sel_out"], i * 16)
                    act.activation(kc_now[:, :], kcT[:, i, :], ACT.Copy).then_inc(S["cmp_staged"], 1)
                    act.activation(vc_now[0:NCMP, :], vc[0:NCMP, i, :], ACT.Copy).then_inc(S["cmp_staged"], 1)
                    for m in range(8):
                        n = (i * 8 + (b + 4 + m + 1), m % 2)
                        if m < 2:
                            copy_proj(n, kT[:, m, :])
                        elif m < 4:
                            copy_proj((i * 8 + (b + 8), m % 2), vN[:, :, m - 2, :])
                        else:
                            copy_proj(n, qT[:, m - 4, :], SCALE)
                    act.wait_ge(S["cmp_shifted"], i + 1)
                    act.activation(pc[:, :, :, :], pc[:, :, :, :], ACT.Exp).then_inc(S["cmp_exp"], 1)

                    def exps(s):
                        t = s % 2
                        n = P * (t + 1)
                        act.wait_ge(S["sel_biased"], i * 16 + (s + 1))
                        for br in range(2):
                            x = prob[:, s % 4, br * n:(br + 1) * n]
                            act.activation(x, x, ACT.Exp, bias=red[:, s % 4, br:br + 1],
                                           accum_out=red[:, s % 4, 2 + br:3 + br]).then_inc(S["sel_exp"], 1)

                    def turned_copy(s):
                        t = s % 2
                        act.wait_ge(S["sel_turned"], i * 16 + (s + 1))
                        n = 2 * P * (t + 1)
                        step(act.activation(pcT[0:NCMP, s % 2, :],
                                            psum[0:NCMP, 3 * t, 256:256 + P], ACT.Copy))
                        step.wait()
                        act.activation(probT[:, s % 2, 0:n], psum[:, s % 2, 0:n], ACT.Copy).then_inc(S["sel_copied"], 1)

                    def store(s):
                        act.wait_ge(S["sel_out"], i * 16 + (s + 1))
                        for half in range(2):
                            rows = slice(64 * half, 64 * half + 64)
                            act.activation(mixT[rows, i * 4 + s // 4, :], psum[rows, 2, half * SEQ:(half + 1) * SEQ],
                                           ACT.Copy).then_inc(S["sel_stored"], 1)

                    step.enter(i, 16)
                    exps(0)
                    exps(1)
                    for s in range(16):
                        if s + 2 < 16:
                            exps(s + 2)
                        turned_copy(s)
                        if s and s % 4 == 0:
                            store(s - 1)
                    store(15)

                turn(0)
                step.leave(1)
                with act.Fori(1, 2) as i:
                    turn(i)
                step.leave(2 - 1)

            def route(layer):
                b = base(layer) + PROJ + OUTW
                def turn(i):
                    for pr in range(2):
                        for s in (2 * pr, 2 * pr + 1):
                            free(act, S["score_ready"], i * 4 + (layer * SUBS + s - 1))
                            copy_proj((i * 4 + (b + s + 1), s % 2), sub_q[:, s % 2, :])
                        for s in (2 * pr, 2 * pr + 1):
                            act.wait_ge(S["score_ready"], i * 4 + (layer * SUBS + s + 1))
                            act.activation(scores[:, :, i * 4 + s, :], psum[:, 6 + s % 2, 0:SEQ].rearrange(
                                "p (t k) -> p t k", t=T), ACT.Copy).then_inc(S["score_copied"], 1)

                turn(0)
                with act.Fori(1, WQ // RING) as i:
                    turn(i)
                for t in range(T):
                    act.wait_ge(S["route_exp_in"], layer * T + t + 1)
                    act.activation(pairs[:, t, 2, :], pairs[:, t, 2, :], ACT.Exp).then_inc(S["route_exp"], 1)
                def weight(i, q):
                    act.wait_ge(S["hot_equal"], i * HOT + (layer * HOT_GROUPS + q + 1))
                    for m in range(HOT_SCALED):
                        x = hot[q % HOT][:, 0, m, :]
                        act.activation(x, x, ACT.Copy, scale=pair_column(i, q, 2, m)).then_inc(S["hot_scaled"], 1)

                def turn(i, last=False):
                    for q in range(HOT):
                        if not last or q + 2 < HOT:
                            weight(i, q + 2)
                        act.wait_ge(S["g_ready"], i * HOT + (layer * HOT_GROUPS + q + 1))
                        act.activation(G[:, :, bass.ds(i * (4 * HOT) + 4 * q, 4)].rearrange("p e m -> p m e"),
                                       psum[:, 4 + q, :].rearrange("p (m e) -> p m e", m=4),
                                       ACT.Copy).then_inc(S["g_copied"], 1)

                act.wait_ge(S["pairs_turned"], T * (layer + 1))
                weight(0, 0)
                weight(0, 1)
                turn(0)
                with act.Fori(1, HOT_TURNS - 1) as i:
                    turn(i)
                turn(HOT_TURNS - 1, last=True)

            def experts(layer):
                b, w = base(layer) + PROJ + OUTW + WQ, layer * KEYS

                def high(slot, land, free):
                    act.wait_ge(slab_loaded[slot], land)
                    act.wait_ge(slab_done, free)
                    for n in range(2):
                        cols = slice(n * 512, (n + 1) * 512)
                        act.activation(slab_hi[:, slot % 2, cols], ring[:, slot, cols],
                                       ACT.Copy).then_inc(S["hi_done"], 1)

                def gelu(parity, done, free):
                    act.wait_ge(slab_done, done)
                    if free is not None:
                        act.wait_ge(S["weighted_ready"], free)
                    act.activation(hidden[:, parity, :], psum[:, 4 + parity, 0:SEQ],
                                   ACT.Gelu_apprx_tanh).then_inc(S["hidden_ready"], 1)

                land = (b // RING + 1) * 16
                high(0, land, b)
                high(1, land, b)
                high(2, land, b + 1)
                gelu(0, b + 1, None)

                def turn(k):
                    high(3, k * 16 + land, k * 4 + (b + 2))
                    gelu(1, k * 4 + (b + 2), k * 2 + w)
                    high(0, k * 16 + (land + 16), k * 4 + (b + 3))
                    high(1, k * 16 + (land + 16), k * 4 + (b + 4))
                    gelu(0, k * 4 + (b + 4), k * 2 + (w + 1))
                    high(2, k * 16 + (land + 16), k * 4 + (b + 5))

                turn(0)
                with act.Fori(1, KEYS // 2 - 1) as k:
                    turn(k)
                high(3, land + 16 * 63, b + 254)
                gelu(1, b + 254, w + 126)

            for layer in range(LAYERS):
                even_mixer() if layer == 0 else odd_mixer(layer)
                layer_norm(layer, 0)
                copy_hidden(2 * layer, True)
                route(layer)
                experts(layer)
                layer_norm(layer, 1)
                if layer + 1 < LAYERS:
                    copy_hidden(2 * layer + 1, False)

        @block.gpsimd
        def _(pool):
            step = Steps(pool, S["pool_steps"])

            def load_ln(ln):
                for k in range(2):
                    pool.dma_start(ln_par[:, k, :], wide(a["ln"][2 * ln + k:2 * ln + k + 1, :], 0, P)).then_inc(
                        S["ln_loaded"], 16)

            def phases():
                pool.wait_ge(S["s5_sine"], 2)
                pool.dma_start(const[:, :], a["const"]).then_inc(S["const_loaded"], 16)
                re, im = phase[:, 0, :, :], phase[:, 1, :, :]
                w = [s5_small[:, 16 + n, :] for n in range(4)]
                step(pool.memset(re[:, :, 0:1], 1.0))
                step(pool.memset(im[:, :, 0:1], 0.0))
                step(pool.tensor_copy(w[0], s5_small[:, 9, :]))
                step(pool.tensor_copy(w[1], s5_small[:, 8, :]))
                step.wait()
                n = 1
                while n < SEQ:
                    a0, b0 = re[:, :, 0:n], im[:, :, 0:n]
                    wr = wide(w[0][:, :].unsqueeze(2), 2, n)
                    wi = wide(w[1][:, :].unsqueeze(2), 2, n)
                    t0, t1 = temp[:, 0, :, 0:n], temp[:, 1, :, 0:n]
                    step(pool.tensor_tensor(t0, a0, wr, ALU.mult))
                    step(pool.tensor_tensor(t1, b0, wi, ALU.mult))
                    step.wait()
                    step(pool.tensor_tensor(re[:, :, n:2 * n], t0, t1, ALU.subtract))
                    step.wait()
                    step(pool.tensor_tensor(t0, a0, wi, ALU.mult))
                    step(pool.tensor_tensor(t1, b0, wr, ALU.mult))
                    step.wait()
                    step(pool.tensor_tensor(im[:, :, n:2 * n], t0, t1, ALU.add))
                    step(pool.tensor_tensor(w[2], w[0], w[0], ALU.mult))
                    step(pool.tensor_tensor(w[3], w[1], w[1], ALU.mult))
                    step(pool.tensor_tensor(w[1], w[0], w[1], ALU.mult))
                    step.wait()
                    step(pool.tensor_tensor(w[0], w[2], w[3], ALU.subtract))
                    step(pool.tensor_scalar(w[1], w[1], 2.0, None, ALU.mult))
                    step.wait()
                    n *= 2
            def flatten(x):
                return x.rearrange("p j t -> p (j t)")

            pr, pi = flatten(phase[:, 0]), flatten(phase[:, 1])
            d_re, d_im = flatten(drive[:, 0]), flatten(drive[:, 1])
            z_re, z_im = flatten(turned[:, 0]), flatten(turned[:, 1])
            t0, t1 = flatten(temp[:, 0]), flatten(temp[:, 1])

            def products():
                step(pool.tensor_tensor(z_re, pr, d_re, ALU.mult))
                step(pool.tensor_tensor(t0, pi, d_im, ALU.mult))
                step(pool.tensor_tensor(z_im, pr, d_im, ALU.mult))
                step(pool.tensor_tensor(t1, pi, d_re, ALU.mult))
                step.wait()

            phases()
            pool.wait_ge(S["s5_pq_used"], ST)
            products()
            step(pool.tensor_tensor(z_re, z_re, t0, ALU.add))
            pool.tensor_tensor(z_im, t1, z_im, ALU.subtract).then_inc(S["s5_turned"], 1)
            pool.wait_ge(S["s5_scanned"], 2 * ST)
            products()
            pool.tensor_tensor(z_re, z_re, t0, ALU.add).then_inc(S["s5_states"], 1)
            pool.tensor_tensor(z_im, z_im, t1, ALU.subtract).then_inc(S["s5_states"], 1)

            def candidates(layer, h):
                pool.wait_ge(S["sub_ranked"], 2 * T * (layer * PEER_HEADS + h + 1))
                free(pool, S["cand_ranked"], T * (layer * PEER_HEADS + h - 1))
                for t in range(T):
                    for first, to, width in CAND_ROWS:
                        at, n = CAND_START[first], to - first
                        pool.tensor_tensor(cand[:, h % 2, t, at:at + n * width].rearrange("p (a b) -> p a b", a=n),
                                           wide(sub_top[:, t, 2 * h, first:to].unsqueeze(2), 2, width),
                                           wide(sub_top[:, t, 2 * h + 1, 0:width].unsqueeze(1), 1, n),
                                           ALU.add).then_inc(S["cand_ready"], 1)

            def take_indices(layer, some, n):
                s, t = TAKEN_BY_POOL[some][n]
                pool.wait_ge(S["match_ready"], (layer * SHARES + some) * 4 + 2 * t + s + 1)
                pool.tensor_tensor(match[:, s, t], match[:, s, t], taken_indices(s, t, some), ALU.mult).then_inc(
                    S["match_taken"], 1)

            def distances(layer):
                pool.wait_ge(S["pairs_turned"], T * (layer + 1))

                def turn(i):
                    for q in range(HOT):
                        k = layer * HOT_GROUPS + q
                        free(pool, S["g_ready"], i * HOT + (k + 1 - HOT))
                        pool.tensor_tensor(hot[q][:, 1, :, :], wide(iota.unsqueeze(1), 1, 4), group_of(i, q, 1, 4),
                                           ALU.subtract).then_inc(S["apart"], 1)

                turn(0)
                with pool.Fori(1, HOT_TURNS) as i:
                    turn(i)

            for layer in range(LAYERS):
                if layer:
                    for n in range(2):
                        pool.wait_ge(S["cmp_leaving"], n + 1)
                        pool.dma_start(blocks[64:P, n, 0:2 * SEQ - CMP_STRIDE], moving[0:64, n, CMP_STRIDE:]).then_inc(
                            S["cmp_moved_" + "kv"[n]], 16)
                        pool.dma_start(blocks[0:64, n, 2 * SEQ:], moving[64:P, n, :]).then_inc(
                            S["cmp_moved_" + "kv"[n]], 16)
                pool.wait_ge(slab_done, base(layer) + PROJ + 1)
                load_ln(2 * layer)
                pool.dma_start(keysT[:, :, :], a["keys"][layer]).then_inc(S["keys_loaded"], 16)
                for h in range(PEER_HEADS):
                    candidates(layer, h)
                    if h % SHARE == 0 and h:
                        for n in range(4):
                            take_indices(layer, h // SHARE - 1, n)
                take_indices(layer, SHARES - 1, 0)
                distances(layer)
                pool.wait_ge(S["weighted_ready"], layer * KEYS + ln_rows[1])
                load_ln(2 * layer + 1)
                if layer + 1 < LAYERS:
                    pool.wait_ge(S["weighted_ready"], layer * KEYS + nsa_rows)
                    for dst, name in ((w1[:, 0], "w1k"), (w1[:, 1], "w1v"), (w2[:, :, :], "w2"),
                                      (peT[:, :, :, :], "pe"), (gate_w[:, :, :], "gate_w")):
                        pool.dma_start(dst, a[name]).then_inc(S["nsa_loaded"], 16)
            pool.wait_ge(S["ln_loaded"], 32 * 2 * LAYERS)
            pool.wait_ge(S["keys_loaded"], 16 * LAYERS)
            pool.wait_ge(S["nsa_loaded"], 5 * 16)
            for n in "kv":
                pool.wait_ge(S["cmp_moved_" + n], 2 * 16)

        @block.vector
        def _(dve):
            step = Steps(dve, S["dve_steps"])

            def run(ins):
                step(ins)
                step.wait()

            def layer_norm(layer, which):
                ln = 2 * layer + which
                done = base(layer) + (PROJ + OUTW if which == 0 else PER_LAYER)
                dve.wait_ge(slab_done, done)
                for t in range(T):
                    y = h_nat[:, t, :]
                    run(dve.scalar_tensor_tensor(out=y, in0=y, scalar=ALPHA,
                                                 in1=psum[:, 2 * t:2 * t + 2, :].rearrange("p a b -> p (a b)"),
                                                 op0=ALU.mult, op1=ALU.add, accum_out=small[:, 4 + t:5 + t]))
                    dve.tensor_scalar(small[:, 8 + t:9 + t], small[:, 4 + t:5 + t], -1.0 / D, None,
                                      ALU.mult).then_inc(S["ln_mean"], 1)
                dve.wait_ge(S["ln_loaded"], 32 * (ln + 1))
                for t in range(T):
                    dve.wait_ge(S["ln_mean"], T * ln + t + 1)
                    step(dve.scalar_tensor_tensor(out=centred[:, t, :], in0=h_nat[:, t, :], scalar=small[:, 8 + t:9 + t],
                                                  in1=ln_par[:, 0, :], op0=ALU.add, op1=ALU.mult))
                    dve.wait_ge(S["ln_square"], T * ln + t + 1)
                    run(dve.tensor_scalar(small[:, 16 + t:17 + t], small[:, 12 + t:13 + t], 1.0 / D, EPS,
                                          ALU.mult, ALU.add))
                    dve.reciprocal(small[:, 16 + t:17 + t], small[:, 16 + t:17 + t]).then_inc(S["ln_var"], 1)
                for t in range(T):
                    dve.wait_ge(S["ln_rstd"], T * ln + t + 1)
                    dve.scalar_tensor_tensor(out=h_nat[:, t, :], in0=centred[:, t, :], scalar=small[:, 20 + t:21 + t],
                                             in1=ln_par[:, 1, :], op0=ALU.mult, op1=ALU.add).then_inc(S["ln_done"], 1)
                dve.wait_ge(S["ln_done"], T * (ln + 1))

            def s5_rates():
                lr, li = s5_par[:, 0:ST], s5_par[:, ST:2 * ST]
                s = [s5_small[:, n, :] for n in range(24)]
                dt, rate, angle, mag, turns = s[0], s[1], s[2], s[3], s[4]
                dve.wait_ge(S["s5_dt"], 1)
                run(dve.tensor_tensor(angle, li, dt, ALU.mult))
                dve.tensor_tensor(rate, lr, dt, ALU.mult).then_inc(S["s5_rates"], 1)
                run(dve.tensor_scalar(turns, angle, 1.0 / TWO_PI, ROUND, ALU.mult, ALU.add))
                run(dve.tensor_scalar(turns, turns, -ROUND, None, ALU.add))
                for part_pi in (PI_A, PI_B, PI_C):
                    run(dve.scalar_tensor_tensor(out=angle, in0=turns, scalar=-part_pi, in1=angle, op0=ALU.mult,
                                                 op1=ALU.add))
                run(dve.tensor_scalar(s[6], angle, PI_IN, -PI_IN, ALU.min, ALU.max))
                run(dve.scalar_tensor_tensor(out=s[5], in0=s[6], scalar=-1.0, in1=s[6], op0=ALU.mult, op1=ALU.max))
                dve.tensor_scalar(s[7], s[5], -1.0, float(np.pi / 2), ALU.mult, ALU.add).then_inc(S["s5_angle"], 1)
                dve.wait_ge(S["s5_sine"], 2)
                sine, cosine, a_re, a_im, den, t0, f_re, f_im, nf = s[8], s[9], s[10], s[11], s[12], s[13], s[14], s[15], s[21]
                run(dve.tensor_tensor(a_re, mag, cosine, ALU.mult))
                run(dve.tensor_tensor(a_im, mag, sine, ALU.mult))
                run(dve.tensor_scalar(a_re, a_re, -1.0, None, ALU.add))
                run(dve.tensor_tensor(den, lr, lr, ALU.mult))
                run(dve.tensor_tensor(t0, li, li, ALU.mult))
                run(dve.tensor_tensor(den, den, t0, ALU.add))
                run(dve.reciprocal(den, den))
                run(dve.tensor_tensor(f_re, a_re, lr, ALU.mult))
                run(dve.tensor_tensor(t0, a_im, li, ALU.mult))
                run(dve.tensor_tensor(f_re, f_re, t0, ALU.add))
                run(dve.tensor_tensor(f_re, f_re, den, ALU.mult))
                run(dve.tensor_tensor(f_im, a_im, lr, ALU.mult))
                run(dve.tensor_tensor(t0, a_re, li, ALU.mult))
                run(dve.tensor_tensor(f_im, f_im, t0, ALU.subtract))
                run(dve.tensor_tensor(f_im, f_im, den, ALU.mult))
                run(dve.tensor_scalar(nf, f_im, -1.0, None, ALU.mult))
                return f_re, f_im, nf, mag

            def s5_drive():
                f_re, f_im, nf, mag = s5_rates()
                for j in range(ST):
                    dve.wait_ge(S["s5_pq"], j + 1)
                    pq = psum[:, 6 + j % 2, :]
                    p, q = pq[:, 0:SEQ], pq[:, SEQ:2 * SEQ]
                    step(dve.tensor_scalar(turned[:, 0, j, :], q, nf[:, j:j + 1], None, ALU.mult))
                    run(dve.tensor_scalar(turned[:, 1, j, :], q, f_re[:, j:j + 1], None, ALU.mult))
                    step(dve.scalar_tensor_tensor(out=drive[:, 0, j, :], in0=p, scalar=f_re[:, j:j + 1],
                                                  in1=turned[:, 0, j, :], op0=ALU.mult, op1=ALU.add))
                    dve.scalar_tensor_tensor(out=drive[:, 1, j, :], in0=p, scalar=f_im[:, j:j + 1],
                                             in1=turned[:, 1, j, :], op0=ALU.mult, op1=ALU.add).then_inc(S["s5_pq_used"], 1)

            def s5_scan():
                mag = s5_small[:, 3, :]
                dve.wait_ge(S["s5_turned"], 1)
                for j in range(ST):
                    for r in range(2):
                        dve.tensor_tensor_scan(drive[:, r, j, :], wide(mag[:, j:j + 1], 1, SEQ), turned[:, r, j, :],
                                               0.0, ALU.mult, ALU.add).then_inc(S["s5_scanned"], 1)

            def even_mixer():
                dve.wait_ge(S["s5_par_loaded"], 16)
                s5_drive()
                dve.wait_ge(S["const_loaded"], 16)
                dve.wait_ge(proj_copied, 8)
                def stick_sums(i, pr):
                    for h in range(2):
                        k = 2 * pr + h
                        s = stick[:, k, 0, :]
                        dve.wait_ge(S["z_log"], i * 4 + (k + 1))
                        run(dve.scalar_tensor_tensor(out=s, in0=psum[:, (6 if pr == 0 else 0) + h, 0:384], scalar=0.0,
                                                     in1=stick[:, k, 1, :], op0=ALU.max, op1=ALU.add))
                        step(dve.tensor_tensor(s[:, 0:P], s[:, 0:P], below, ALU.mult))
                        dve.tensor_tensor(s[:, 2 * P:3 * P], s[:, 2 * P:3 * P], below,
                                          ALU.mult).then_inc(S["stick_ready"], 1)

                def mask(i, pr):
                    for h in range(2):
                        z = psum[:, (6 if pr % 2 == 0 else 0) + h, :].rearrange("p (a b) -> p a b", a=2)[:, :, 0:P]
                        dve.wait_ge(S["tails_ready"], i * 4 + (2 * pr + h + 1))
                        dve.tensor_tensor(z, z, wide(neg_diag.unsqueeze(1), 1, 2), ALU.add).then_inc(S["masked"], 1)

                def turn(i):
                    step.enter(i, 8)
                    for pr in range(2):
                        free(dve, S["pv_ready"], i * 2 + (pr - 1))
                        dve.tensor_copy(v_pair[:, pr, :, :],
                                        v_nat[:, :, bass.ds(i * 2 * P + pr * P, P)]).then_inc(S["v_staged"], 1)
                        stick_sums(i, pr)
                        if not isinstance(i, int) or pr:
                            mask(i, pr - 1)

                turn(0)
                step.leave(1)
                s5_scan()
                with dve.Fori(1, SB_PAIRS // 2) as i:
                    turn(i)
                step.leave(SB_PAIRS // 2 - 1)
                mask(SB_PAIRS // 2, -1)
                dve.wait_ge(S["s5_loaded"], 3 * 16)
                dve.wait_ge(S["s5_y"], 1)
                for c in range(UT):
                    run(dve.scalar_tensor_tensor(out=yT[:, 0, c, :], in0=uT[:, c, :],
                                                 scalar=s5_par[:, 3 * ST + c:3 * ST + c + 1],
                                                 in1=psum[:, 3, c * SEQ:(c + 1) * SEQ], op0=ALU.mult, op1=ALU.add))
                dve.memset(small[:, 0:1], 0.0).then_inc(S["s5_y_in"], 1)
                for c in range(UT):
                    dve.wait_ge(S["s5_gate"], c + 1)
                    dve.tensor_tensor(mixT[:, c, :], yT[:, 1, c, :], yT[:, 2, c, :], ALU.mult).then_inc(S["s5_out"], 1)

            def odd_mixer():
                dve.wait_ge(S["nsa_loaded"], 5 * 16)
                for n in range(2):
                    dve.wait_ge(proj_copied, PROJ_PER_LAYER + 2 * n + 2)
                    x = kvc[:, 2 * n:2 * n + 2, :].rearrange("p g t -> p (g t)")

                    def placed(out, x, pe):
                        count = x.shape[1] // CMP_STRIDE
                        return dve.tensor_tensor(out.rearrange("p (m o) -> p m o", o=CMP_STRIDE),
                                                 x.rearrange("p (m o) -> p m o", o=CMP_STRIDE),
                                                 wide(pe.unsqueeze(1), 1, count), ALU.add)

                    placed(moving[:, n, :], x, peT[:, n, 1, :]).then_inc(S["cmp_leaving"], 1)
                    placed(blocks[0:64, n, 0:2 * SEQ], x[0:64, :], peT[0:64, n, 0, :]).then_inc(S["cmp_staying"], 1)
                    placed(blocks[64:P, n, 2 * SEQ - CMP_STRIDE:4 * SEQ - CMP_STRIDE], x[64:P, :],
                           peT[64:P, n, 0, :]).then_inc(S["cmp_staying"], 1)
                def turn(i):
                    step.enter(i, 8 + 16 * 6)
                    dve.wait_ge(S["gate_done"], 1)
                    dve.wait_ge(S["cmp_scores"], i + 1)
                    for t in range(T):
                        bias = const[:, bass.ds(i * (8 * NCMP) + (C_CMPBIAS + t * NSA_HEADS * NCMP), 8 * NCMP)]
                        bias = bias.rearrange("p (r f m) -> p r f m", r=4, f=2)
                        now = pc[:, t, :, :].rearrange("p (r f) m -> p r f m", f=2)
                        for f in range(2):
                            got = psum[:, 3 * f, t * 4 * NCMP:(t + 1) * 4 * NCMP].rearrange("p (r m) -> p r m", r=4)
                            step(dve.tensor_tensor(now[:, :, f, :], got, bias[:, :, f, :], ALU.add))
                    step.wait()
                    flat_pc = pc[:, :, :, :].rearrange("p t h m -> p (t h) m")
                    mx, sm = (pc_red[:, n, :, :].rearrange("p t h -> p (t h)") for n in range(2))
                    run(dve.tensor_reduce(mx, flat_pc, AX.X, ALU.max))
                    dve.tensor_tensor(flat_pc, flat_pc, wide(mx.unsqueeze(2), 2, NCMP),
                                      ALU.subtract).then_inc(S["cmp_shifted"], 1)
                    dve.wait_ge(S["cmp_exp"], i + 1)
                    for t in range(T):
                        keep = const[:, C_CMPMASK + t * NCMP:C_CMPMASK + (t + 1) * NCMP]
                        step(dve.tensor_tensor(pc[:, t, :, :], pc[:, t, :, :], wide(keep.unsqueeze(1), 1, 8),
                                               ALU.mult))
                    step.wait()
                    run(dve.tensor_reduce(sm, flat_pc, AX.X, ALU.add))
                    dve.tensor_scalar(sm, sm, 1e-30, None, ALU.max).then_inc(S["cmp_aux"], 1)
                    dve.wait_ge(S["cmp_aux"], i * 3 + 1)
                    dve.reciprocal(sm, sm).then_inc(S["cmp_aux"], 1)
                    dve.wait_ge(S["cmp_aux"], i * 3 + 2)
                    dve.tensor_tensor(pc_red[:, 1, :, :], pc_red[:, 1, :, :], gates[:, :, i, 0:8],
                                      ALU.mult).then_inc(S["cmp_aux"], 1)
                    dve.wait_ge(S["cmp_aux"], i * 3 + 3)
                    dve.tensor_tensor(flat_pc, flat_pc, wide(sm.unsqueeze(2), 2, NCMP),
                                      ALU.mult).then_inc(S["cmp_probs"], 1)

                    def biased(s):
                        r, half, t = s // 4, s // 2 % 2, s % 2
                        n = P * (t + 1)
                        dve.wait_ge(S["sel_scores"], i * 16 + (s + 1))
                        if s >= 4:
                            dve.wait_ge(S["sel_turned"], i * 16 + (s - 3))
                        d = C_DIST + (P if t else 0)
                        x = prob[:, s % 4, 0:2 * n].rearrange("p (b n) -> p b n", b=2)
                        h = 2 * r + half
                        run(dve.scalar_tensor_tensor(
                            out=x, in0=wide(const[:, d:d + n].unsqueeze(1), 1, 2),
                            scalar=const[:, bass.ds(i * 8 + (C_SLOPE + h), 1)],
                            in1=psum[:, SCORE_BANKS[s % 4], 0:2 * n].rearrange("p (b n) -> p b n", b=2),
                            op0=ALU.mult, op1=ALU.add))
                        dve.tensor_reduce(red[:, s % 4, 0:2], x, AX.X, ALU.max, negate=True).then_inc(
                            S["sel_biased"], 1)

                    def scaled(s):
                        r, half, t = s // 4, s // 2 % 2, s % 2
                        n, h = P * (t + 1), 2 * r + half
                        sums = red[:, s % 4, 2:4]
                        dve.wait_ge(S["sel_exp"], i * 32 + 2 * (s + 1))
                        run(dve.tensor_scalar(sums, sums, 1e-30, None, ALU.max))
                        run(dve.reciprocal(sums, sums))
                        for br in range(2):
                            g = 8 * (br + 1) + h
                            step(dve.tensor_tensor(sums[:, br:br + 1], sums[:, br:br + 1], gates[:, t, i, g:g + 1],
                                                   ALU.mult))
                        step.wait()
                        x = prob[:, s % 4, :]
                        run(dve.tensor_scalar(x[:, 0:n], x[:, 0:n], sums[:, 0:1], None, ALU.mult))
                        dve.tensor_scalar(x[:, n:2 * n], x[:, n:2 * n], sums[:, 1:2], None,
                                          ALU.mult).then_inc(S["sel_prob"], 1)

                    biased(0)
                    biased(1)
                    for s in range(16):
                        if s + 2 < 16:
                            biased(s + 2)
                        scaled(s)

                turn(0)
                step.leave(1)
                with dve.Fori(1, 2) as i:
                    turn(i)
                step.leave(2 - 1)

            def top16(rows, ranked):
                stages = (lambda v, b, x: dve.max(b[:, 0:8], v),
                          lambda v, b, x: dve.max_index(x[:, 0:8].bitcast(U32), b[:, 0:8], v),
                          lambda v, b, x: dve.match_replace(v, b[:, 0:8], v, NEG * 1e8),
                          lambda v, b, x: dve.max(b[:, 8:16], v),
                          lambda v, b, x: dve.max_index(x[:, 8:16].bitcast(U32), b[:, 8:16], v))
                for n, stage in enumerate(stages):
                    final = n == len(stages) - 1
                    for r, (values, best_out, index_out) in enumerate(rows):
                        if n:
                            step.wait(len(rows) - 1 - (r if final else 0))
                        ins = stage(values, best_out, index_out)
                        if final:
                            ins.then_inc(ranked, 1)
                        else:
                            step(ins)

            def ranks(layer, some):
                c, b, m, mi = place[:, 0], place[:, 1], place[:, 2:5], place[:, 5]
                dve.wait_ge(S["sub_ranked"], 2 * T * (layer * PEER_HEADS + (some + 1) * SHARE))
                dve.wait_ge(S["cand_ranked"], T * (layer * PEER_HEADS + (some + 1) * SHARE))
                heads = slice(some * SHARE, (some + 1) * SHARE)
                at = flat[:, :, heads, :].rearrange("p t h k -> p t (h k)").bitcast(U32)
                step(dve.tensor_copy(c, at))
                idf = sub_idf[:, :, 2 * some * SHARE:2 * (some + 1) * SHARE, :]
                step(dve.tensor_copy(idf, sub_idx[:, :, 2 * some * SHARE:2 * (some + 1) * SHARE, :].bitcast(U32)))
                step.wait(1)
                width = CAND_ROWS[0][2]
                for n, (first, _, now) in enumerate(CAND_ROWS[1:]):
                    low_bits = now - 1
                    step(dve.tensor_scalar(m[:, n], c, float(CAND_START[first]), float(low_bits - (width - 1)),
                                           ALU.is_ge, ALU.mult))
                    width = now
                step.wait(1)
                step(dve.scalar_tensor_tensor(out=m[:, 0], in0=m[:, 0], scalar=float(TOPK - 1), in1=m[:, 1],
                                              op0=ALU.add, op1=ALU.add))
                step.wait()
                step(dve.tensor_tensor(m[:, 0], m[:, 0], m[:, 2], ALU.add))
                both = sub_idf.rearrange("p t (h s) k -> p t h s k", s=2)[:, :, heads, 0, :]
                step.wait()
                step(dve.tensor_copy(mi.bitcast(U32), m[:, 0]))
                for t in range(T):
                    x = both[:, t]
                    y = spare[:, t]
                    step(dve.tensor_tensor(y, x[:, :, 1:TOPK], x[:, :, 0:TOPK - 1], ALU.subtract))
                step.wait()
                for t in range(T):
                    step(dve.tensor_copy(both[:, t, :, 1:TOPK], spare[:, t]))
                step(dve.tensor_tensor(mi.bitcast(U32), mi.bitcast(U32), at, ALU.bitwise_and))
                step.wait()
                step(dve.tensor_copy(b, mi.bitcast(U32)))
                step.wait()
                for t in range(T):
                    for s in range(2):
                        of = wide(place[:, s, t, :].unsqueeze(2), 2, TOPK)
                        against = wide((cand_start, iota16)[s].unsqueeze(1), 1, SHARE * TOPK)
                        dve.tensor_tensor(match[:, s, t].rearrange("p h k c -> p (h k) c"), of, against,
                                          (ALU.is_ge, ALU.is_equal)[s]).then_inc(S["match_ready"], 1)

            def sums(some, s, t):
                step(dve.tensor_reduce(pairs[:, t, s, some * SHARE * TOPK:(some + 1) * SHARE * TOPK],
                                       match[:, s, t].rearrange("p h k c -> p (h k) c"), AX.X, ALU.add))

            def route(layer):
                for b in range(4):
                    dve.wait_ge(S["hidden_hi"], 4 * layer + b + 1)
                    dve.tensor_tensor(hT_lo[:, 2 * b:2 * b + 2, :], hT[:, 2 * b:2 * b + 2, :],
                                      hT_hi[:, 2 * b:2 * b + 2, :].bitcast(F32), ALU.subtract).then_inc(
                                          S["hidden_lo"], 1)
                def halves(h):
                    for j in (2 * h, 2 * h + 1):
                        dve.wait_ge(S["score_copied"], layer * SUBS + j + 1)
                        top16([(scores[:, t, j, :], sub_top[:, t, j, :], sub_idx[:, t, j, :]) for t in range(T)],
                              S["sub_ranked"])

                halves(0)
                for h in range(PEER_HEADS):
                    if h + 1 < PEER_HEADS:
                        halves(h + 1)
                    dve.wait_ge(S["cand_ready"], len(CAND_ROWS) * T * (layer * PEER_HEADS + h + 1))
                    top16([(cand[:, h % 2, t, :], best[:, t, h, :], flat[:, t, h, :]) for t in range(T)],
                          S["cand_ranked"])
                    some = h // SHARE
                    if h % SHARE == 0 and h:
                        for n, (s, t) in enumerate(TAKEN_BY_POOL[some - 1]):
                            dve.wait_ge(S["match_taken"], layer * POOL_TAKES + 4 * (some - 1) + n + 1)
                            sums(some - 1, s, t)
                    if (h + 1) % SHARE == 0 and h + 1 < PEER_HEADS:
                        ranks(layer, some)
                step.wait()
                for t in range(T):
                    g = pairs[:, t, 2, :].rearrange("p (h k) -> p h k", h=PEER_HEADS)
                    dve.tensor_tensor(g, best[:, t, :, :], wide(best[:, t, :, 0:1], 2, TOPK),
                                      ALU.subtract).then_inc(S["route_exp_in"], 1)
                ranks(layer, SHARES - 1)
                dve.wait_ge(S["match_ready"], 4 * SHARES * (layer + 1))
                for t in range(T):
                    g = pairs[:, t, 2, :].rearrange("p (h k) -> p h k", h=PEER_HEADS)
                    own = [s for s in range(2) if (s, t) not in TAKEN_BY_POOL[-1]]
                    for s in own:
                        step(dve.tensor_tensor(match[:, s, t], match[:, s, t], taken_indices(s, t, SHARES - 1), ALU.mult))
                    dve.wait_ge(S["route_exp"], layer * T + t + 1)
                    step(dve.tensor_reduce(soft_red[:, 0, t, :], g, AX.X, ALU.add))
                    step.wait()
                    step(dve.reciprocal(soft_red[:, 1, t, :], soft_red[:, 0, t, :]))
                    for s in own:
                        sums(SHARES - 1, s, t)
                    if len(own) < 2:
                        dve.wait_ge(S["match_taken"], (layer + 1) * POOL_TAKES)
                        sums(SHARES - 1, 0, t)
                    step.wait()
                    dve.tensor_tensor(g, g, wide(soft_red[:, 1, t, :].unsqueeze(2), 2, TOPK),
                                      ALU.mult).then_inc(S["route_out"], 1)
                for t in range(T):
                    dve.wait_ge(S["route_turned"], layer * T + t + 1)
                    dve.tensor_copy(pairsT[:, t * P // 4:(t + 1) * P // 4, :, :].rearrange("p g n m -> p n g m"),
                                    psum[:, 6 + t, 0:3 * P].rearrange("p (n g m) -> p n g m", n=3, m=4)).then_inc(
                                        S["pairs_turned"], 1)
                dve.wait_ge(S["pairs_turned"], T * (layer + 1))
                def turn(i):
                    for q in range(HOT):
                        k = layer * HOT_GROUPS + q
                        free(dve, S["g_ready"], i * HOT + (k + 1 - HOT))
                        dve.tensor_tensor(hot[q][:, 0, 0:HOT_SCALED, :], wide(iota.unsqueeze(1), 1, HOT_SCALED),
                                          group_of(i, q, 0, HOT_SCALED), ALU.is_equal).then_inc(S["hot_equal"], 1)
                        for m in range(HOT_SCALED, 4):
                            dve.tensor_scalar(hot[q][:, 0, m, :], iota, pair_column(i, q, 0, m),
                                              pair_column(i, q, 2, m), ALU.is_equal, ALU.mult).then_inc(
                                                  S["hot_rows"], 1)
                        dve.wait_ge(S["apart"], i * HOT + (k + 1))
                        x = hot[q][:, 1, :, :]
                        dve.tensor_scalar(x, x, 0.0, None, ALU.is_equal).then_inc(S["hot_ready"], 1)

                turn(0)
                with dve.Fori(1, HOT_TURNS) as i:
                    turn(i)

            def experts(layer):
                b, w = base(layer) + PROJ + OUTW + WQ, layer * KEYS
                dve.wait_ge(S["g_copied"], (layer + 1) * (SEQ // 4))

                def low(slot, high):
                    for n in range(2):
                        cols = slice(n * 512, (n + 1) * 512)
                        dve.wait_ge(S["hi_done"], high + 1 + n)
                        dve.tensor_tensor(slab_lo[:, slot % 2, cols], ring[:, slot, cols],
                                          slab_hi[:, slot % 2, cols].bitcast(F32), ALU.subtract).then_inc(
                                              split_done, 1)

                def weigh(parity, e, ready, free):
                    dve.wait_ge(S["hidden_ready"], ready)
                    if free is not None:
                        dve.wait_ge(slab_done, free)
                    x = hidden[:, parity, :]
                    dve.tensor_tensor(x, x, G[:, e, :], ALU.mult).then_inc(S["raw_weighted"], 1)
                    dve.wait_ge(S["raw_weighted"], ready)
                    step(dve.tensor_copy(weighted_hi[:, parity, :], x))
                    step.wait()
                    dve.tensor_tensor(weighted_lo[:, parity, :], x, weighted_hi[:, parity, :].bitcast(F32),
                                      ALU.subtract).then_inc(S["weighted_ready"], 1)

                z = 2 * layer * EXP
                low(0, z)
                low(1, z + 2)
                low(2, z + 4)
                weigh(0, 0, w + 1, None)

                def turn(k):
                    step.enter(k, 2)
                    low(3, k * 8 + (z + 6))
                    weigh(1, k * 2 + 1, k * 2 + (w + 2), k * 4 + (b + 1))
                    low(0, k * 8 + (z + 8))
                    low(1, k * 8 + (z + 10))
                    weigh(0, k * 2 + 2, k * 2 + (w + 3), k * 4 + (b + 3))
                    low(2, k * 8 + (z + 12))

                turn(0)
                step.leave(1)
                with dve.Fori(1, KEYS // 2 - 1) as k:
                    turn(k)
                step.leave(KEYS // 2 - 2)
                low(3, z + 510)
                weigh(1, KEYS - 1, w + KEYS, b + 253)

            for layer in range(LAYERS):
                even_mixer() if layer == 0 else odd_mixer()
                layer_norm(layer, 0)
                route(layer)
                experts(layer)
                layer_norm(layer, 1)


def _cols(w, order=None):
    w = w if order is None else w[:, order]
    return w.reshape(KC, P, -1, P).transpose(2, 1, 0, 3).reshape(-1, P, D)


def _rows(w):
    return w.reshape(-1, P, D)


def lay_out(x):
    even, odd = x["even_w_in"][0], x["odd_w_in"][0]
    c, n = GROUPS * CH, SB_PAIRS * P
    u, q, k, v = even[:, :c], even[:, c:c + n], even[:, c + n:c + 2 * n], even[:, c + 2 * n:]
    qk = np.stack([_cols(q), _cols(k)], 1).reshape(-1, P, D)
    even_slabs = [_cols(u), _cols(v), qk, _rows(x["even_w_out"][0])]
    order = np.array([((2 * p + half) * 4 + r) * HEAD + d for p in range(2) for r in range(4) for half in range(2)
                      for d in range(HEAD)])
    kv = [_cols(odd[:, D + 256 * m:D + 256 * (m + 1)]) for m in range(6)]
    qs = _cols(odd[:, order])
    kc, vc, ks, vs, kw, vw = kv
    odd_slabs = [kc, vc]
    for p in range(2):
        odd_slabs += [ks[p:p + 1], kw[p:p + 1], vs[p:p + 1], vw[p:p + 1], qs[4 * p:4 * p + 4]]
    odd_slabs.append(_rows(x["odd_w_out"][0][order]))
    slabs = []
    for layer, mixer in ((0, even_slabs), (1, odd_slabs)):
        slabs += mixer
        slabs.append(_cols(x["peer_w_q"][layer]))
        up = x["peer_u"][layer].reshape(KEYS, P, KC, P).transpose(0, 3, 2, 1).reshape(KEYS, P, D)
        down = _rows(x["peer_v"][layer])
        both = np.empty((EXP, P, D), np.float32)
        ups = [0] + [4 * k + 1 if e % 2 else 4 * k + 3 for e in range(1, KEYS) for k in [(e - 1) // 2]]
        downs = [4 * (e // 2) + 2 if e % 2 == 0 else 4 * ((e + 1) // 2) for e in range(KEYS)]
        ups[KEYS - 1], downs[KEYS - 1] = EXP - 3, EXP - 1
        both[ups], both[downs] = up, down
        slabs.append(both)
    lam = [x["even_lam_re"][0], x["even_lam_im"][0], np.repeat(x["even_log_dt"][0][:, None], STATE, 1)]
    lam = [m.reshape(ST, P).T for m in lam]
    par = np.concatenate(lam + [x["even_d"][0].reshape(UT, P).T, x["even_b_glu"][0].reshape(UT, P).T], 1)
    b_lay = np.zeros((P, ST, 2, P), np.float32)
    c_lay = np.zeros((P, ST, 2, P), np.float32)
    for g in range(GROUPS):
        j, s, ch = g // 2, (g % 2) * STATE, (g % 8) * CH
        for r, (bm, cm) in enumerate((("even_b_re", "even_c_re"), ("even_b_im", "even_c_im"))):
            b_lay[ch:ch + CH, j, r, s:s + STATE] = x[bm][0, g].T
            c_lay[s:s + STATE, j, r, ch:ch + CH] = x[cm][0, g].T
    gate = odd[:, D + 6 * 256:].reshape(D, NBR, 2, 2, 4).transpose(0, 2, 1, 4, 3).reshape(KC, P, 48).transpose(1, 0, 2)

    w1 = {n: x[f"odd_w1_{n}"][0].reshape(2, CMP_STRIDE, HEAD, P).transpose(0, 2, 1, 3).reshape(P, CMP_STRIDE, P)
          for n in "kv"}
    w2 = np.stack([np.concatenate([x[f"odd_w2_{n}"][0]] * 2, 1) for n in "kv"], 1)
    pe = [x[f"odd_pe_{n}"][0].reshape(2, CMP_STRIDE, HEAD).transpose(0, 2, 1) for n in "kv"]
    pe = np.stack([np.stack([m.reshape(P, CMP_STRIDE), m[::-1].reshape(P, CMP_STRIDE)], 1) for m in pe], 1)
    keys = x["peer_sub_keys"].reshape(LAYERS, SUBS, KEYS, P).transpose(0, 3, 1, 2)
    ln = np.stack([x[n][layer] for layer in range(LAYERS) for k in (1, 2) for n in (f"ln{k}_g", f"ln{k}_b")])
    xs = x["x"][0]
    out = {
        "slabs": np.concatenate(slabs), "x": xs.reshape(T, P, D).transpose(1, 0, 2),
        "xT": xs.T.reshape(KC, P, SEQ).transpose(1, 0, 2), "s5_par": par, "s5_b": b_lay, "s5_c": c_lay,
        "glu_w": x["even_w_glu"][0].reshape(UT, P, UT * P).transpose(1, 0, 2), "gate_w": gate,
        "w1k": w1["k"], "w1v": w1["v"], "w2": w2, "pe": pe, "keys": keys, "ln": ln, "const": constants(),
    }
    return {n: np.ascontiguousarray(m) for n, m in out.items()}


def kernel(**inputs):
    import concourse.bacc as bacc
    from concourse.bass_utils import run_bass_kernel_spmd

    arrays = lay_out({n: np.asarray(m) for n, m in inputs.items()})
    nc = bacc.Bacc("TRN2", target_bir_lowering=False, num_devices=1)
    aps = {n: nc.dram_tensor(f"in_{n}", m.shape, F32, kind="ExternalInput").ap() for n, m in arrays.items()}
    aps["out"] = nc.dram_tensor("out", (SEQ, D), F32, kind="ExternalOutput").ap()
    build(nc, aps)
    r = run_bass_kernel_spmd(nc, [{f"in_{n}": m for n, m in arrays.items()}], core_ids=[0])
    return r.results[0]["out"].reshape(1, SEQ, D)
```
